# Optimizing a Trainium2 kernel written in Bass

```python
import jax
import jax.numpy as jnp
from jax import lax
import numpy as np
import jax, jax.numpy as jnp

D_MODEL = 1024
BATCH = 1
SEQ = 512
DEPTH = 1

GRID_W = 64
CTX_LEN = 256
N_MIXERS = 4
EPS = 1e-6
N_MOD = 6

FNET_GROUPS = 4
FNET_GROUP_DIM = D_MODEL // FNET_GROUPS

NA_HEADS = 16
NA_HEAD_DIM = D_MODEL // NA_HEADS
NA_WIN_ROWS = 8
NA_WIN_COLS = 16

SG_CHUNK = 128
SG_GROUPS = 4
SG_DIM = D_MODEL
SG_GROUP_DIM = SG_DIM // SG_GROUPS

ATT_HEADS = 16
ATT_KV_HEADS = 4
ATT_GROUP = ATT_HEADS // ATT_KV_HEADS
ATT_HEAD_DIM = D_MODEL // ATT_HEADS
ATT_Q_BLOCK = 128
ROPE_THETA = 10000.0

FFN_DIM = 2816
FFN_CONV = 3


def _layers_using(m):
    return (DEPTH - m + N_MIXERS - 1) // N_MIXERS

def rms_norm(x, g):
    xf = x.astype(jnp.float32)
    y = xf * lax.rsqrt(jnp.mean(xf * xf, axis=-1, keepdims=True) + EPS)
    return (y * g.astype(jnp.float32)).astype(x.dtype)

def modulate(h, g, shift, scale):
    return rms_norm(h, g) * (1 + scale) + shift

def ada_params(cond, w_mod, b_mod):
    m = jax.nn.silu(cond) @ w_mod + b_mod
    return jnp.split(m[:, None, :], N_MOD, axis=-1)

def depthwise_conv_seq(h, w, b):
    pad = FFN_CONV // 2
    y = lax.conv_general_dilated(h, w[:, None, :].astype(h.dtype), window_strides=(1,),
                                 padding=((pad, FFN_CONV - 1 - pad),),
                                 dimension_numbers=("NWC", "WIO", "NWC"),
                                 feature_group_count=h.shape[-1])
    return y + b

def conv_ffn(h, w_up, w_conv, b_conv, w_down):
    g, v = jnp.split(h @ w_up, 2, axis=-1)
    g = depthwise_conv_seq(g, w_conv, b_conv)
    return (jax.nn.silu(g) * v) @ w_down

def fourier_mix(a, w_out):
    B, L, D = a.shape
    ag = a.reshape(B, L, FNET_GROUPS, FNET_GROUP_DIM).astype(jnp.float32)
    f = jnp.fft.fft2(ag, axes=(1, 3), norm="ortho").real
    return f.astype(a.dtype).reshape(B, L, D) @ w_out

def spatial_gating_mix(a, w_in, g_v, w_s, b_s, w_out):
    B, L, _ = a.shape
    z = jax.nn.gelu(a @ w_in)
    u, v = jnp.split(z, 2, axis=-1)
    v = rms_norm(v, g_v)
    n = L // SG_CHUNK
    vg = v.reshape(B, n, SG_CHUNK, SG_GROUPS, SG_GROUP_DIM)
    mixed = jnp.einsum("gpq,bnqgc->bnpgc", w_s, vg) + b_s.T[None, None, :, :, None]
    return (u * mixed.reshape(B, L, SG_DIM)) @ w_out

def axial_rope(L):
    t = jnp.arange(L)
    row = (t // GRID_W).astype(jnp.float32)
    col = (t % GRID_W).astype(jnp.float32)
    n_freq = ATT_HEAD_DIM // 4
    inv_freq = ROPE_THETA ** (-jnp.arange(n_freq, dtype=jnp.float32) / n_freq)
    ang = jnp.concatenate([row[:, None] * inv_freq, col[:, None] * inv_freq], axis=-1)
    return jnp.cos(ang), jnp.sin(ang)

def apply_rope(x, cos, sin):
    xf = x.astype(jnp.float32)
    x1, x2 = jnp.split(xf, 2, axis=-1)
    c = cos[None, :, None, :]
    s = sin[None, :, None, :]
    return jnp.concatenate([x1 * c - x2 * s, x1 * s + x2 * c], axis=-1).astype(x.dtype)

def _gqa_attend(q, k, v):
    s = jnp.einsum("bqkgd,bskd->bkgqs", q, k).astype(jnp.float32) * (ATT_HEAD_DIM ** -0.5)
    p = jax.nn.softmax(s, axis=-1).astype(v.dtype)
    return jnp.einsum("bkgqs,bskd->bqkgd", p, v)

def gqa_mix(a_lat, a_ctx, w_qkv, g_q, g_k, w_out, need_ctx_out):
    B, L, _ = a_lat.shape
    H, KV, G, Dh = ATT_HEADS, ATT_KV_HEADS, ATT_GROUP, ATT_HEAD_DIM
    q, k, v = jnp.split(a_lat @ w_qkv, [H * Dh, (H + KV) * Dh], axis=-1)
    q = rms_norm(q.reshape(B, L, H, Dh), g_q)
    k = rms_norm(k.reshape(B, L, KV, Dh), g_k)
    v = v.reshape(B, L, KV, Dh)
    cos, sin = axial_rope(L)
    q = apply_rope(q, cos, sin)
    k = apply_rope(k, cos, sin)
    n_ctx = a_ctx.shape[1]
    kc, vc = jnp.split(a_ctx @ w_qkv[:, H * Dh:], 2, axis=-1)
    kc = rms_norm(kc.reshape(B, n_ctx, KV, Dh), g_k)
    vc = vc.reshape(B, n_ctx, KV, Dh)
    k_all = jnp.concatenate([k, kc], axis=1)
    v_all = jnp.concatenate([v, vc], axis=1)
    nblk = L // ATT_Q_BLOCK
    q_blocks = q.reshape(B, nblk, ATT_Q_BLOCK, KV, G, Dh).swapaxes(0, 1)
    o = lax.map(lambda qb: _gqa_attend(qb, k_all, v_all), q_blocks)
    y_lat = o.swapaxes(0, 1).reshape(B, L, H * Dh) @ w_out
    y_ctx = None
    if need_ctx_out:
        qc = rms_norm((a_ctx @ w_qkv[:, :H * Dh]).reshape(B, n_ctx, H, Dh), g_q)
        oc = _gqa_attend(qc.reshape(B, n_ctx, KV, G, Dh), kc, vc)
        y_ctx = oc.reshape(B, n_ctx, H * Dh) @ w_out
    return y_lat, y_ctx

def neighbourhood_mix(a_lat, a_ctx, w_qkv, rpb, w_out, need_ctx_out):
    B, L, D = a_lat.shape
    H, Dh = NA_HEADS, NA_HEAD_DIM
    rows = L // GRID_W
    kh = min(NA_WIN_ROWS, rows)
    kw = NA_WIN_COLS
    scale = Dh ** -0.5
    q, k, v = jnp.split(a_lat @ w_qkv, 3, axis=-1)
    n_ctx = a_ctx.shape[1]
    kc, vc = jnp.split(a_ctx @ w_qkv[:, D:], 2, axis=-1)
    kc = kc.reshape(B, n_ctx, H, Dh)
    vc = vc.reshape(B, n_ctx, H, Dh)
    k_grid = k.reshape(B, rows, GRID_W, H, Dh)
    v_grid = v.reshape(B, rows, GRID_W, H, Dh)
    col = jnp.arange(GRID_W)
    col_start = jnp.clip(col - kw // 2, 0, GRID_W - kw)
    col_idx = col_start[:, None] + jnp.arange(kw)[None, :]
    col_off = col_idx - col[:, None] + (NA_WIN_COLS - 1)
    q_rows = q.reshape(B, rows, GRID_W, H, Dh).swapaxes(0, 1)

    def row_block(args):
        r, q_r = args
        r_start = jnp.clip(r - kh // 2, 0, rows - kh)
        k_r = lax.dynamic_slice_in_dim(k_grid, r_start, kh, axis=1)[:, :, col_idx]
        v_r = lax.dynamic_slice_in_dim(v_grid, r_start, kh, axis=1)[:, :, col_idx]
        row_off = r_start + jnp.arange(kh) - r + (NA_WIN_ROWS - 1)
        bias = rpb[:, row_off[:, None, None], col_off[None, :, :]].astype(jnp.float32)
        s_nb = jnp.einsum("bwhd,bawjhd->bhwaj", q_r, k_r).astype(jnp.float32) * scale
        s_nb = (s_nb + bias.transpose(0, 2, 1, 3)[None]).reshape(B, H, GRID_W, kh * kw)
        s_ctx = jnp.einsum("bwhd,bchd->bhwc", q_r, kc).astype(jnp.float32) * scale
        p = jax.nn.softmax(jnp.concatenate([s_nb, s_ctx], axis=-1), axis=-1).astype(q_r.dtype)
        p_nb = p[..., :kh * kw].reshape(B, H, GRID_W, kh, kw)
        p_ctx = p[..., kh * kw:]
        return (jnp.einsum("bhwaj,bawjhd->bwhd", p_nb, v_r)
                + jnp.einsum("bhwc,bchd->bwhd", p_ctx, vc))

    o = lax.map(row_block, (jnp.arange(rows), q_rows))
    y_lat = o.swapaxes(0, 1).reshape(B, L, D) @ w_out
    y_ctx = None
    if need_ctx_out:
        qc = (a_ctx @ w_qkv[:, :D]).reshape(B, n_ctx, H, Dh)
        s = jnp.einsum("bqhd,bkhd->bhqk", qc, kc).astype(jnp.float32) * scale
        p = jax.nn.softmax(s, axis=-1).astype(vc.dtype)
        y_ctx = jnp.einsum("bhqk,bkhd->bqhd", p, vc).reshape(B, n_ctx, D) @ w_out
    return y_lat, y_ctx

def _normal(k, shape, scale):
    return jax.random.normal(k, shape, jnp.float32) * scale

def first_inputs(seed: int = 0) -> dict:
    key = jax.random.key(seed)
    ks = iter(jax.random.split(key, 32))
    D = D_MODEL
    inv = D ** -0.5
    n_a, n_b, n_c, n_d = (_layers_using(m) for m in range(N_MIXERS))
    qkv_dim = (ATT_HEADS + 2 * ATT_KV_HEADS) * ATT_HEAD_DIM
    return {
        "x": _normal(next(ks), (BATCH, SEQ, D), 1.0),
        "c": _normal(next(ks), (BATCH, D), 1.0),
        "ctx": _normal(next(ks), (BATCH, CTX_LEN, D), 1.0),
        "c_ctx": _normal(next(ks), (D,), 1.0),
        "w_mod": _normal(next(ks), (DEPTH, D, N_MOD * D), 0.5 * inv),
        "b_mod": _normal(next(ks), (DEPTH, N_MOD * D), 0.01),
        "g_norm_mix": 1.0 + _normal(next(ks), (DEPTH, D), 0.02),
        "g_norm_ffn": 1.0 + _normal(next(ks), (DEPTH, D), 0.02),
        "w_ffn_up": _normal(next(ks), (DEPTH, D, 2 * FFN_DIM), inv),
        "w_ffn_conv": _normal(next(ks), (DEPTH, FFN_CONV, FFN_DIM), FFN_CONV ** -0.5),
        "b_ffn_conv": _normal(next(ks), (DEPTH, FFN_DIM), 0.01),
        "w_ffn_down": _normal(next(ks), (DEPTH, FFN_DIM, D), FFN_DIM ** -0.5),
        "w_fnet_out": _normal(next(ks), (n_a, D, D), inv),
        "w_na_qkv": _normal(next(ks), (n_b, D, 3 * D), inv),
        "na_rel_bias": _normal(next(ks), (n_b, NA_HEADS, 2 * NA_WIN_ROWS - 1, 2 * NA_WIN_COLS - 1), 0.1),
        "w_na_out": _normal(next(ks), (n_b, D, D), inv),
        "w_sg_in": _normal(next(ks), (n_c, D, 2 * SG_DIM), inv),
        "g_sg_v": 1.0 + _normal(next(ks), (n_c, SG_DIM), 0.02),
        "w_sg_spatial": _normal(next(ks), (n_c, SG_GROUPS, SG_CHUNK, SG_CHUNK), SG_CHUNK ** -0.5),
        "b_sg_spatial": 1.0 + _normal(next(ks), (n_c, SG_GROUPS, SG_CHUNK), 0.01),
        "w_sg_out": _normal(next(ks), (n_c, SG_DIM, D), SG_DIM ** -0.5),
        "w_att_qkv": _normal(next(ks), (n_d, D, qkv_dim), inv),
        "g_att_q": 1.0 + _normal(next(ks), (n_d, ATT_HEAD_DIM), 0.02),
        "g_att_k": 1.0 + _normal(next(ks), (n_d, ATT_HEAD_DIM), 0.02),
        "w_att_out": _normal(next(ks), (n_d, ATT_HEADS * ATT_HEAD_DIM, D), (ATT_HEADS * ATT_HEAD_DIM) ** -0.5),
        "g_final": 1.0 + _normal(next(ks), (D,), 0.02),
    }

def first_block(x, c, ctx, c_ctx, w_mod, b_mod, g_norm_mix, g_norm_ffn, w_ffn_up, w_ffn_conv, b_ffn_conv,
              w_ffn_down, w_fnet_out, w_na_qkv, na_rel_bias, w_na_out, w_sg_in, g_sg_v, w_sg_spatial,
              b_sg_spatial, w_sg_out, w_att_qkv, g_att_q, g_att_k, w_att_out, g_final):
    h_lat, h_ctx = x, ctx
    for i in range(DEPTH):
        m, j = i % N_MIXERS, i // N_MIXERS
        last = i == DEPTH - 1
        ctx_in_needed = (not last) or m in (1, 3)
        sh1, sc1, gt1, sh2, sc2, gt2 = ada_params(c, w_mod[i], b_mod[i])
        a_lat = modulate(h_lat, g_norm_mix[i], sh1, sc1)
        if ctx_in_needed:
            csh1, csc1, cgt1, csh2, csc2, cgt2 = ada_params(c_ctx[None, :], w_mod[i], b_mod[i])
            a_ctx = modulate(h_ctx, g_norm_mix[i], csh1, csc1)
        if m == 0:
            y_lat = fourier_mix(a_lat, w_fnet_out[j])
            y_ctx = None if last else fourier_mix(a_ctx, w_fnet_out[j])
        elif m == 1:
            y_lat, y_ctx = neighbourhood_mix(a_lat, a_ctx, w_na_qkv[j], na_rel_bias[j], w_na_out[j], not last)
        elif m == 2:
            y_lat = spatial_gating_mix(a_lat, w_sg_in[j], g_sg_v[j], w_sg_spatial[j], b_sg_spatial[j], w_sg_out[j])
            y_ctx = None if last else spatial_gating_mix(a_ctx, w_sg_in[j], g_sg_v[j], w_sg_spatial[j],
                                                         b_sg_spatial[j], w_sg_out[j])
        else:
            y_lat, y_ctx = gqa_mix(a_lat, a_ctx, w_att_qkv[j], g_att_q[j], g_att_k[j], w_att_out[j], not last)
        h_lat = h_lat + gt1 * y_lat
        h_lat = h_lat + gt2 * conv_ffn(modulate(h_lat, g_norm_ffn[i], sh2, sc2),
                                       w_ffn_up[i], w_ffn_conv[i], b_ffn_conv[i], w_ffn_down[i])
        if not last:
            h_ctx = h_ctx + cgt1 * y_ctx
            h_ctx = h_ctx + cgt2 * conv_ffn(modulate(h_ctx, g_norm_ffn[i], csh2, csc2),
                                           w_ffn_up[i], w_ffn_conv[i], b_ffn_conv[i], w_ffn_down[i])
    return rms_norm(h_lat, g_final)


CONV_WIDTH = D_MODEL
CONV_K = 3
RET_HEADS = 4
RET_QK_DIM = D_MODEL // RET_HEADS
RET_V_DIM = 2 * RET_QK_DIM
RET_QK = RET_HEADS * RET_QK_DIM
RET_V = RET_HEADS * RET_V_DIM
CHUNK = 128
ROPE_BASE = 10000.0
D_FF = -(-8 * D_MODEL // (3 * 256)) * 256
IN_SIZES = (CONV_WIDTH, CONV_WIDTH, CONV_WIDTH, RET_QK, RET_QK, RET_V, RET_V, D_MODEL, D_MODEL)
N_IN = sum(IN_SIZES)


def rmsnorm(x, g):
    xf = x.astype(jnp.float32)
    y = xf * lax.rsqrt(jnp.mean(xf * xf, axis=-1, keepdims=True) + EPS)
    return (y * g.astype(jnp.float32)).astype(x.dtype)

def rotary(t):
    s, d = t.shape[1], t.shape[-1]
    pos = jnp.arange(s, dtype=jnp.float32)
    freqs = ROPE_BASE ** (-jnp.arange(0, d, 2, dtype=jnp.float32) / d)
    ang = pos[:, None] * freqs[None, :]
    cos = jnp.cos(ang)[None, :, None, :]
    sin = jnp.sin(ang)[None, :, None, :]
    t1, t2 = t[..., : d // 2], t[..., d // 2:]
    return jnp.concatenate([t1 * cos - t2 * sin, t1 * sin + t2 * cos], axis=-1)

def retention_chunkwise(q, k, v, log_gamma, strict):
    b, h, s, dk = q.shape
    dv = v.shape[-1]
    n_chunks = s // CHUNK

    def chunks(t):
        return jnp.moveaxis(t.reshape(b, h, n_chunks, CHUNK, t.shape[-1]), 2, 0)

    idx = jnp.arange(CHUNK, dtype=jnp.float32)
    diff = idx[:, None] - idx[None, :]
    mask = (diff > 0) if strict else (diff >= 0)
    lg = log_gamma[:, None, None]
    intra_decay = jnp.where(mask[None], jnp.exp(jnp.maximum(diff, 0.0)[None] * lg), 0.0)
    xi = jnp.exp((idx + 1.0)[None, :] * log_gamma[:, None])[..., None]
    zeta = jnp.exp((CHUNK - 1.0 - idx)[None, :] * log_gamma[:, None])[..., None]
    chunk_decay = jnp.exp(CHUNK * log_gamma)[:, None, None]

    def step(state, qkv):
        qc, kc, vc = qkv
        scores = jnp.einsum('bhcd,bhmd->bhcm', qc, kc) * intra_decay
        inner = jnp.einsum('bhcm,bhme->bhce', scores, vc)
        cross = jnp.einsum('bhcd,bhde->bhce', qc, state) * xi
        state = chunk_decay * state + jnp.einsum('bhcd,bhce->bhde', kc * zeta, vc)
        return state, inner + cross

    state0 = jnp.zeros((b, h, dk, dv), jnp.float32)
    _, out = lax.scan(step, state0, (chunks(q), chunks(k), chunks(v)))
    return jnp.moveaxis(out, 0, 2).reshape(b, h, s, dv)

def second_inputs(seed: int = 0) -> dict:
    key = jax.random.key(seed)
    ks = jax.random.split(key, 16)
    f32 = jnp.float32

    def normal(k, shape, scale):
        return jax.random.normal(k, shape, f32) * scale

    def gain(k, shape):
        return 1.0 + 0.05 * jax.random.normal(k, shape, f32)

    base_logit = jnp.log(2.0 ** (5.0 + jnp.arange(RET_HEADS, dtype=f32)) - 1.0)
    return {
        "x": jax.random.normal(ks[0], (BATCH, SEQ, D_MODEL), f32),
        "g_mix": gain(ks[1], (DEPTH, D_MODEL)),
        "w_in": normal(ks[2], (DEPTH, D_MODEL, N_IN), D_MODEL ** -0.5),
        "w_conv": normal(ks[3], (DEPTH, CONV_K, CONV_WIDTH), CONV_K ** -0.5),
        "dec_f": base_logit[None] + 0.01 * jax.random.normal(ks[4], (DEPTH, RET_HEADS), f32),
        "dec_b": base_logit[None] + 0.01 * jax.random.normal(ks[5], (DEPTH, RET_HEADS), f32),
        "g_ret": gain(ks[6], (DEPTH, RET_V)),
        "w_a_out": normal(ks[7], (DEPTH, CONV_WIDTH, D_MODEL), CONV_WIDTH ** -0.5),
        "w_r_out": normal(ks[8], (DEPTH, RET_V, D_MODEL), RET_V ** -0.5),
        "w_o": normal(ks[9], (DEPTH, D_MODEL, D_MODEL), D_MODEL ** -0.5),
        "g_ffn": gain(ks[10], (DEPTH, D_MODEL)),
        "w_ff_gate": normal(ks[11], (DEPTH, D_MODEL, D_FF), D_MODEL ** -0.5),
        "w_ff_up": normal(ks[12], (DEPTH, D_MODEL, D_FF), D_MODEL ** -0.5),
        "w_ff_down": normal(ks[13], (DEPTH, D_FF, D_MODEL), D_FF ** -0.5),
        "g_final": gain(ks[14], (D_MODEL,)),
    }

def second_block(x, g_mix, w_in, w_conv, dec_f, dec_b, g_ret, w_a_out, w_r_out, w_o,
              g_ffn, w_ff_gate, w_ff_up, w_ff_down, g_final):
    b, s, _ = x.shape
    dt = x.dtype
    split_points = [int(p) for p in np.cumsum(IN_SIZES)[:-1]]
    for l in range(DEPTH):
        h = rmsnorm(x, g_mix[l])
        proj = h @ w_in[l]
        xc, gb, gc, q, k, v, g_sw, gate_a, gate_r = jnp.split(proj, split_points, axis=-1)

        u = gc * xc
        u_pad = jnp.pad(u, ((0, 0), (CONV_K // 2, CONV_K // 2), (0, 0)))
        conv = u_pad[:, 0:s] * w_conv[l, 0]
        for tap in range(1, CONV_K):
            conv = conv + u_pad[:, tap:tap + s] * w_conv[l, tap]
        y_a = (gb * conv) @ w_a_out[l]

        qf = rotary(q.reshape(b, s, RET_HEADS, RET_QK_DIM).astype(jnp.float32)) * (RET_QK_DIM ** -0.5)
        kf = rotary(k.reshape(b, s, RET_HEADS, RET_QK_DIM).astype(jnp.float32))
        vf = v.reshape(b, s, RET_HEADS, RET_V_DIM).astype(jnp.float32)
        qf, kf, vf = (jnp.transpose(t, (0, 2, 1, 3)) for t in (qf, kf, vf))
        lg_f = jax.nn.log_sigmoid(dec_f[l].astype(jnp.float32))
        lg_b = jax.nn.log_sigmoid(dec_b[l].astype(jnp.float32))
        ret_f = retention_chunkwise(qf, kf, vf, lg_f, strict=False)
        ret_b = jnp.flip(retention_chunkwise(jnp.flip(qf, 2), jnp.flip(kf, 2), jnp.flip(vf, 2),
                                             lg_b, strict=True), 2)
        ret = ret_f + ret_b
        mu = jnp.mean(ret, axis=-1, keepdims=True)
        var = jnp.mean(jnp.square(ret - mu), axis=-1, keepdims=True)
        ret = (ret - mu) * lax.rsqrt(var + EPS)
        ret = jnp.transpose(ret, (0, 2, 1, 3)).reshape(b, s, RET_V) * g_ret[l].astype(jnp.float32)
        y_r = (ret.astype(dt) * jax.nn.silu(g_sw)) @ w_r_out[l]

        merged = jax.nn.sigmoid(gate_a) * y_a + jax.nn.sigmoid(gate_r) * y_r
        x = x + merged @ w_o[l]

        h2 = rmsnorm(x, g_ffn[l])
        x = x + (jax.nn.silu(h2 @ w_ff_gate[l]) * (h2 @ w_ff_up[l])) @ w_ff_down[l]
    return rmsnorm(x, g_final)


def setup_inputs(seed=0):
    out = dict(first_inputs(seed))
    for name, value in second_inputs(seed + 1).items():
        if name != "x":
            out[name + "_2"] = value
    return out


def reference(
    x, c, ctx, c_ctx, w_mod, b_mod, g_norm_mix, g_norm_ffn, w_ffn_up, w_ffn_conv, b_ffn_conv,
    w_ffn_down, w_fnet_out, w_na_qkv, na_rel_bias, w_na_out, w_sg_in, g_sg_v, w_sg_spatial,
    b_sg_spatial, w_sg_out, w_att_qkv, g_att_q, g_att_k, w_att_out, g_final, g_mix_2, w_in_2,
    w_conv_2, dec_f_2, dec_b_2, g_ret_2, w_a_out_2, w_r_out_2, w_o_2, g_ffn_2, w_ff_gate_2,
    w_ff_up_2, w_ff_down_2, g_final_2,
):
    x = first_block(
        x, c, ctx, c_ctx, w_mod, b_mod, g_norm_mix, g_norm_ffn, w_ffn_up, w_ffn_conv,
        b_ffn_conv, w_ffn_down, w_fnet_out, w_na_qkv, na_rel_bias, w_na_out, w_sg_in, g_sg_v,
        w_sg_spatial, b_sg_spatial, w_sg_out, w_att_qkv, g_att_q, g_att_k, w_att_out, g_final,
    )
    return second_block(
        x, g_mix_2, w_in_2, w_conv_2, dec_f_2, dec_b_2, g_ret_2, w_a_out_2, w_r_out_2, w_o_2,
        g_ffn_2, w_ff_gate_2, w_ff_up_2, w_ff_down_2, g_final_2,
    )


_drawn_inputs = setup_inputs


def setup_inputs(seed=0):
    import zlib

    import numpy as np

    out = dict(_drawn_inputs(seed))
    spreads = {}
    factors = {'b_mod': 3.503,
     'g_norm_mix': 8.0,
     'g_norm_ffn': 6.199,
     'b_ffn_conv': 21.598,
     'g_ret_2': 3.775}
    for name, (base, spread) in spreads.items():
        noise = np.random.default_rng([zlib.crc32(name.encode()), seed]).standard_normal(out[name].shape)
        drawn = base * np.exp(spread * noise) if base else spread * noise
        out[name] = jnp.asarray(drawn.astype(out[name].dtype))
    for name, factor in factors.items():
        out[name] = (out[name] * factor).astype(out[name].dtype)
    return out
```

```python
from contextlib import ExitStack

import numpy as np
import concourse.bass as bass
from concourse import mybir

P = 128
D = 1024
T = 512
KT = D // P
TT = T // P
FF = 2816
FT = FF // P
GROUP = 256
HEADS, QK, V = 4, 256, 512
QT, VT = QK // P, V // P
EPS = 1e-6
PANEL = 8 * P
RAW, SPLIT = 4, 2
MODC = 512
MODN = 6 * D // MODC
PAIR = 2
QUAD = 4
DOWN = FT // 2
REL = T + (TT - 1) * P

FNET = 0
UP = [FNET + KT, 0]
DN = [UP[0] + PAIR * FT, 0]
MIX = DN[0] + 2 * DOWN
GATE = MIX + 3 * KT
HEAD0 = GATE + 2 * KT
HEAD1 = HEAD0 + 2 * QT + VT + KT + VT
HEADP = 2 * QT + VT + VT + VT
ROUT = HEAD1 + (HEADS - 1) * HEADP
WO = ROUT + VT
UP[1] = WO + KT
DN[1] = UP[1] + PAIR * FT
PANELS = DN[1] + 2 * DOWN

XC, GB, GC, WQ, WK, WV, GSW, GA, GR = np.cumsum([0, D, D, D, D, D, 2 * D, 2 * D, D]).tolist()

VECTORS = [("c", KT), ("b_mod", 6 * KT), ("g_norm_mix", KT),
           ("g_norm_ffn", KT), ("g_final", KT),
           ("w_ffn_conv", 3 * FT), ("b_ffn_conv", FT), ("g_mix_2", KT), ("w_conv_2", 3 * KT),
           ("g_ret_2", HEADS * VT), ("g_ffn_2", KT), ("g_final_2", KT)]
AT, _n = {}, 0
for _name, _count in VECTORS:
    AT[_name] = _n
    _n += _count
COLS = _n
EARLY = AT["g_norm_ffn"]

S_XR, S_DFT, S_DFTD, S_U = 0, 8, 12, 14
S_CONV, S_RET, S_MERGE, S_Q, S_K, S_V, S_S = 0, 0, 4, 8, 10, 12, 16


def tables():
    l, k = np.arange(T)[:, None], np.arange(T // 2 + 1)[None]
    ang = 2 * np.pi * ((l * k) % T) / T
    dft_tokens = np.concatenate([np.cos(ang), np.sin(ang[:, 1:T // 2])], axis=1)
    d = np.arange(GROUP)
    ang = 2 * np.pi * ((d[:, None] * d[None]) % GROUP) / GROUP
    dft_features = np.concatenate([np.cos(ang), np.sin(ang)], axis=1) / np.sqrt(T * GROUP)
    freqs = np.float32(10000.0) ** (-np.arange(0, QK, 2, dtype=np.float32) / np.float32(QK))
    ang = (freqs[:, None] * np.arange(T, dtype=np.float32)[None]).astype(np.float32).astype(np.float64)
    rope = np.stack([np.cos(ang), np.sin(ang)])
    relative = np.arange(REL)[None] - (TT - 1) * P - np.arange(P)[:, None]
    made = {"dft_tokens": dft_tokens, "dft_features": dft_features, "rope": rope, "relative": relative,
            "identity": np.eye(P)}
    return {n: np.ascontiguousarray(v.astype(np.float32)) for n, v in made.items()}


def build(nc, t, out):
    F32, F32R = mybir.dt.float32, mybir.dt.float32r
    ALU, ACT = mybir.AluOpType, mybir.ActivationFunctionType
    MUL, ADD, SUB = ALU.mult, ALU.add, ALU.subtract
    ds = bass.ds
    ctx = ExitStack()
    with ctx:
        def sb(name, shape, dt=F32):
            return ctx.enter_context(nc.sbuf_tensor(name, shape, dt))

        def sem(name):
            return ctx.enter_context(nc.semaphore(name))

        res = sb("res", [P, KT, T])
        act_hi, act_lo = sb("act_hi", [P, KT, T], F32R), sb("act_lo", [P, KT, T], F32R)
        wide_hi, wide_lo = sb("wide_hi", [P, FT, T], F32R), sb("wide_lo", [P, FT, T], F32R)
        gates = sb("gates", [P, 2 * KT, T])
        raw = sb("raw", [P, RAW, PANEL])
        w_hi, w_lo = sb("w_hi", [P, SPLIT, PANEL], F32R), sb("w_lo", [P, SPLIT, PANEL], F32R)
        tmp = sb("tmp", [P, 7, T])
        rope = sb("rope", [P, 2, T])
        decay = sb("decay", [P, REL])
        cols = sb("cols", [P, COLS - EARLY])
        lg = sb("lg", [P, 2 * HEADS])
        mod = sb("mod", [P, 6 * KT])
        gain_ffn, gain_12 = sb("gain_ffn", [P, KT]), sb("gain_12", [P, KT])
        small = sb("small", [P, 8, TT])
        eps, zero = sb("eps", [P, 1]), sb("zero", [P, 1])
        ones = sb("ones", [P, P])
        ident = sb("ident", [P, P])
        ps = ctx.enter_context(nc.psum_tensor("ps", [P, 8, T], F32))

        early = tmp[:, 4, :]
        dec, silu_c, gain_mix, shift_dc, udc = (early[:, EARLY + 8 * i:EARLY + 8 * (i + 1)] for i in range(5))
        lgt = early[:, EARLY + 40:EARLY + 80].rearrange("p (i n) -> p i n", i=5)

        x_tok = res[:, :, :].rearrange("p k t -> p (k t)").rearrange("p (a d) -> p a d", a=TT)
        xr_hi, xr_lo = (w[:, S_XR:S_XR + 2 * TT, :].rearrange("p s t -> p (s t)").rearrange("p (a d) -> p a d", a=TT)
                        for w in (wide_hi, wide_lo))
        modw = gates[:, :, :].rearrange("p s t -> p (s t)").rearrange("p (s k n) -> p s k n", s=4, k=KT // 2)
        modacc = tmp[:, 5:7, :]
        tmp_wide = tmp[:, 5:7, :].rearrange("p s t -> p (s t)")[:, 0:REL]

        def col(name, i=0):
            return cols[:, ds(i + AT[name] - EARLY, 1)]

        def early_cols(name, i, n):
            return early[:, AT[name] + i:AT[name] + i + n]

        def late_cols(name, n):
            return cols[:, AT[name] - EARLY:AT[name] - EARLY + n]

        def f32(ap):
            return ap.bitcast(F32)

        x_loaded = [sem(f"x_loaded{i}") for i in range(TT)]
        early_loaded, dft_loaded, dftd_loaded, cols_loaded, dec_loaded = sem("early_loaded"), sem("dft_loaded"), sem("dftd_loaded"), sem("cols_loaded"), sem("dec_loaded")
        rope_loaded, ident_loaded, xt_loaded, rel_loaded = sem("rope_loaded"), sem("ident_loaded"), sem("xt_loaded"), sem("rel_loaded")
        modw_loaded = [sem(f"modw_loaded{i}") for i in range(4)]
        raw_loaded = [sem(f"raw_loaded{i}") for i in range(RAW)]
        dft_hi_made, dft_split = sem("dft_hi_made"), sem("dft_split")
        hi_made, split_done, panel_used = sem("hi_made"), sem("split_done"), sem("panel_used")
        consts_set = sem("consts_set")
        chain, act_chain = sem("chain"), sem("act_chain")
        silu_c_made, x_squared, x_std, x_rstd = sem("silu_c_made"), sem("x_squared"), sem("x_std"), sem("x_rstd")
        xr_hi_made, xr_made = sem("xr_hi_made"), sem("xr_made")
        lg_exp, lg_made = sem("lg_exp"), sem("lg_made")
        mod_step, mod_summed, u_scale_made, gate2_made = sem("mod_step"), sem("mod_summed"), sem("u_scale_made"), sem("gate2_made")
        res_scaled, sums_ready, o_recip = sem("res_scaled"), sem("sums_ready"), sem("o_recip")
        u_done, u_hi_made, u_made = sem("u_done"), sem("u_hi_made"), sem("u_made")
        f_done, f_q_copied, f_made, f_hi_made = sem("f_done"), sem("f_q_copied"), sem("f_made"), sem("f_hi_made")
        act_ready = sem("act_ready")
        fnet_done, fnet_free = sem("fnet_done"), sem("fnet_free")
        res_squared, squares_added = sem("res_squared"), sem("squares_added")
        norm_summed, norm_std, norm_rstd = sem("norm_summed"), sem("norm_std"), sem("norm_rstd")
        norm_spread, normed, norm_hi_made = sem("norm_spread"), sem("normed"), sem("norm_hi_made")
        up_done, conv_step, silu_made, prod_made, prod_hi_made, wide_ready = (
            [sem(f"{n}{f}") for f in range(2)]
            for n in ("up_done", "conv_step", "silu_made", "prod_made", "prod_hi_made", "wide_ready"))
        dn_done, dn_free = [sem("dn_done0"), sem("dn_done1")], [sem("dn_free0"), sem("dn_free1")]
        mix_done, xc_copied, mix_step, mix_free, mix_hi_made, mix_ready = (
            sem(n) for n in ("mix_done", "xc_copied", "mix_step", "mix_free", "mix_hi_made", "mix_ready"))
        gate_done, gate_free = sem("gate_done"), sem("gate_free")
        decay_args, decay_made = sem("decay_args"), sem("decay_made")
        qk_done, rot_step, rot_made, rot_hi_made, rot_ready = (
            sem(n) for n in ("qk_done", "rot_step", "rot_made", "rot_hi_made", "rot_ready"))
        v_done, v_summed, v_mean, v_hi_made, v_ready = (sem(n) for n in ("v_done", "v_summed", "v_mean", "v_hi_made", "v_ready"))
        s_done, s_decayed, s_hi_made, s_ready = (sem(n) for n in ("s_done", "s_decayed", "s_hi_made", "s_ready"))
        mid_done, mid_free, mid_added = sem("mid_done"), sem("mid_free"), sem("mid_added")
        o_done, o_squared, o_added, o_summed, o_std, o_rstd, o_spread = (
            sem(n) for n in ("o_done", "o_squared", "o_added", "o_summed", "o_std", "o_rstd", "o_spread"))
        gsw_done, gsw_silu, o_gated, ret_made, ret_hi_made, ret_ready = (
            sem(n) for n in ("gsw_done", "gsw_silu", "o_gated", "ret_made", "ret_hi_made", "ret_ready"))
        merge_hi_made, merge_ready = sem("merge_hi_made"), sem("merge_ready")
        wo_done, wo_free = sem("wo_done"), sem("wo_free")
        out_made, out_stored = sem("out_made"), sem("out_stored")

        block = ctx.enter_context(nc.Block())

        @block.sync
        def _(sp):
            def view(w, k):
                return w.rearrange("(k p) n -> p k n", k=k)

            w_up = view(t["w_ffn_up"], KT)
            w_in = view(t["w_in_2"], KT)
            w_out_r = t["w_r_out_2"].rearrange("(h k p) n -> p h k n", h=HEADS, k=VT)

            def panel(p, slot, src, blocks, first=False):
                if not first:
                    sp.wait_ge(split_done, p - RAW + 1)
                dst = raw[:, slot, :].rearrange("p (k n) -> p k n", k=blocks)
                sp.dma_start(dst, src).then_inc(raw_loaded[slot], 16)

            def mod_chunk(c):
                for half in range(2):
                    n, k0 = 2 * c + half, half * (KT // 2)
                    if n >= 4:
                        sp.wait_ge(mod_step, (n - 3) * (KT // 2))
                    sp.dma_start(modw[:, n % 4, :, :], view(t["w_mod"], KT)[:, k0:k0 + KT // 2, c * MODC:(c + 1) * MODC]
                                 ).then_inc(modw_loaded[n % 4], 16)

            w_fnet = view(t["w_fnet_out"], KT)

            def fnet_panel(m):
                panel(FNET + m, m % RAW, w_fnet[:, :, m * P:(m + 1) * P], KT, first=m < RAW)

            sp.dma_start(early[:, 0:EARLY], t["columns"][:, 0:EARLY]).then_inc(early_loaded, 16)
            sp.dma_start(x_tok[:, 0, :], t["x"][0:P, :]).then_inc(x_loaded[0], 16)
            sp.dma_start(raw[:, 0:2, :].rearrange("p s n -> p (s n)").rearrange("p (k n) -> p k n", k=TT),
                         view(t["dft_tokens"], TT)).then_inc(dft_loaded, 16)
            for a in range(1, TT):
                sp.dma_start(x_tok[:, a, :], t["x"][a * P:(a + 1) * P, :]).then_inc(x_loaded[a], 16)
            mod_chunk(0)
            mod_chunk(1)
            sp.dma_start(raw[:, 2, :].rearrange("p (k n) -> p k n", k=2), view(t["dft_features"], 2)).then_inc(dftd_loaded, 16)
            mod_chunk(2)
            mod_chunk(3)
            sp.wait_ge(dft_split, 3)
            fnet_panel(0)
            fnet_panel(1)
            mod_chunk(4)
            mod_chunk(5)
            sp.dma_start(cols[:, :], t["columns"][:, EARLY:]).then_inc(cols_loaded, 16)
            sp.dma_start(ident[:, :], t["identity"]).then_inc(ident_loaded, 16)
            sp.dma_start(dec, t["decays"]).then_inc(dec_loaded, 16)
            sp.wait_ge(xr_made, TT)
            sp.wait_ge(xr_hi_made, TT)
            sp.dma_start(res[:, :, :], view(t["x_t"], KT)).then_inc(xt_loaded, 16)
            for m in range(2, KT):
                fnet_panel(m)
                if m < 6:
                    mod_chunk(m + 4)
            sp.dma_start(rope[:, :, :], t["rope"].rearrange("s p n -> p s n")).then_inc(rope_loaded, 16)

            def up_panels(f, j, u):
                base = UP[f] + PAIR * j
                slot = (UP[f] + PAIR * u) % RAW
                if f == 0:
                    g, v = w_up[:, :, ds(j * P, P)], w_up[:, :, ds(j * P + FF, P)]
                else:
                    g, v = (view(t[n], KT)[:, :, ds(j * P, P)] for n in ("w_ff_gate_2", "w_ff_up_2"))
                panel(base, slot, g, KT)
                panel(base + 1, (slot + 1) % RAW, v, KT)

            def ffn_panels(f, w_down, peel=0):
                for j in range(peel):
                    up_panels(f, j, j % 2)
                if peel:
                    mod_chunk(10)
                    mod_chunk(11)
                with sp.Fori(peel // 2, FT // 2) as i:
                    for u in range(2):
                        up_panels(f, i * 2 + u, u)
                w_dn = view(w_down, FT)
                for q in range(2):
                    for k in range(DOWN):
                        p = DN[f] + q * DOWN + k
                        panel(p, p % RAW, w_dn[:, 2 * k:2 * k + 2, q * QUAD * P:(q + 1) * QUAD * P], 2)

            ffn_panels(0, t["w_ffn_down"], peel=2)

            with sp.Fori(0, KT // 4) as i:
                for u in range(12):
                    j = i * 4 + u // 3
                    panel(i * 12 + MIX + u, (MIX + u) % RAW, w_in[:, :, ds(j * P + (XC, GB, GC)[u % 3], P)], KT)
            with sp.Fori(0, 2 * KT // 4) as i:
                for u in range(4):
                    panel(i * 4 + GATE + u, (GATE + u) % RAW, w_in[:, :, ds(i * 4 * P + GA + u * P, P)], KT)

            def rel_table(h):
                if isinstance(h, int):
                    assert h == 0
                else:
                    sp.wait_ge(s_decayed, h * TT)
                sp.dma_start(decay[:, :], t["relative"]).then_inc(rel_loaded, 16)

            def head_projections(h, base, b0):
                for u in range(2 * QT):
                    src = w_in[:, :, ds(h * QK + (WQ, WK)[u // QT] + (u % QT) * P, P)]
                    panel(base + u, (b0 + u) % RAW, src, KT)
                for u in range(VT):
                    src = w_in[:, 2 * u:2 * u + 2, ds(h * V + WV, V)]
                    panel(base + 2 * QT + u, (b0 + u) % RAW, src, 2)

            def head_gate(h, base, b0):
                for u in range(VT):
                    panel(base + u, (b0 + u) % RAW, w_in[:, :, ds(h * V + GSW + u * P, P)], KT)

            def ret_out(h, base, b0):
                for u in range(VT):
                    if isinstance(h, int):
                        src = w_out_r[:, h, :, 2 * u * P:2 * (u + 1) * P]
                    else:
                        src = w_out_r[:, ds(h, 1), :, 2 * u * P:2 * (u + 1) * P].rearrange("p h k n -> p (h k) n")
                    panel(base + u, (b0 + u) % RAW, src, VT)

            rel_table(0)
            head_projections(0, HEAD0, HEAD0)
            w_a = view(t["w_a_out_2"], KT)
            for m in range(KT):
                p = HEAD0 + 2 * QT + VT + m
                panel(p, p % RAW, w_a[:, :, m * P:(m + 1) * P], KT)
            head_gate(0, HEAD1 - VT, HEAD1)
            with sp.Fori(1, HEADS) as h:
                base = h * HEADP + (HEAD1 - HEADP)
                rel_table(h)
                head_projections(h, base, HEAD1)
                ret_out(h - 1, base + 2 * QT + VT, HEAD1)
                head_gate(h, base + 2 * QT + 2 * VT, HEAD1)
            ret_out(HEADS - 1, ROUT, ROUT)
            w_o = view(t["w_o_2"], KT)
            for m in range(KT):
                panel(WO + m, (WO + m) % RAW, w_o[:, :, m * P:(m + 1) * P], KT)
            ffn_panels(1, t["w_ff_down_2"])
            for m in range(KT):
                sp.wait_ge(out_made, m + 1)
                sp.dma_start(out[m * P:(m + 1) * P, :], gates[:, m, :]).then_inc(out_stored, 16)
            sp.wait_ge(out_stored, 16 * KT)

        @block.gpsimd
        def _(pool):
            nc.gpsimd.memset(ones[:, :], 1.0).then_inc(consts_set, 1)
            nc.gpsimd.memset(zero[:, :], 0.0).then_inc(consts_set, 1)
            nc.gpsimd.memset(eps[:, :], EPS).then_inc(consts_set, 1)
            pool.wait_ge(consts_set, 3)
            for n, (slots, s0) in enumerate((((0, 1), S_DFT), ((1, 2), S_DFT + 2), ((2, 3), S_DFTD))):
                src = raw[:, slots[0], :]
                dst_hi, dst_lo = (w[:, s0:s0 + 2, :].rearrange("p s t -> p (s t)") for w in (wide_hi, wide_lo))
                if n != 1:
                    pool.wait_ge(dft_loaded if n == 0 else dftd_loaded, 16)
                nc.gpsimd.tensor_scalar(dst_hi, src, 1.0, 0.0, MUL, ADD).then_inc(dft_hi_made, 1)
                pool.wait_ge(dft_hi_made, n + 1)
                nc.gpsimd.tensor_tensor(dst_lo, src, f32(dst_hi), SUB).then_inc(dft_split, 1)

            def split(p, slot, two, loads, first=False):
                pool.wait_ge(raw_loaded[slot], loads)
                if not first:
                    pool.wait_ge(panel_used, p - SPLIT + 1)
                nc.gpsimd.tensor_tensor(w_hi[:, two, 0:1], raw[:, slot, 0:1], zero[:, :], ADD)
                nc.gpsimd.tensor_scalar(w_hi[:, two, 1:], raw[:, slot, 1:], 1.0, 0.0, MUL, ADD).then_inc(hi_made, 1)
                pool.wait_ge(hi_made, p + 1)
                nc.gpsimd.tensor_tensor(w_lo[:, two, :], raw[:, slot, :], f32(w_hi[:, two, :]), SUB).then_inc(split_done, 1)

            for p in range(RAW):
                split(p, p, p % SPLIT, 16, first=p < SPLIT)
            with pool.Fori(1, PANELS // RAW) as i:
                for u in range(RAW):
                    split(i * RAW + u, u, u % SPLIT, i * 16 + 16)

        @block.tensor
        def _(pe):
            mm = nc.tensor.matmul

            def product(o, w, wl, a, al, start, stop, opens=False):
                ins = mm(o, w, a, start=start, stop=False)
                if opens:
                    ins.then_inc(panel_used, 1)
                mm(o, wl, a, start=False, stop=False)
                return mm(o, w, al, start=False, stop=stop)

            def w_block(two, b, n=P):
                return w_hi[:, two, b * n:(b + 1) * n], w_lo[:, two, b * n:(b + 1) * n]

            def tile(o, p, two, a_hi, a_lo, ready=None, k=KT, part=0, parts=1):
                if part == 0:
                    pe.wait_ge(split_done, p + 1)
                for b in range(k):
                    if ready:
                        pe.wait_ge(ready[0], ready[1] + b + 1)
                    ins = product(o, *w_block(two, parts * b + part), a_hi[:, b, :], a_lo[:, b, :], b == 0, b == k - 1,
                                  opens=not (isinstance(p, int) and p == 0) and part == 0 and b == 0)
                return ins

            def dft_tokens(m, bank):
                for k in range(TT):
                    if m == 0:
                        pe.wait_ge(xr_made, k + 1)
                    ins = product(ps[:, bank, :], xr_hi[:, k, m * P:(m + 1) * P], xr_lo[:, k, m * P:(m + 1) * P],
                                  wide_hi[:, S_DFT + k, :], wide_lo[:, S_DFT + k, :], k == 0, k == TT - 1)
                ins.then_inc(u_done, 1)

            def mod_sums(c):
                pe.wait_ge(mod_step, KT * (c + 1))
                for u in range(MODC // P):
                    n = c * (MODC // P) + u
                    ins = mm(ps[:, 7, n:n + 1], modacc[:, c % 2, u * P:(u + 1) * P], ones[:, 0:1], start=True, stop=True)
                ins.then_inc(mod_summed, 1)

            pe.wait_ge(dft_split, 2)
            pe.wait_ge(consts_set, 3)
            for m in range(KT - 1):
                dft_tokens(m, m)
                if m >= 4:
                    mod_sums(m - 4)
            mod_sums(3)
            pe.wait_ge(u_made, 1)
            dft_tokens(KT - 1, 0)

            pe.wait_ge(dft_split, 3)
            half = T // 2
            for m in range(KT):
                if m < 3:
                    pe.wait_ge(u_made, 2 * m + 3)
                else:
                    pe.wait_ge(f_made, 3 * (m - 2))
                pe.wait_ge(u_made, m // 2 * 2 + 2)
                g, e = m // 2, m % 2
                for part, (c0, n) in enumerate(((0, half + 2), (half, half))):
                    for k in range(2):
                        sl = slice(part * GROUP + e * P, part * GROUP + (e + 1) * P)
                        ins = product(ps[:, 1 + 2 * (m % 3) + part, 0:n], wide_hi[:, S_DFTD + k, sl], wide_lo[:, S_DFTD + k, sl],
                                      wide_hi[:, S_U + 2 * g + k, c0:c0 + n], wide_lo[:, S_U + 2 * g + k, c0:c0 + n],
                                      k == 0, k == 1)
                ins.then_inc(f_done, 1)

            pe.wait_ge(f_made, 3 * KT)
            for m in range(KT):
                if m >= 4:
                    pe.wait_ge(fnet_free, m - 3)
                tile(ps[:, m % 4, :], FNET + m, m % 2, act_hi, act_lo, (act_ready, 0) if m == 0 else None
                     ).then_inc(fnet_done, 1)
                if m >= 2:
                    mod_sums(m + 2)

            def norm(n, sums, spreads, bank_sum, banks, s_in, n_in, s_sum, s_rstd, n_rstd, s_out):
                pe.wait_ge(s_in, n_in)
                for i, sq in enumerate(sums):
                    for a in range(TT):
                        ins = mm(ps[:, bank_sum, TT * i + a:TT * i + a + 1], sq[:, a * P:(a + 1) * P], ones[:, 0:1],
                                 start=True, stop=True)
                ins.then_inc(s_sum, 1)
                pe.wait_ge(s_rstd, n_rstd)
                for i, diag in enumerate(spreads):
                    for a in range(TT):
                        ins = mm(ps[:, banks[i], a * P:(a + 1) * P], ones[:, :], diag[:, a * P:(a + 1) * P],
                                 start=True, stop=True)
                ins.then_inc(s_out, 1)

            def ffn_up(f, act_base):
                def pair(j, u, first=False):
                    if not first:
                        pe.wait_ge(prod_made[f], j - 1)
                    for s in range(PAIR):
                        tile(ps[:, 2 * u + s, :], j * PAIR + UP[f] + s, s, act_hi, act_lo,
                             (act_ready, act_base) if first and u + s == 0 else None).then_inc(up_done[f], 1)

                for j in range(2):
                    pair(j, j, first=True)
                with pe.Fori(1, FT // 2) as i:
                    for u in range(2):
                        pair(i * 2 + u, u)

            def down_panel(f, q, k, two, p, order, start=False, stop=False, a0=None):
                pe.wait_ge(split_done, p + 1)
                if q == 0:
                    pe.wait_ge(wide_ready[f], k * 2 + 2)
                for n, (o, c) in enumerate(order):
                    a_hi, a_lo = (w[:, k * 2 + c, :] for w in (wide_hi, wide_lo))
                    ins = product(ps[:, 4 * q + o, :], *w_block(two, c * QUAD + o), a_hi, a_lo, start and c == 0, stop and c == 1,
                                  opens=n == 0)
                    if stop and c == 1:
                        ins.then_inc(dn_done[f], 1)

            def ffn_down(f):
                pe.wait_ge(prod_made[f], FT)
                by_c = [(o, c) for c in range(2) for o in range(QUAD)]
                by_o = [(o, c) for o in range(QUAD) for c in range(2)]
                for q in range(2):
                    p = DN[f] + q * DOWN
                    if f == 0 and q == 1:
                        mod_sums(10)
                        mod_sums(11)
                        pe.wait_ge(gate2_made, 1)
                    down_panel(f, q, 0, p % 2, p, by_c, start=True)
                    with pe.Fori(0, (DOWN - 3) // 2) as i:
                        for u in range(2):
                            down_panel(f, q, i * 2 + u + 1, (p + 1 + u) % 2, i * 2 + p + 1 + u, by_c)
                    down_panel(f, q, DOWN - 2, (p + DOWN - 2) % 2, p + DOWN - 2, by_c)
                    down_panel(f, q, DOWN - 1, (p + DOWN - 1) % 2, p + DOWN - 1, by_o, stop=True)

            norm(0, [tmp[:, 0, :]], [tmp[:, 2, :]], 4, [5], squares_added, KT - 1, norm_summed, norm_rstd, 1, norm_spread)
            ffn_up(0, KT)
            ffn_down(0)
            norm(1, [tmp[:, 0, :], tmp[:, 1, :]], [tmp[:, 3, :], tmp[:, 4, :]], 0, [1, 2],
                 squares_added, 2 * (KT - 1), norm_summed, norm_rstd, 2, norm_spread)

            def conv_tiles(j, u, first=False):
                if not first:
                    pe.wait_ge(mix_free, j - 1)
                for s in range(3):
                    tile(ps[:, (3 + 3 * u + s) % 8, :], j * 3 + MIX + s, (u + s) % 2, act_hi, act_lo,
                         (act_ready, 2 * KT) if first and u + s == 0 else None).then_inc(mix_done, 1)

            for j in range(2):
                conv_tiles(j, j, first=True)
            with pe.Fori(1, KT // 2) as i:
                for u in range(2):
                    conv_tiles(i * 2 + u, u)

            pe.wait_ge(mix_free, KT - 1)
            for g in range(4):
                tile(ps[:, 1 + g, :], GATE + g, g % 2, act_hi, act_lo).then_inc(gate_done, 1)
            with pe.Fori(1, 2 * KT // 4) as i:
                for u in range(4):
                    pe.wait_ge(gate_free, i * 4 + u - 3)
                    tile(ps[:, 1 + u, :], i * 4 + GATE + u, u % 2, act_hi, act_lo).then_inc(gate_done, 1)
            pe.wait_ge(mix_free, KT)
            pe.wait_ge(gate_free, 2 * KT)

            def head_projections(h, base):
                for u in range(2 * QT):
                    if u == 2 * QT - 1 and not isinstance(h, int):
                        pe.wait_ge(ret_made, h * VT)
                    tile(ps[:, u, :], base + u, u % 2, act_hi, act_lo).then_inc(qk_done, 1)
                for u in range(VT):
                    p = base + 2 * QT + u
                    pe.wait_ge(split_done, p + 1)
                    order = [(a, c) for c in range(2) for a in range(TT)] if u < VT - 1 else [(a, c) for a in range(TT) for c in range(2)]
                    for n, (a, c) in enumerate(order):
                        k = 2 * u + c
                        wh, wl = w_block(u % 2, c, V)
                        sl = slice(a * P, (a + 1) * P)
                        ins = product(ps[:, 4 + a, :], act_hi[:, k, sl], act_lo[:, k, sl], wh, wl, k == 0, k == KT - 1, opens=n == 0)
                        if u == VT - 1 and c == 1:
                            ins.then_inc(v_done, 1)

            def scores(h):
                pe.wait_ge(rot_ready, h * 2 * QT + 2 * QT)
                for a in range(TT):
                    sl = slice(a * P, (a + 1) * P)
                    for k in range(QT):
                        ins = product(ps[:, a, :], wide_hi[:, S_K + k, sl], wide_lo[:, S_K + k, sl],
                                      wide_hi[:, S_Q + k, :], wide_lo[:, S_Q + k, :], k == 0, k == QT - 1)
                    ins.then_inc(s_done, 1)

            def attend(h):
                pe.wait_ge(v_ready, h * TT + TT)
                for e in range(VT):
                    sl = slice(e * P, (e + 1) * P)
                    for k in range(TT):
                        if e == 0:
                            pe.wait_ge(s_ready, h * TT + k + 1)
                        ins = product(ps[:, 4 + e, :], wide_hi[:, S_V + k, sl], wide_lo[:, S_V + k, sl],
                                      wide_hi[:, S_S + k, :], wide_lo[:, S_S + k, :], k == 0, k == TT - 1)
                    ins.then_inc(o_done, 1)

            def head_gate(h, base):
                pe.wait_ge(mid_free, h * KT + KT)
                for e in range(VT):
                    if e >= 2:
                        pe.wait_ge(gsw_silu, h * VT + e - 1)
                    tile(ps[:, e % 2, :], base + e, e % 2, act_hi, act_lo).then_inc(gsw_done, 1)
                    if e == 0:
                        pe.wait_ge(o_added, h * (VT - 1) + VT - 1)
                        for a in range(TT):
                            ins = mm(ps[:, 2, a:a + 1], tmp[:, 5, a * P:(a + 1) * P], ones[:, 0:1], start=True, stop=True)
                        ins.then_inc(o_summed, 1)
                    if e == 1:
                        pe.wait_ge(o_rstd, h + 1)
                        for a in range(TT):
                            ins = mm(ps[:, 3, a * P:(a + 1) * P], ones[:, :], tmp[:, 6, a * P:(a + 1) * P], start=True, stop=True)
                        ins.then_inc(o_spread, 1)

            def ret_out(h, base, n):
                for m in range(KT):
                    if m < 4:
                        if n is not None:
                            pe.wait_ge(s_decayed, h * TT + TT + m + 1)
                        elif m == 0:
                            pe.wait_ge(gsw_silu, HEADS * VT)
                            pe.wait_ge(o_spread, HEADS)
                        elif m == 3:
                            pe.wait_ge(ret_made, HEADS * VT)
                    else:
                        pe.wait_ge(mid_free, (h + 1) * KT + m - 3)
                    ins = tile(ps[:, m % 4, :], base + m // 2, (m // 2) % 2, wide_hi[:, S_RET:S_RET + VT, :],
                               wide_lo[:, S_RET:S_RET + VT, :], (ret_ready, h * VT) if m == 0 else None,
                               k=VT, part=m % 2, parts=2)
                    ins.then_inc(mid_done, 1)

            head_projections(0, HEAD0)
            scores(0)
            for m in range(KT):
                if m < 4:
                    pe.wait_ge(s_decayed, m + 1)
                else:
                    pe.wait_ge(mid_free, m - 3)
                tile(ps[:, m % 4, :], HEAD0 + 2 * QT + VT + m, m % 2, wide_hi[:, S_CONV:S_CONV + KT, :],
                     wide_lo[:, S_CONV:S_CONV + KT, :], (mix_ready, 0) if m == 0 else None).then_inc(mid_done, 1)
            attend(0)
            head_gate(0, HEAD1 - VT)
            with pe.Fori(1, HEADS) as h:
                base = h * HEADP + (HEAD1 - HEADP)
                pe.wait_ge(gsw_silu, h * VT)
                head_projections(h, base)
                scores(h)
                ret_out(h - 1, base + 2 * QT + VT, 0)
                attend(h)
                head_gate(h, base + 2 * QT + 2 * VT)
            ret_out(HEADS - 1, ROUT, None)

            for m in range(KT):
                if m >= 4:
                    pe.wait_ge(wo_free, m - 3)
                tile(ps[:, 4 + m % 4, :], WO + m, m % 2, wide_hi[:, S_MERGE:S_MERGE + KT, :], wide_lo[:, S_MERGE:S_MERGE + KT, :],
                     (merge_ready, 0) if m == 0 else None).then_inc(wo_done, 1)
            norm(2, [tmp[:, 0, :]], [tmp[:, 2, :]], 4, [5], squares_added, 3 * (KT - 1), norm_summed, norm_rstd, 3, norm_spread)
            ffn_up(1, 3 * KT)
            ffn_down(1)
            norm(3, [tmp[:, 0, :]], [tmp[:, 2, :]], 0, [1], squares_added, 4 * (KT - 1), norm_summed, norm_rstd, 4, norm_spread)

        @block.scalar
        def _(act):
            do = nc.scalar.activation

            def hi_of(dst, src, made, **how):
                do(dst, src, ACT.Identity, **how).then_inc(made, 1)

            act.wait_ge(early_loaded, 16)
            do(silu_c, early_cols("c", 0, KT), ACT.Silu).then_inc(silu_c_made, 1)
            for a in range(TT):
                act.wait_ge(x_loaded[a], 16)
                if a:
                    act.wait_ge(x_squared, a)
                do(tmp[:, 0:2, :].rearrange("p s t -> p (s t)"), x_tok[:, a, :], ACT.Square,
                   accum_out=small[:, 0, a:a + 1]).then_inc(x_squared, 1)
            act.wait_ge(x_squared, TT)
            act.wait_ge(consts_set, 3)
            do(small[:, 1, :], small[:, 0, :], ACT.Sqrt, scale=1.0 / D, bias=eps[:, :]).then_inc(x_std, 1)
            act.wait_ge(x_rstd, 1)
            for a in range(TT):
                hi_of(xr_hi[:, a, :], x_tok[:, a, :], xr_hi_made, scale=small[:, 2, a:a + 1])
            act.wait_ge(dec_loaded, 16)
            do(lgt[:, 0, :], dec, ACT.Abs).then_inc(act_chain, 1)
            act.wait_ge(act_chain, 1)
            do(lgt[:, 1, :], lgt[:, 0, :], ACT.Exp, scale=-1.0).then_inc(lg_exp, 1)
            act.wait_ge(u_scale_made, 2)
            for m in range(KT):
                act.wait_ge(u_done, m + 1)
                do(wide_hi[:, S_U + m, 0:1], ps[:, m % 7, 0:1], ACT.Identity, scale=gain_mix[:, m:m + 1],
                   bias=shift_dc[:, m:m + 1])
                hi_of(wide_hi[:, S_U + m, 1:T], ps[:, m % 7, 1:T], u_hi_made, scale=gain_mix[:, m:m + 1])
            def f_hi(m):
                act.wait_ge(f_made, 3 * (m + 1))
                hi_of(act_hi[:, m, :], tmp[:, 1 + 2 * (m % 2), :], f_hi_made)

            for m in range(KT):
                act.wait_ge(f_done, m + 1)
                if m >= 2:
                    act.wait_ge(f_made, 3 * (m - 1))
                do(tmp[:, 2 * (m % 2), 0:T // 2], ps[:, 2 + 2 * (m % 3), 0:T // 2], ACT.Identity).then_inc(f_q_copied, 1)
                if m:
                    f_hi(m - 1)
            f_hi(KT - 1)

            def squares(n, free, two=False):
                for m in range(KT):
                    act.wait_ge(free, m + 1)
                    if m >= 2:
                        act.wait_ge(squares_added, n * (KT - 1) + m - 1)
                    if two:
                        do(tmp[:, 1 if m == 0 else 3, :], res[:, m, :], ACT.Square, scale=col("g_final", m))
                    do(tmp[:, 0 if m == 0 else 2, :], res[:, m, :], ACT.Square).then_inc(res_squared, 1)

            def norm_hi(n, shift=False):
                act.wait_ge(norm_summed, n + 1)
                bank = (4, 0, 4, 0)[n]
                do(small[:, 0, :], ps[:, bank, 0:TT], ACT.Sqrt, scale=1.0 / D, bias=eps[:, :]).then_inc(norm_std, 1)
                if n == 1:
                    act.wait_ge(sums_ready, 1)
                    do(small[:, 3, :], small[:, 2, :], ACT.Sqrt, scale=1.0 / D, bias=eps[:, :]).then_inc(norm_std, 1)
                if n < 3:
                    for k in range(KT):
                        act.wait_ge(normed, n * KT + k + 1)
                        hi_of(act_hi[:, k, :], tmp[:, 5 + k % 2, :], norm_hi_made,
                              **({"bias": mod[:, 3 * KT + k:3 * KT + k + 1]} if shift else {}))

            def ffn_gate(f):
                def pair(j, u):
                    if f == 0:
                        act.wait_ge(conv_step[f], j * 3 + 3)
                        do(tmp[:, 1, :], tmp[:, 0, :], ACT.Silu).then_inc(silu_made[f], 1)
                    else:
                        act.wait_ge(up_done[f], j * 2 + 1)
                        do(tmp[:, 1, :], ps[:, 2 * u, :], ACT.Silu).then_inc(silu_made[f], 1)
                    act.wait_ge(prod_made[f], j + 1)
                    do(wide_hi[:, j, :], tmp[:, 2, :], ACT.Identity
                       ).then_inc(prod_hi_made[f], 1)

                with act.Fori(0, FT // 2) as i:
                    for u in range(2):
                        pair(i * 2 + u, u)

            squares(0, fnet_free)
            norm_hi(0, shift=True)
            ffn_gate(0)
            squares(1, dn_free[0], two=True)
            norm_hi(1)

            with act.Fori(0, KT // 2) as i:
                for u in range(2):
                    j = i * 2 + u
                    act.wait_ge(mix_done, j * 3 + 1)
                    do(tmp[:, 0, :], ps[:, 3 + 3 * u, :], ACT.Identity).then_inc(xc_copied, 1)
                    act.wait_ge(mix_free, j + 1)
                    do(wide_hi[:, j + S_CONV, :], tmp[:, 3, :], ACT.Identity
                       ).then_inc(mix_hi_made, 1)
            with act.Fori(0, 2 * KT // 4) as i:
                for u in range(4):
                    act.wait_ge(gate_done, i * 4 + u + 1)
                    do(gates[:, i * 4 + u, :], ps[:, 1 + u, :], ACT.Sigmoid
                       ).then_inc(gate_free, 1)

            def head(h):
                act.wait_ge(decay_args, h + 1)
                do(decay[:, :], decay[:, :], ACT.Exp).then_inc(decay_made, 1)
                for u in range(2 * QT):
                    act.wait_ge(rot_made, h * 2 * QT + u + 1)
                    hi_of(wide_hi[:, S_Q + u, :], tmp[:, 2 + u % 2, :], rot_hi_made)
                for a in range(TT):
                    act.wait_ge(v_done, h * TT + a + 1)
                    do(ps[:, 4 + a, :], ps[:, 4 + a, :], ACT.Identity, accum_out=small[:, 6, a:a + 1]).then_inc(v_summed, 1)
                act.wait_ge(v_summed, h * TT + TT)
                do(small[:, 7, :], small[:, 6, :], ACT.Identity, scale=-1.0 / V).then_inc(v_mean, 1)
                act.wait_ge(v_mean, h + 1)
                for a in range(TT):
                    hi_of(wide_hi[:, S_V + a, :], ps[:, 4 + a, :], v_hi_made, bias=small[:, 7, a:a + 1])
                for a in range(TT):
                    act.wait_ge(s_decayed, h * TT + a + 1)
                    hi_of(wide_hi[:, S_S + a, :], tmp[:, a % 2, :], s_hi_made)
                for e in range(VT):
                    act.wait_ge(o_done, h * VT + e + 1)
                    if e >= 2:
                        act.wait_ge(o_added, h * (VT - 1) + e - 1)
                    do(tmp[:, 5 if e == 0 else 6, :], ps[:, 4 + e, :], ACT.Square).then_inc(o_squared, 1)
                def gate(e):
                    act.wait_ge(gsw_done, h * VT + e + 1)
                    do(tmp[:, e, :], ps[:, e % 2, :], ACT.Silu).then_inc(gsw_silu, 1)

                def ret_hi(e):
                    act.wait_ge(ret_made, h * VT + e + 1)
                    hi_of(wide_hi[:, S_RET + e, :], tmp[:, e, :], ret_hi_made)

                gate(0)
                act.wait_ge(o_summed, h + 1)
                do(small[:, 0, :], ps[:, 2, 0:TT], ACT.Sqrt, scale=1.0 / V, bias=eps[:, :]).then_inc(o_std, 1)
                gate(1)
                gate(2)
                ret_hi(0)
                ret_hi(1)
                gate(3)
                ret_hi(2)
                ret_hi(3)

            head(0)
            with act.Fori(1, HEADS) as h:
                head(h)
            for m in range(KT):
                act.wait_ge(mid_added, (HEADS - 1) * KT + m + 1)
                hi_of(wide_hi[:, S_MERGE + m, :], gates[:, m, :], merge_hi_made)
            squares(2, wo_free)
            norm_hi(2)
            ffn_gate(1)
            squares(3, dn_free[1])
            norm_hi(3)

        @block.vector
        def _(dve):
            tt, ts, stt = nc.vector.tensor_tensor, nc.vector.tensor_scalar, nc.vector.scalar_tensor_tensor
            links = [0]

            def link(ins):
                links[0] += 1
                ins.then_inc(chain, 1)
                dve.wait_ge(chain, links[0])

            def lo_of(dst, src, hi, made, ready, n):
                dve.wait_ge(made, n)
                tt(dst, src, f32(hi), SUB).then_inc(ready, 1)

            dve.wait_ge(x_std, 1)
            nc.vector.reciprocal(small[:, 2, :], small[:, 1, :]).then_inc(x_rstd, 1)
            dve.wait_ge(x_rstd, 1)
            for a in range(TT):
                dve.wait_ge(xr_hi_made, a + 1)
                stt(out=xr_lo[:, a, :], in0=x_tok[:, a, :], scalar=small[:, 2, a:a + 1], in1=f32(xr_hi[:, a, :]),
                    op0=MUL, op1=SUB).then_inc(xr_made, 1)

            def mod_chunk(c):
                if c >= 2:
                    dve.wait_ge(mod_summed, c - 1)
                acc = modacc[:, c % 2, :]
                for k in range(KT):
                    n = 2 * c + k // (KT // 2)
                    w = modw[:, n % 4, k % (KT // 2), :]
                    if k % (KT // 2) == 0:
                        dve.wait_ge(modw_loaded[n % 4], 16 * (n // 4 + 1))
                    if k == 0:
                        ts(acc, w, silu_c[:, 0:1], None, MUL).then_inc(mod_step, 1)
                    else:
                        dve.wait_ge(mod_step, KT * c + k)
                        stt(out=acc, in0=w, scalar=silu_c[:, k:k + 1], in1=acc, op0=MUL, op1=ADD).then_inc(mod_step, 1)

            def mod_columns(c0, c1):
                s = slice(c0 * KT, c1 * KT)
                b = early_cols("b_mod", c0 * KT, (c1 - c0) * KT)
                dve.wait_ge(mod_summed, 2 * c1)
                return tt(mod[:, s], ps[:, 7, s], b, ADD)

            dve.wait_ge(silu_c_made, 1)
            for c in range(4):
                mod_chunk(c)
            link(mod_columns(0, 2))
            stt(out=gain_mix, in0=mod[:, KT:2 * KT], scalar=1.0, in1=early_cols("g_norm_mix", 0, KT),
                op0=ADD, op1=MUL).then_inc(u_scale_made, 1)
            ts(shift_dc, mod[:, 0:KT], float(T), None, MUL).then_inc(u_scale_made, 1)
            dve.wait_ge(u_scale_made, 2)
            for m in range(KT):
                dve.wait_ge(u_hi_made, m + 1)
                link(ts(udc[:, m:m + 1], ps[:, m % 7, 0:1], gain_mix[:, m:m + 1], shift_dc[:, m:m + 1], MUL, ADD))
                tt(wide_lo[:, S_U + m, 0:1], udc[:, m:m + 1], f32(wide_hi[:, S_U + m, 0:1]), SUB)
                stt(out=wide_lo[:, S_U + m, 1:T], in0=ps[:, m % 7, 1:T], scalar=gain_mix[:, m:m + 1],
                    in1=f32(wide_hi[:, S_U + m, 1:T]), op0=MUL, op1=SUB).then_inc(u_made, 1)
            half = T // 2
            for m in range(KT + 1):
                if m < KT:
                    even, odd, f = ps[:, 1 + 2 * (m % 3), :], tmp[:, 2 * (m % 2), :], tmp[:, 1 + 2 * (m % 2), :]
                    if m >= 2:
                        dve.wait_ge(act_ready, m - 1)
                    dve.wait_ge(f_q_copied, m + 1)
                    tt(f[:, 1:half], even[:, 1:half], odd[:, 1:half], SUB).then_inc(f_made, 1)
                    tt(f[:, T - 1:half:-1], even[:, 1:half], odd[:, 1:half], ADD).then_inc(f_made, 1)
                    nc.vector.tensor_copy(f[:, 0:half + 1:half], even[:, 0:half + 1:half]).then_inc(f_made, 1)
                if m:
                    lo_of(act_lo[:, m - 1, :], tmp[:, 1 + 2 * ((m - 1) % 2), :], act_hi[:, m - 1, :], f_hi_made, act_ready, m)
            for c in range(4, 6):
                mod_chunk(c)
            link(mod_columns(2, 3))

            dve.wait_ge(lg_exp, 1)
            u, s, s2, p = (lgt[:, i, :] for i in (1, 2, 3, 4))
            link(ts(s, u, 2.0, None, ADD))
            link(nc.vector.reciprocal(s2, s))
            link(tt(s, u, s2, MUL))
            link(tt(s2, s, s, MUL))
            link(ts(p, s2, 1.0 / 17, None, MUL))
            for n in (15, 13, 11, 9, 7, 5, 3):
                link(stt(out=p, in0=p, scalar=1.0 / n, in1=s2, op0=ADD, op1=MUL))
            link(stt(out=p, in0=p, scalar=1.0, in1=s, op0=ADD, op1=MUL))
            link(ts(s, dec, 0.0, None, ALU.min))
            link(stt(out=lg[:, :], in0=p, scalar=-2.0, in1=s, op0=MUL, op1=ADD))
            link(ts(lg[:, HEADS:], lg[:, HEADS:], -1.0, None, MUL))
            dve.wait_ge(cols_loaded, 16)
            link(tt(gain_12[:, :], late_cols("g_final", KT), late_cols("g_mix_2", KT), MUL))

            def add_squares(n, m, two=False):
                if m:
                    dve.wait_ge(res_squared, n * KT + m + 1)
                    if two:
                        tt(tmp[:, 1, :], tmp[:, 1, :], tmp[:, 3, :], ADD)
                    tt(tmp[:, 0, :], tmp[:, 0, :], tmp[:, 2, :], ADD).then_inc(squares_added, 1)
                    dve.wait_ge(squares_added, n * (KT - 1) + m)

            dve.wait_ge(xt_loaded, 16)
            for m in range(KT):
                dve.wait_ge(fnet_done, m + 1)
                stt(out=res[:, m, :], in0=ps[:, m % 4, :], scalar=mod[:, 2 * KT + m:2 * KT + m + 1], in1=res[:, m, :],
                    op0=MUL, op1=ADD).then_inc(fnet_free, 1)
                if m < 4:
                    mod_chunk(6 + m)
                add_squares(0, m)
            link(mod_columns(3, 5))
            link(stt(out=gain_ffn[:, :], in0=mod[:, 4 * KT:5 * KT], scalar=1.0,
                     in1=late_cols("g_norm_ffn", KT), op0=ADD, op1=MUL))

            def diag(dst, rstd, done=None):
                for a in range(TT):
                    ins = ts(dst[:, a * P:(a + 1) * P], ident[:, :], rstd[:, a:a + 1], None, MUL)
                return ins.then_inc(done, 1) if done else ins

            dve.wait_ge(ident_loaded, 16)

            def norm(n, gain, shift=False):
                dve.wait_ge(norm_std, n + 1 + (n > 1))
                if n:
                    dve.wait_ge(norm_rstd, n)
                link(nc.vector.reciprocal(small[:, 1, :], small[:, 0, :]))
                if n == 1:
                    link(tt(small[:, 4, :], small[:, 1, :], small[:, 1, :], MUL))
                    tt(small[:, 2, :], small[:, 4, :], ps[:, 0, TT:2 * TT], MUL).then_inc(sums_ready, 1)
                    dve.wait_ge(norm_std, 3)
                    link(nc.vector.reciprocal(small[:, 5, :], small[:, 3, :]))
                    link(tt(small[:, 6, :], small[:, 5, :], small[:, 1, :], MUL))
                    diag(tmp[:, 3, :], small[:, 6, :])
                    diag(tmp[:, 4, :], small[:, 1, :], norm_rstd)
                else:
                    diag(tmp[:, 2, :], small[:, 1, :], norm_rstd)
                dve.wait_ge(norm_spread, n + 1)
                spread = ps[:, (5, 1, 5, 1)[n], :]
                for k in range(KT + 1):
                    if k < KT:
                        dst = tmp[:, 5 + k % 2, :] if n < 3 else gates[:, k, :]
                        if n < 3 and k >= 2:
                            dve.wait_ge(act_ready, (n + 1) * KT + k - 1)
                        stt(out=dst, in0=res[:, k, :], scalar=gain(k), in1=spread, op0=MUL, op1=MUL
                            ).then_inc(normed if n < 3 else out_made, 1)
                    if k == 0 or n == 3:
                        continue
                    k -= 1
                    dve.wait_ge(norm_hi_made, n * KT + k + 1)
                    hi = f32(act_hi[:, k, :])
                    if shift:
                        stt(out=act_lo[:, k, :], in0=tmp[:, 5 + k % 2, :], scalar=mod[:, 3 * KT + k:3 * KT + k + 1], in1=hi,
                            op0=ADD, op1=SUB).then_inc(act_ready, 1)
                    else:
                        tt(act_lo[:, k, :], tmp[:, 5 + k % 2, :], hi, SUB).then_inc(act_ready, 1)

            def ffn_product(f):
                def pair(j, u):
                    dve.wait_ge(up_done[f], j * 2 + 2 - (f == 0))
                    if f == 0:
                        g = ps[:, 2 * u, :]
                        w = [col("w_ffn_conv", j + FT * i) for i in range(3)]
                        c = tmp[:, 0, :]
                        ts(c, g, w[1], col("b_ffn_conv", j), MUL, ADD).then_inc(conv_step[f], 1)
                        dve.wait_ge(conv_step[f], j * 3 + 1)
                        stt(out=c[:, 1:T], in0=g[:, 0:T - 1], scalar=w[0], in1=c[:, 1:T], op0=MUL, op1=ADD).then_inc(conv_step[f], 1)
                        dve.wait_ge(conv_step[f], j * 3 + 2)
                        stt(out=c[:, 0:T - 1], in0=g[:, 1:T], scalar=w[2], in1=c[:, 0:T - 1], op0=MUL, op1=ADD).then_inc(conv_step[f], 1)
                        dve.wait_ge(up_done[f], j * 2 + 2)
                    dve.wait_ge(silu_made[f], j + 1)
                    tt(tmp[:, 2, :], ps[:, 2 * u + 1, :], tmp[:, 1, :], MUL).then_inc(prod_made[f], 1)
                    hi, lo = (w[:, j, :] for w in (wide_hi, wide_lo))
                    lo_of(lo, tmp[:, 2, :], hi, prod_hi_made[f], wide_ready[f], j + 1)
                    dve.wait_ge(wide_ready[f], j + 1)

                with dve.Fori(0, FT // 2) as i:
                    for u in range(2):
                        pair(i * 2 + u, u)

            norm(0, lambda k: gain_ffn[:, k:k + 1], shift=True)
            ffn_product(0)
            for c in range(10, MODN):
                mod_chunk(c)
            mod_columns(5, 6).then_inc(gate2_made, 1)
            dve.wait_ge(gate2_made, 1)
            for m in range(KT):
                dve.wait_ge(dn_done[0], m + 1)
                stt(out=res[:, m, :], in0=ps[:, m, :], scalar=mod[:, 5 * KT + m:5 * KT + m + 1], in1=res[:, m, :],
                    op0=MUL, op1=ADD).then_inc(dn_free[0], 1)
                add_squares(1, m, two=True)
            norm(1, lambda k: gain_12[:, k:k + 1])
            for k in range(KT):
                stt(out=res[:, k, :], in0=res[:, k, :], scalar=col("g_final", k), in1=ps[:, 2, :], op0=MUL, op1=MUL
                    ).then_inc(res_scaled, 1)

            with dve.Fori(0, KT // 2) as i:
                for u in range(2):
                    j = i * 2 + u
                    gb, gc = ps[:, (4 + 3 * u) % 8, :], ps[:, (5 + 3 * u) % 8, :]
                    w = [col("w_conv_2", j + KT * n) for n in range(3)]
                    dve.wait_ge(mix_done, j * 3 + 3)
                    dve.wait_ge(xc_copied, j + 1)
                    g, c = tmp[:, 1, :], tmp[:, 2, :]
                    tt(g, gc, tmp[:, 0, :], MUL).then_inc(mix_step, 1)
                    dve.wait_ge(mix_step, j * 4 + 1)
                    ts(c, g, w[1], None, MUL).then_inc(mix_step, 1)
                    dve.wait_ge(mix_step, j * 4 + 2)
                    stt(out=c[:, 1:T], in0=g[:, 0:T - 1], scalar=w[0], in1=c[:, 1:T], op0=MUL, op1=ADD).then_inc(mix_step, 1)
                    dve.wait_ge(mix_step, j * 4 + 3)
                    stt(out=c[:, 0:T - 1], in0=g[:, 1:T], scalar=w[2], in1=c[:, 0:T - 1], op0=MUL, op1=ADD).then_inc(mix_step, 1)
                    dve.wait_ge(mix_step, j * 4 + 4)
                    tt(tmp[:, 3, :], gb, c, MUL).then_inc(mix_free, 1)
                    hi, lo = (x[:, j + S_CONV, :] for x in (wide_hi, wide_lo))
                    lo_of(lo, tmp[:, 3, :], hi, mix_hi_made, mix_ready, j + 1)
                    dve.wait_ge(mix_ready, j + 1)

            def head(h):
                if not isinstance(h, int):
                    dve.wait_ge(ret_ready, h * VT)
                dve.wait_ge(rel_loaded, h * 16 + 16)
                ts(tmp_wide, decay[:, :], 0.0, lg[:, ds(h, 1)], ALU.max, MUL).then_inc(rot_step, 1)
                dve.wait_ge(rot_step, h * 10 + 1)
                ts(decay[:, :], decay[:, :], 0.0, lg[:, ds(h + HEADS, 1)], ALU.min, MUL).then_inc(rot_step, 1)
                dve.wait_ge(rot_step, h * 10 + 2)
                tt(decay[:, :], decay[:, :], tmp_wide, ADD).then_inc(decay_args, 1)
                for r in range(2):
                    a, b = ps[:, QT * r, :], ps[:, QT * r + 1, :]
                    n = h * 10 + 2 + 4 * r
                    dve.wait_ge(qk_done, h * 2 * QT + QT * (r + 1))
                    if r or not isinstance(h, int):
                        dve.wait_ge(rot_ready, h * 2 * QT + QT * r)
                    for i, (x0, x1, op) in enumerate(((0, 1, SUB), (1, 0, ADD))):
                        if i:
                            dve.wait_ge(rot_made, h * 2 * QT + QT * r + i)
                        tt(tmp[:, 0, :], a, rope[:, x0, :], MUL).then_inc(rot_step, 1)
                        tt(tmp[:, 1, :], b, rope[:, x1, :], MUL).then_inc(rot_step, 1)
                        dve.wait_ge(rot_step, n + 2 * i + 2)
                        tt(tmp[:, 2 + i, :], tmp[:, 0, :], tmp[:, 1, :], op).then_inc(rot_made, 1)
                    for i in range(QT):
                        lo_of(wide_lo[:, S_Q + QT * r + i, :], tmp[:, 2 + i, :], wide_hi[:, S_Q + QT * r + i, :],
                              rot_hi_made, rot_ready, h * 2 * QT + QT * r + i + 1)
                for a in range(TT):
                    dve.wait_ge(v_hi_made, h * TT + a + 1)
                    stt(out=wide_lo[:, S_V + a, :], in0=ps[:, 4 + a, :], scalar=small[:, 7, a:a + 1],
                        in1=f32(wide_hi[:, S_V + a, :]), op0=ADD, op1=SUB).then_inc(v_ready, 1)
                dve.wait_ge(decay_made, h + 1)
                for a in range(TT + 1):
                    if a < TT:
                        dve.wait_ge(s_done, h * TT + a + 1)
                        if a >= 2:
                            dve.wait_ge(s_ready, h * TT + a - 1)
                        c0 = (TT - 1 - a) * P
                        stt(out=tmp[:, a % 2, :], in0=ps[:, a, :], scalar=QK ** -0.5, in1=decay[:, c0:c0 + T],
                            op0=MUL, op1=MUL).then_inc(s_decayed, 1)
                    if a:
                        lo_of(wide_lo[:, S_S + a - 1, :], tmp[:, (a - 1) % 2, :], wide_hi[:, S_S + a - 1, :],
                              s_hi_made, s_ready, h * TT + a)
                if isinstance(h, int):
                    for m in range(KT):
                        dve.wait_ge(mid_done, m + 1)
                        tt(gates[:, m, :], ps[:, m % 4, :], gates[:, m, :], MUL).then_inc(mid_free, 1)
                else:
                    merge(h - 1)
                for e in range(1, VT):
                    dve.wait_ge(o_squared, h * VT + e + 1)
                    tt(tmp[:, 5, :], tmp[:, 5, :], tmp[:, 6, :], ADD).then_inc(o_added, 1)
                    dve.wait_ge(o_added, h * (VT - 1) + e)
                dve.wait_ge(o_std, h + 1)
                if not isinstance(h, int):
                    dve.wait_ge(o_rstd, h)
                nc.vector.reciprocal(small[:, 1, :], small[:, 0, :]).then_inc(o_recip, 1)
                dve.wait_ge(o_recip, h + 1)
                diag(tmp[:, 6, :], small[:, 1, :], o_rstd)

                def gated(e):
                    dve.wait_ge(gsw_silu, h * VT + e + 1)
                    stt(out=tmp[:, e, :], in0=ps[:, 4 + e, :], scalar=col("g_ret_2", h * VT + e), in1=tmp[:, e, :],
                        op0=MUL, op1=MUL).then_inc(o_gated, 1)

                def scaled(e):
                    dve.wait_ge(o_spread, h + 1)
                    dve.wait_ge(o_gated, h * VT + e + 1)
                    tt(tmp[:, e, :], tmp[:, e, :], ps[:, 3, :], MUL).then_inc(ret_made, 1)

                def ret_lo(e):
                    lo_of(wide_lo[:, S_RET + e, :], tmp[:, e, :], wide_hi[:, S_RET + e, :], ret_hi_made, ret_ready, h * VT + e + 1)

                gated(0)
                gated(1)
                scaled(0)
                scaled(1)
                gated(2)
                scaled(2)
                ret_lo(0)
                ret_lo(1)
                gated(3)
                scaled(3)
                ret_lo(2)
                ret_lo(3)

            def merge(h, last=False):
                dve.wait_ge(ret_ready, h * VT + VT)
                dve.wait_ge(s_ready, h * TT + (TT if last else 2 * TT))
                for m in range(KT):
                    if m >= 2:
                        dve.wait_ge(mid_added, h * KT + m - 1)
                    dve.wait_ge(mid_done, (h + 1) * KT + m + 1)
                    tt(tmp[:, m % 2, :], ps[:, m % 4, :], gates[:, KT + m, :], MUL).then_inc(mid_free, 1)
                    dve.wait_ge(mid_free, (h + 1) * KT + m + 1)
                    tt(gates[:, m, :], gates[:, m, :], tmp[:, m % 2, :], ADD).then_inc(mid_added, 1)
                    if last:
                        lo_of(wide_lo[:, S_MERGE + m, :], gates[:, m, :], wide_hi[:, S_MERGE + m, :], merge_hi_made, merge_ready, m + 1)

            dve.wait_ge(rope_loaded, 16)
            dve.wait_ge(mix_ready, KT)
            dve.wait_ge(gate_free, 2 * KT)
            head(0)
            with dve.Fori(1, HEADS) as h:
                head(h)
            merge(HEADS - 1, last=True)

            dve.wait_ge(res_scaled, KT)
            for m in range(KT):
                dve.wait_ge(wo_done, m + 1)
                tt(res[:, m, :], ps[:, 4 + m % 4, :], res[:, m, :], ADD).then_inc(wo_free, 1)
                add_squares(2, m)
            norm(2, lambda k: col("g_ffn_2", k))
            ffn_product(1)
            for m in range(KT):
                dve.wait_ge(dn_done[1], m + 1)
                tt(res[:, m, :], ps[:, m, :], res[:, m, :], ADD).then_inc(dn_free[1], 1)
                add_squares(3, m)
            norm(3, lambda k: col("g_final_2", k))


def kernel(**inputs):
    from concourse import bacc
    from concourse.bass_utils import run_bass_kernel_spmd

    F32 = mybir.dt.float32
    nc = bacc.Bacc("TRN2", target_bir_lowering=False, num_devices=1, dynamic_dma_scratch_size=64)
    a = {n: np.asarray(v) for n, v in inputs.items()}
    arrays = {n: np.ascontiguousarray(a[n][0]) for n in (
        "w_mod", "w_ffn_up", "w_ffn_down", "w_fnet_out", "w_in_2", "w_a_out_2", "w_r_out_2", "w_o_2",
        "w_ff_gate_2", "w_ff_up_2", "w_ff_down_2")}
    arrays["x"] = np.ascontiguousarray(a["x"][0])
    arrays["x_t"] = np.ascontiguousarray(a["x"][0].T)
    arrays["columns"] = np.ascontiguousarray(np.concatenate([a[n].reshape(-1) for n, _ in VECTORS]).reshape(COLS, P).T)
    arrays["decays"] = np.ascontiguousarray(np.broadcast_to(
        np.concatenate([a["dec_f_2"].reshape(-1), a["dec_b_2"].reshape(-1)]), (P, 2 * HEADS)))
    arrays.update(tables())
    t = {n: nc.dram_tensor(f"in_{n}", v.shape, F32, kind="ExternalInput").ap() for n, v in arrays.items()}
    out = nc.dram_tensor("out", (D, T), F32, kind="ExternalOutput").ap()
    build(nc, t, out)
    r = run_bass_kernel_spmd(nc, [{f"in_{n}": v for n, v in arrays.items()}], core_ids=[0])
    return np.ascontiguousarray(r.results[0]["out"].T)[None]
```

```python
from contextlib import ExitStack

import numpy as np
import concourse.bass as bass
from concourse import mybir

P = 128
D = 1024
T = 512
KT = D // P
TT = T // P
FF = 2816
FT = FF // P
GROUP = 256
HEADS, QK, V = 4, 256, 512
QT, VT = QK // P, V // P
EPS = 1e-6
PANEL = 8 * P
RAW, SPLIT = 4, 2
MOD_STEPS = 2
MOD_LOADS = KT // MOD_STEPS
MOD_AFTER = {2: 2, 4: 3, 7: 4}
PAIR = 2
QUAD = 4
DOWN = FT // 2
REL = T + (TT - 1) * P

FNET = 0
UP = [FNET + KT, 0]
DN = [UP[0] + PAIR * FT, 0]
MIX = DN[0] + 2 * DOWN
GATE = MIX + 3 * KT
HEAD0 = GATE + 2 * KT
HEAD1 = HEAD0 + 2 * QT + VT + KT + VT
HEADP = 2 * QT + VT + VT + VT
ROUT = HEAD1 + (HEADS - 1) * HEADP
WO = ROUT + VT
UP[1] = WO + KT
DN[1] = UP[1] + PAIR * FT
PANELS = DN[1] + 2 * DOWN

XC, GB, GC, WQ, WK, WV, GSW, GA, GR = np.cumsum([0, D, D, D, D, D, 2 * D, 2 * D, D]).tolist()

VECTORS = [("c", KT), ("b_mod", 6 * KT), ("g_norm_mix", KT),
           ("g_norm_ffn", KT), ("g_final", KT),
           ("w_ffn_conv", 3 * FT), ("b_ffn_conv", FT), ("g_mix_2", KT), ("w_conv_2", 3 * KT),
           ("g_ret_2", HEADS * VT), ("g_ffn_2", KT), ("g_final_2", KT)]
AT, _n = {}, 0
for _name, _count in VECTORS:
    AT[_name] = _n
    _n += _count
COLS = _n
EARLY = AT["g_norm_ffn"]

S_XR, S_DFT, S_DFTD, S_U = 0, 8, 12, 14
S_CONV, S_RET, S_MERGE, S_Q, S_K, S_V, S_S = 0, 0, 4, 8, 10, 12, 16


def tables():
    l, k = np.arange(T)[:, None], np.arange(T // 2 + 1)[None]
    ang = 2 * np.pi * ((l * k) % T) / T
    dft_tokens = np.concatenate([np.cos(ang), np.sin(ang[:, 1:T // 2])], axis=1)
    d = np.arange(GROUP)
    ang = 2 * np.pi * ((d[:, None] * d[None]) % GROUP) / GROUP
    dft_features = np.concatenate([np.cos(ang), np.sin(ang)], axis=1) / np.sqrt(T * GROUP)
    freqs = np.float32(10000.0) ** (-np.arange(0, QK, 2, dtype=np.float32) / np.float32(QK))
    ang = (freqs[:, None] * np.arange(T, dtype=np.float32)[None]).astype(np.float32).astype(np.float64)
    rope = np.stack([np.cos(ang), np.sin(ang)])
    relative = np.arange(REL)[None] - (TT - 1) * P - np.arange(P)[:, None]
    made = {"dft_tokens": dft_tokens, "dft_features": dft_features, "rope": rope, "relative": relative}
    return {n: np.ascontiguousarray(v.astype(np.float32)) for n, v in made.items()}


def build(nc, t, out):
    F32, F32R = mybir.dt.float32, mybir.dt.float32r
    ALU, ACT = mybir.AluOpType, mybir.ActivationFunctionType
    MUL, ADD, SUB = ALU.mult, ALU.add, ALU.subtract
    ds = bass.ds
    ctx = ExitStack()
    with ctx:
        def sb(name, shape, dt=F32):
            return ctx.enter_context(nc.sbuf_tensor(name, shape, dt))

        def sem(name):
            return ctx.enter_context(nc.semaphore(name))

        res = sb("res", [P, KT, T])
        act_hi, act_lo = sb("act_hi", [P, KT, T], F32R), sb("act_lo", [P, KT, T], F32R)
        wide_hi, wide_lo = sb("wide_hi", [P, FT, T], F32R), sb("wide_lo", [P, FT, T], F32R)
        gates = sb("gates", [P, 2 * KT, T])
        raw = sb("raw", [P, RAW, PANEL])
        w_hi, w_lo = sb("w_hi", [P, SPLIT, PANEL], F32R), sb("w_lo", [P, SPLIT, PANEL], F32R)
        tmp = sb("tmp", [P, 7, T])
        rope = sb("rope", [P, 2, T])
        decay = sb("decay", [P, REL])
        cols = sb("cols", [P, COLS - EARLY])
        lg = sb("lg", [P, 2 * HEADS])
        mod = sb("mod", [P, 6 * KT])
        gain_ffn, gain_12 = sb("gain_ffn", [P, KT]), sb("gain_12", [P, KT])
        small = sb("small", [P, 8, TT])
        eps, eps_squared, zero = sb("eps", [P, 1]), sb("eps_squared", [P, 1]), sb("zero", [P, 1])
        ones = sb("ones", [P, P])
        eps_ones = sb("eps_ones", [P, P])
        ps = ctx.enter_context(nc.psum_tensor("ps", [P, 8, T], F32))

        early = tmp[:, 4, :]
        dec, silu_c, gain_mix, shift_dc, udc = (early[:, EARLY + 8 * i:EARLY + 8 * (i + 1)] for i in range(5))
        lgt = early[:, EARLY + 40:EARLY + 80].rearrange("p (i n) -> p i n", i=5)

        x_tok = res[:, :, :].rearrange("p k t -> p (k t)").rearrange("p (a d) -> p a d", a=TT)
        xr_hi, xr_lo = (w[:, S_XR:S_XR + 2 * TT, :].rearrange("p s t -> p (s t)").rearrange("p (a d) -> p a d", a=TT)
                        for w in (wide_hi, wide_lo))
        modw = gates[:, :, :].rearrange("p s t -> p (s t)").rearrange("p (k n) -> p k n", k=KT)
        modw_res = res[:, :, :].rearrange("p s t -> p (s t)").rearrange("p (k n) -> p k n", k=KT // 2)
        tmp_flat = tmp[:, :, :].rearrange("p s t -> p (s t)")
        tmp_wide = tmp[:, 5:7, :].rearrange("p s t -> p (s t)")[:, 0:REL]

        def col(name, i=0):
            return cols[:, ds(i + AT[name] - EARLY, 1)]

        def early_cols(name, i, n):
            return early[:, AT[name] + i:AT[name] + i + n]

        def late_cols(name, n):
            return cols[:, AT[name] - EARLY:AT[name] - EARLY + n]

        def u_tile(m):
            return tmp[:, 0, :] if m == 0 else ps[:, m % 7, :]

        def f32(ap):
            return ap.bitcast(F32)

        def mod_place(c, k):
            if c == 1:
                return k - KT // 2 if k >= KT // 2 else None
            return k if c == 0 else (k + KT // 2) % KT

        def mod_weights(c, k, n=1):
            at = mod_place(c, k)
            return modw_res[:, k:k + n, :] if at is None else modw[:, at:at + n, :]

        def mod_loaded(c, k):
            at = mod_place(c, k)
            if at is None:
                return modw_res_loaded[k // MOD_STEPS], 16
            before = [b for b in range(c) if any(mod_place(b, j) == at for j in range(KT))]
            return modw_loaded[at // MOD_STEPS], 16 * (len(before) + 1)

        def mod_acc(c):
            first = 2 if c in (1, 3) else 5
            return tmp_flat[:, first * T:first * T + D]

        x_loaded = [sem(f"x_loaded{i}") for i in range(TT)]
        early_loaded, dft_loaded, dftd_loaded, cols_loaded, dec_loaded = sem("early_loaded"), sem("dft_loaded"), sem("dftd_loaded"), sem("cols_loaded"), sem("dec_loaded")
        rope_loaded, xt_loaded, rel_loaded = sem("rope_loaded"), sem("xt_loaded"), sem("rel_loaded")
        modw_loaded = [sem(f"modw_loaded{i}") for i in range(MOD_LOADS)]
        modw_res_loaded = [sem(f"modw_res_loaded{i}") for i in range(MOD_LOADS // 2)]
        raw_loaded = [sem(f"raw_loaded{i}") for i in range(RAW)]
        dft_hi_made, dft_split = sem("dft_hi_made"), sem("dft_split")
        hi_made, split_done, panel_used = sem("hi_made"), sem("split_done"), sem("panel_used")
        consts_set = sem("consts_set")
        chain, act_chain = sem("chain"), sem("act_chain")
        silu_c_made, x_squared, x_std, x_rstd = sem("silu_c_made"), sem("x_squared"), sem("x_std"), sem("x_rstd")
        xr_hi_made, xr_made = sem("xr_hi_made"), sem("xr_made")
        lg_exp, lg_made = sem("lg_exp"), sem("lg_made")
        mod_step, mod_summed, mod_read, u_scale_made = (
            sem(n) for n in ("mod_step", "mod_summed", "mod_read", "u_scale_made"))
        res_scaled = sem("res_scaled")
        u_done, u0_copied, u_hi_made, u_made = sem("u_done"), sem("u0_copied"), sem("u_hi_made"), sem("u_made")
        f_ready, f_done, f_q_copied, f_made, f_hi_made = sem("f_ready"), sem("f_done"), sem("f_q_copied"), sem("f_made"), sem("f_hi_made")
        act_ready = sem("act_ready")
        fnet_done, fnet_free = sem("fnet_done"), sem("fnet_free")
        res_squared, squares_added = sem("res_squared"), sem("squares_added")
        norm_summed, norm_std, norm_rstd = sem("norm_summed"), sem("norm_std"), sem("norm_rstd")
        normed, norm_hi_made = sem("normed"), sem("norm_hi_made")
        up_done, conv_step, silu_made, prod_made, prod_hi_made, wide_ready = (
            [sem(f"{n}{f}") for f in range(2)]
            for n in ("up_done", "conv_step", "silu_made", "prod_made", "prod_hi_made", "wide_ready"))
        dn_done, dn_free = [sem("dn_done0"), sem("dn_done1")], [sem("dn_free0"), sem("dn_free1")]
        mix_done, xc_copied, mix_step, mix_free, mix_hi_made, mix_ready = (
            sem(n) for n in ("mix_done", "xc_copied", "mix_step", "mix_free", "mix_hi_made", "mix_ready"))
        gate_done, gate_free = sem("gate_done"), sem("gate_free")
        decay_args, decay_made = sem("decay_args"), sem("decay_made")
        qk_done, rot_step, rot_made, rot_hi_made, rot_ready = (
            sem(n) for n in ("qk_done", "rot_step", "rot_made", "rot_hi_made", "rot_ready"))
        v_done, v_summed, v_mean, v_hi_made, v_ready = (sem(n) for n in ("v_done", "v_summed", "v_mean", "v_hi_made", "v_ready"))
        s_done, s_decayed, s_hi_made, s_ready = (sem(n) for n in ("s_done", "s_decayed", "s_hi_made", "s_ready"))
        mid_done, mid_free, mid_added = sem("mid_done"), sem("mid_free"), sem("mid_added")
        o_done, o_squared, o_added, o_summed, o_std, o_rstd = (
            sem(n) for n in ("o_done", "o_squared", "o_added", "o_summed", "o_std", "o_rstd"))
        gsw_done, gsw_silu, o_gated, ret_made, ret_hi_made, ret_ready = (
            sem(n) for n in ("gsw_done", "gsw_silu", "o_gated", "ret_made", "ret_hi_made", "ret_ready"))
        merge_hi_made, merge_ready = sem("merge_hi_made"), sem("merge_ready")
        wo_done, wo_free = sem("wo_done"), sem("wo_free")
        out_made, out_stored = sem("out_made"), sem("out_stored")

        block = ctx.enter_context(nc.Block())

        @block.sync
        def _(sp):
            def view(w, k):
                return w.rearrange("(k p) n -> p k n", k=k)

            w_up = view(t["w_ffn_up"], KT)
            w_in = view(t["w_in_2"], KT)
            w_out_r = t["w_r_out_2"].rearrange("(h k p) n -> p h k n", h=HEADS, k=VT)

            def panel(p, slot, src, blocks, first=False):
                if not first:
                    sp.wait_ge(split_done, p - RAW + 1)
                dst = raw[:, slot, :].rearrange("p (k n) -> p k n", k=blocks)
                sp.dma_start(dst, src).then_inc(raw_loaded[slot], 16)

            def mod_chunk(c):
                for k in range(0, KT, MOD_STEPS):
                    at = mod_place(c, k)
                    if at is None:
                        sp.wait_ge(xr_made, TT)
                        sp.wait_ge(xr_hi_made, TT)
                    before = [(b, j) for b in range(c) for j in range(KT) if at is not None and mod_place(b, j) == at]
                    if before:
                        b, j = before[-1]
                        sp.wait_ge(mod_step, b * KT + j + MOD_STEPS)
                    sp.dma_start(mod_weights(c, k, MOD_STEPS), view(t["w_mod"], KT)[:, k:k + MOD_STEPS, c * D:(c + 1) * D]
                                 ).then_inc(mod_loaded(c, k)[0], 16)

            w_fnet = view(t["w_fnet_out"], KT)

            def fnet_panel(m):
                panel(FNET + m, m % RAW, w_fnet[:, :, m * P:(m + 1) * P], KT, first=m < RAW)

            sp.dma_start(early[:, 0:EARLY], t["columns"][:, 0:EARLY]).then_inc(early_loaded, 16)
            sp.dma_start(raw[:, 0:2, :].rearrange("p s n -> p (s n)").rearrange("p (k n) -> p k n", k=TT),
                         view(t["dft_tokens"], TT)).then_inc(dft_loaded, 16)
            for a in range(TT):
                sp.dma_start(x_tok[:, a, :], t["x"][a * P:(a + 1) * P, :]).then_inc(x_loaded[a], 16)
            mod_chunk(0)
            mod_chunk(1)
            sp.dma_start(raw[:, 2, :].rearrange("p (k n) -> p k n", k=2), view(t["dft_features"], 2)).then_inc(dftd_loaded, 16)
            sp.wait_ge(dft_split, 2)
            fnet_panel(0)
            fnet_panel(1)
            mod_chunk(2)
            sp.dma_start(cols[:, :], t["columns"][:, EARLY:]).then_inc(cols_loaded, 16)
            sp.dma_start(dec, t["decays"]).then_inc(dec_loaded, 16)
            sp.wait_ge(mod_step, KT + KT // 2)
            sp.dma_start(res[:, :, :], view(t["x_t"], KT)).then_inc(xt_loaded, 16)
            sp.wait_ge(dft_split, 3)
            fnet_panel(2)
            fnet_panel(3)
            mod_chunk(3)
            fnet_panel(4)
            fnet_panel(5)
            mod_chunk(4)
            fnet_panel(6)
            fnet_panel(7)
            sp.dma_start(rope[:, :, :], t["rope"].rearrange("s p n -> p s n")).then_inc(rope_loaded, 16)

            def up_panels(f, j, u):
                base = UP[f] + PAIR * j
                slot = (UP[f] + PAIR * u) % RAW
                if f == 0:
                    g, v = w_up[:, :, ds(j * P, P)], w_up[:, :, ds(j * P + FF, P)]
                else:
                    g, v = (view(t[n], KT)[:, :, ds(j * P, P)] for n in ("w_ff_gate_2", "w_ff_up_2"))
                panel(base, slot, g, KT)
                panel(base + 1, (slot + 1) % RAW, v, KT)

            def ffn_panels(f, w_down, peel=0):
                for j in range(peel):
                    up_panels(f, j, j % 2)
                if peel:
                    mod_chunk(5)
                with sp.Fori(peel // 2, FT // 2) as i:
                    for u in range(2):
                        up_panels(f, i * 2 + u, u)
                w_dn = view(w_down, FT)
                for q in range(2):
                    for k in range(DOWN):
                        p = DN[f] + q * DOWN + k
                        panel(p, p % RAW, w_dn[:, 2 * k:2 * k + 2, q * QUAD * P:(q + 1) * QUAD * P], 2)

            ffn_panels(0, t["w_ffn_down"], peel=2)

            with sp.Fori(0, KT // 4) as i:
                for u in range(12):
                    j = i * 4 + u // 3
                    panel(i * 12 + MIX + u, (MIX + u) % RAW, w_in[:, :, ds(j * P + (XC, GB, GC)[u % 3], P)], KT)
            with sp.Fori(0, 2 * KT // 4) as i:
                for u in range(4):
                    panel(i * 4 + GATE + u, (GATE + u) % RAW, w_in[:, :, ds(i * 4 * P + GA + u * P, P)], KT)

            def rel_table(h):
                if isinstance(h, int):
                    assert h == 0
                else:
                    sp.wait_ge(s_decayed, h * TT)
                sp.dma_start(decay[:, :], t["relative"]).then_inc(rel_loaded, 16)

            def head_projections(h, base, b0):
                for u in range(2 * QT):
                    src = w_in[:, :, ds(h * QK + (WQ, WK)[u // QT] + (u % QT) * P, P)]
                    panel(base + u, (b0 + u) % RAW, src, KT)
                for u in range(VT):
                    src = w_in[:, 2 * u:2 * u + 2, ds(h * V + WV, V)]
                    panel(base + 2 * QT + u, (b0 + u) % RAW, src, 2)

            def head_gate(h, base, b0):
                for u in range(VT):
                    panel(base + u, (b0 + u) % RAW, w_in[:, :, ds(h * V + GSW + u * P, P)], KT)

            def ret_out(h, base, b0):
                for u in range(VT):
                    if isinstance(h, int):
                        src = w_out_r[:, h, :, 2 * u * P:2 * (u + 1) * P]
                    else:
                        src = w_out_r[:, ds(h, 1), :, 2 * u * P:2 * (u + 1) * P].rearrange("p h k n -> p (h k) n")
                    panel(base + u, (b0 + u) % RAW, src, VT)

            rel_table(0)
            head_projections(0, HEAD0, HEAD0)
            w_a = view(t["w_a_out_2"], KT)
            for m in range(KT):
                p = HEAD0 + 2 * QT + VT + m
                panel(p, p % RAW, w_a[:, :, m * P:(m + 1) * P], KT)
            head_gate(0, HEAD1 - VT, HEAD1)
            with sp.Fori(1, HEADS) as h:
                base = h * HEADP + (HEAD1 - HEADP)
                rel_table(h)
                head_projections(h, base, HEAD1)
                ret_out(h - 1, base + 2 * QT + VT, HEAD1)
                head_gate(h, base + 2 * QT + 2 * VT, HEAD1)
            ret_out(HEADS - 1, ROUT, ROUT)
            w_o = view(t["w_o_2"], KT)
            for m in range(KT):
                panel(WO + m, (WO + m) % RAW, w_o[:, :, m * P:(m + 1) * P], KT)
            ffn_panels(1, t["w_ff_down_2"])
            for m in range(KT):
                sp.wait_ge(out_made, m + 1)
                sp.dma_start(out[m * P:(m + 1) * P, :], gates[:, m, :]).then_inc(out_stored, 16)
            sp.wait_ge(out_stored, 16 * KT)

        @block.gpsimd
        def _(pool):
            nc.gpsimd.memset(ones[:, :], 1.0).then_inc(consts_set, 1)
            nc.gpsimd.memset(zero[:, :], 0.0).then_inc(consts_set, 1)
            nc.gpsimd.memset(eps[:, :], EPS).then_inc(consts_set, 1)
            nc.gpsimd.memset(eps_squared[:, :], EPS * EPS).then_inc(consts_set, 1)
            nc.gpsimd.memset(eps_ones[:, :], EPS).then_inc(consts_set, 1)
            pool.wait_ge(consts_set, 5)
            for n, (slots, s0) in enumerate((((0, 1), S_DFT), ((1, 2), S_DFT + 2), ((2, 3), S_DFTD))):
                src = raw[:, slots[0], :]
                dst_hi, dst_lo = (w[:, s0:s0 + 2, :].rearrange("p s t -> p (s t)") for w in (wide_hi, wide_lo))
                if n != 1:
                    pool.wait_ge(dft_loaded if n == 0 else dftd_loaded, 16)
                nc.gpsimd.tensor_scalar(dst_hi, src, 1.0, 0.0, MUL, ADD).then_inc(dft_hi_made, 1)
                pool.wait_ge(dft_hi_made, n + 1)
                nc.gpsimd.tensor_tensor(dst_lo, src, f32(dst_hi), SUB).then_inc(dft_split, 1)

            def split(p, slot, two, loads, first=False):
                pool.wait_ge(raw_loaded[slot], loads)
                if not first:
                    pool.wait_ge(panel_used, p - SPLIT + 1)
                nc.gpsimd.tensor_tensor(w_hi[:, two, 0:1], raw[:, slot, 0:1], zero[:, :], ADD)
                nc.gpsimd.tensor_scalar(w_hi[:, two, 1:], raw[:, slot, 1:], 1.0, 0.0, MUL, ADD).then_inc(hi_made, 1)
                pool.wait_ge(hi_made, p + 1)
                nc.gpsimd.tensor_tensor(w_lo[:, two, :], raw[:, slot, :], f32(w_hi[:, two, :]), SUB).then_inc(split_done, 1)

            for p in range(RAW):
                split(p, p, p % SPLIT, 16, first=p < SPLIT)
                if p == SPLIT - 1:
                    for m in range(KT):
                        pool.wait_ge(f_hi_made, m + 1)
                        nc.gpsimd.tensor_tensor(act_lo[:, m, :], tmp[:, 1 + 2 * (m % 2), :], f32(act_hi[:, m, :]), SUB
                                                ).then_inc(f_ready, 1)
            with pool.Fori(1, PANELS // RAW) as i:
                for u in range(RAW):
                    split(i * RAW + u, u, u % SPLIT, i * 16 + 16)

        @block.tensor
        def _(pe):
            mm = nc.tensor.matmul

            def product(o, w, wl, a, al, start, stop, opens=False):
                ins = mm(o, w, a, start=start, stop=False)
                if opens:
                    ins.then_inc(panel_used, 1)
                mm(o, wl, a, start=False, stop=False)
                return mm(o, w, al, start=False, stop=stop)

            def w_block(two, b, n=P):
                return w_hi[:, two, b * n:(b + 1) * n], w_lo[:, two, b * n:(b + 1) * n]

            def tile(o, p, two, a_hi, a_lo, ready=None, k=KT, part=0, parts=1):
                if part == 0:
                    pe.wait_ge(split_done, p + 1)
                for b in range(k):
                    if ready:
                        pe.wait_ge(ready[0], ready[1] + b + 1)
                    ins = product(o, *w_block(two, parts * b + part), a_hi[:, b, :], a_lo[:, b, :], b == 0, b == k - 1,
                                  opens=not (isinstance(p, int) and p == 0) and part == 0 and b == 0)
                return ins

            def dft_tokens(tiles):
                for k in range(TT):
                    if tiles[0] == 0:
                        pe.wait_ge(xr_made, k + 1)
                    for m in tiles:
                        ins = product(ps[:, m % 7, :], xr_hi[:, k, m * P:(m + 1) * P], xr_lo[:, k, m * P:(m + 1) * P],
                                      wide_hi[:, S_DFT + k, :], wide_lo[:, S_DFT + k, :], k == 0, k == TT - 1)
                        if k == TT - 1:
                            ins.then_inc(u_done, 1)

            def mod_sums(c):
                pe.wait_ge(mod_step, KT * (c + 1))
                if c in (2, 3, 5):
                    pe.wait_ge(mod_read, {2: 1, 3: 2, 5: 3}[c])
                for u in range(KT):
                    ins = mm(ps[:, 7, c * KT + u:c * KT + u + 1], mod_acc(c)[:, u * P:(u + 1) * P], ones[:, 0:1],
                             start=True, stop=True)
                ins.then_inc(mod_summed, 1)

            pe.wait_ge(dft_split, 2)
            pe.wait_ge(consts_set, 5)
            dft_tokens(range(4))
            dft_tokens([4])
            dft_tokens([5])
            dft_tokens([6])
            mod_sums(0)
            pe.wait_ge(u0_copied, 1)
            dft_tokens([7])
            mod_sums(1)

            pe.wait_ge(dft_split, 3)
            half = T // 2
            for m in range(KT):
                if m < 3:
                    pe.wait_ge(u_made, 2 * m + 3)
                else:
                    pe.wait_ge(f_made, 3 * (m - 2))
                pe.wait_ge(u_made, m // 2 * 2 + 2)
                g, e = m // 2, m % 2
                for part, (c0, n) in enumerate(((0, half + 2), (half, half))):
                    for k in range(2):
                        sl = slice(part * GROUP + e * P, part * GROUP + (e + 1) * P)
                        ins = product(ps[:, 1 + 2 * (m % 3) + part, 0:n], wide_hi[:, S_DFTD + k, sl], wide_lo[:, S_DFTD + k, sl],
                                      wide_hi[:, S_U + 2 * g + k, c0:c0 + n], wide_lo[:, S_U + 2 * g + k, c0:c0 + n],
                                      k == 0, k == 1)
                ins.then_inc(f_done, 1)

            pe.wait_ge(f_made, 3 * KT)
            for m in range(KT):
                if m == 7:
                    pe.wait_ge(fnet_free, 1)
                tile(ps[:, m % 7, :], FNET + m, m % 2, act_hi, act_lo, (f_ready, 0) if m == 0 else None
                     ).then_inc(fnet_done, 1)
                if m in MOD_AFTER:
                    mod_sums(MOD_AFTER[m])

            def norm(n, banks):
                pe.wait_ge(squares_added, (n + 1) * (KT - 2))
                if len(banks) == 1:
                    mm(ps[:, banks[0], :], ones[:, :], tmp[:, 0, :], start=True, stop=False)
                    pe.wait_ge(res_squared, (n + 1) * KT)
                    mm(ps[:, banks[0], :], ones[:, :], tmp[:, 1, :], start=False, stop=True).then_inc(norm_summed, 1)
                else:
                    mm(ps[:, banks[1], :], ones[:, :], tmp[:, 1, :], start=True, stop=False)
                    mm(ps[:, banks[1], :], eps_ones[:, :], tmp[:, 0, :], start=False, stop=False)
                    mm(ps[:, banks[0], :], ones[:, :], tmp[:, 0, :], start=True, stop=False)
                    pe.wait_ge(res_squared, (n + 1) * KT)
                    mm(ps[:, banks[1], :], ones[:, :], tmp[:, 3, :], start=False, stop=False)
                    mm(ps[:, banks[1], :], eps_ones[:, :], tmp[:, 2, :], start=False, stop=True)
                    mm(ps[:, banks[0], :], ones[:, :], tmp[:, 2, :], start=False, stop=True).then_inc(norm_summed, 1)

            def ffn_up(f, act_base):
                def pair(j, u, first=False):
                    if not first:
                        pe.wait_ge(prod_made[f], j - 1)
                    for s in range(PAIR):
                        tile(ps[:, 2 * u + s, :], j * PAIR + UP[f] + s, s, act_hi, act_lo,
                             (act_ready, act_base) if first and u + s == 0 else None).then_inc(up_done[f], 1)

                for j in range(2):
                    pair(j, j, first=True)
                with pe.Fori(1, FT // 2) as i:
                    for u in range(2):
                        pair(i * 2 + u, u)

            def down_panel(f, q, k, two, p, order, start=False, stop=False, a0=None):
                pe.wait_ge(split_done, p + 1)
                if q == 0:
                    pe.wait_ge(wide_ready[f], k * 2 + 2)
                for n, (o, c) in enumerate(order):
                    a_hi, a_lo = (w[:, k * 2 + c, :] for w in (wide_hi, wide_lo))
                    ins = product(ps[:, 4 * q + o, :], *w_block(two, c * QUAD + o), a_hi, a_lo, start and c == 0, stop and c == 1,
                                  opens=n == 0)
                    if stop and c == 1:
                        ins.then_inc(dn_done[f], 1)

            def ffn_down(f):
                pe.wait_ge(prod_made[f], FT)
                by_c = [(o, c) for c in range(2) for o in range(QUAD)]
                by_o = [(o, c) for o in range(QUAD) for c in range(2)]
                for q in range(2):
                    p = DN[f] + q * DOWN
                    if f == 0 and q == 1:
                        mod_sums(5)
                        pe.wait_ge(mod_read, 4)
                    down_panel(f, q, 0, p % 2, p, by_c, start=True)
                    with pe.Fori(0, (DOWN - 3) // 2) as i:
                        for u in range(2):
                            down_panel(f, q, i * 2 + u + 1, (p + 1 + u) % 2, i * 2 + p + 1 + u, by_c)
                    down_panel(f, q, DOWN - 2, (p + DOWN - 2) % 2, p + DOWN - 2, by_c)
                    down_panel(f, q, DOWN - 1, (p + DOWN - 1) % 2, p + DOWN - 1, by_o, stop=True)

            norm(0, [4])
            ffn_up(0, 0)
            ffn_down(0)
            norm(1, [0, 1])

            def conv_tiles(j, u, first=False):
                if not first:
                    pe.wait_ge(mix_free, j - 1)
                for s in range(3):
                    tile(ps[:, (3 + 3 * u + s) % 8, :], j * 3 + MIX + s, (u + s) % 2, act_hi, act_lo,
                         (act_ready, KT) if first and u + s == 0 else None).then_inc(mix_done, 1)

            for j in range(2):
                conv_tiles(j, j, first=True)
            with pe.Fori(1, KT // 2) as i:
                for u in range(2):
                    conv_tiles(i * 2 + u, u)

            pe.wait_ge(mix_free, KT - 1)
            for g in range(4):
                tile(ps[:, 1 + g, :], GATE + g, g % 2, act_hi, act_lo).then_inc(gate_done, 1)
            with pe.Fori(1, 2 * KT // 4) as i:
                for u in range(4):
                    pe.wait_ge(gate_free, i * 4 + u - 3)
                    tile(ps[:, 1 + u, :], i * 4 + GATE + u, u % 2, act_hi, act_lo).then_inc(gate_done, 1)
            pe.wait_ge(mix_free, KT)
            pe.wait_ge(gate_free, 2 * KT)

            def head_projections(h, base):
                for u in range(2 * QT):
                    if u == 2 * QT - 1 and not isinstance(h, int):
                        pe.wait_ge(ret_made, h * VT)
                    tile(ps[:, u, :], base + u, u % 2, act_hi, act_lo).then_inc(qk_done, 1)
                for u in range(VT):
                    p = base + 2 * QT + u
                    pe.wait_ge(split_done, p + 1)
                    order = [(a, c) for c in range(2) for a in range(TT)] if u < VT - 1 else [(a, c) for a in range(TT) for c in range(2)]
                    for n, (a, c) in enumerate(order):
                        k = 2 * u + c
                        wh, wl = w_block(u % 2, c, V)
                        sl = slice(a * P, (a + 1) * P)
                        ins = product(ps[:, 4 + a, :], act_hi[:, k, sl], act_lo[:, k, sl], wh, wl, k == 0, k == KT - 1, opens=n == 0)
                        if u == VT - 1 and c == 1:
                            ins.then_inc(v_done, 1)

            def scores(h):
                pe.wait_ge(rot_ready, h * 2 * QT + 2 * QT)
                for a in range(TT):
                    sl = slice(a * P, (a + 1) * P)
                    for k in range(QT):
                        ins = product(ps[:, a, :], wide_hi[:, S_K + k, sl], wide_lo[:, S_K + k, sl],
                                      wide_hi[:, S_Q + k, :], wide_lo[:, S_Q + k, :], k == 0, k == QT - 1)
                    ins.then_inc(s_done, 1)

            def attend(h):
                pe.wait_ge(v_ready, h * TT + TT)
                for e in range(VT):
                    sl = slice(e * P, (e + 1) * P)
                    for k in range(TT):
                        if e == 0:
                            pe.wait_ge(s_ready, h * TT + k + 1)
                        ins = product(ps[:, 4 + e, :], wide_hi[:, S_V + k, sl], wide_lo[:, S_V + k, sl],
                                      wide_hi[:, S_S + k, :], wide_lo[:, S_S + k, :], k == 0, k == TT - 1)
                    ins.then_inc(o_done, 1)

            def head_gate(h, base):
                pe.wait_ge(mid_free, h * KT + KT)
                for e in range(VT):
                    if e >= 2:
                        pe.wait_ge(gsw_silu, h * VT + e - 1)
                    tile(ps[:, e % 2, :], base + e, e % 2, act_hi, act_lo).then_inc(gsw_done, 1)
                    if e == 0:
                        pe.wait_ge(o_added, h * (VT - 1) + VT - 1)
                        mm(ps[:, 2, :], ones[:, :], tmp[:, 5, :], start=True, stop=True).then_inc(o_summed, 1)

            def ret_out(h, base, n):
                for m in range(KT):
                    if m < 4:
                        if n is not None:
                            pe.wait_ge(s_decayed, h * TT + TT + m + 1)
                        elif m == 0:
                            pe.wait_ge(gsw_silu, HEADS * VT)
                    else:
                        pe.wait_ge(mid_free, (h + 1) * KT + m - 3)
                    ins = tile(ps[:, m % 4, :], base + m // 2, (m // 2) % 2, wide_hi[:, S_RET:S_RET + VT, :],
                               wide_lo[:, S_RET:S_RET + VT, :], (ret_ready, h * VT) if m == 0 else None,
                               k=VT, part=m % 2, parts=2)
                    ins.then_inc(mid_done, 1)

            head_projections(0, HEAD0)
            scores(0)
            for m in range(KT):
                if m < 4:
                    pe.wait_ge(s_decayed, m + 1)
                else:
                    pe.wait_ge(mid_free, m - 3)
                tile(ps[:, m % 4, :], HEAD0 + 2 * QT + VT + m, m % 2, wide_hi[:, S_CONV:S_CONV + KT, :],
                     wide_lo[:, S_CONV:S_CONV + KT, :], (mix_ready, 0) if m == 0 else None).then_inc(mid_done, 1)
            attend(0)
            head_gate(0, HEAD1 - VT)
            with pe.Fori(1, HEADS) as h:
                base = h * HEADP + (HEAD1 - HEADP)
                pe.wait_ge(gsw_silu, h * VT)
                head_projections(h, base)
                scores(h)
                ret_out(h - 1, base + 2 * QT + VT, 0)
                attend(h)
                head_gate(h, base + 2 * QT + 2 * VT)
            ret_out(HEADS - 1, ROUT, None)

            for m in range(KT):
                if m >= 4:
                    pe.wait_ge(wo_free, m - 3)
                tile(ps[:, 4 + m % 4, :], WO + m, m % 2, wide_hi[:, S_MERGE:S_MERGE + KT, :], wide_lo[:, S_MERGE:S_MERGE + KT, :],
                     (merge_ready, 0) if m == 0 else None).then_inc(wo_done, 1)
            norm(2, [2])
            ffn_up(1, 2 * KT)
            ffn_down(1)
            norm(3, [0])

        @block.scalar
        def _(act):
            do = nc.scalar.activation

            def hi_of(dst, src, made, **how):
                do(dst, src, ACT.Identity, **how).then_inc(made, 1)

            act.wait_ge(early_loaded, 16)
            do(silu_c, early_cols("c", 0, KT), ACT.Silu).then_inc(silu_c_made, 1)
            act.wait_ge(consts_set, 5)
            do(small[:, 6, 0:1], eps[:, :], ACT.Sqrt)
            def x_squares(a):
                act.wait_ge(x_loaded[a], 16)
                if a:
                    act.wait_ge(x_squared, a)
                do(tmp[:, 0:2, :].rearrange("p s t -> p (s t)"), x_tok[:, a, :], ACT.Square,
                   accum_out=small[:, 0, a:a + 1]).then_inc(x_squared, 1)
                act.wait_ge(x_squared, a + 1)
                do(small[:, 1, a:a + 1], small[:, 0, a:a + 1], ACT.Sqrt, scale=1.0 / D, bias=eps[:, :]).then_inc(x_std, 1)

            def x_hi(a):
                act.wait_ge(x_rstd, a + 1)
                hi_of(xr_hi[:, a, :], x_tok[:, a, :], xr_hi_made, scale=small[:, 2, a:a + 1])

            x_squares(0)
            x_hi(0)
            x_squares(1)
            x_squares(2)
            x_hi(1)
            x_squares(3)
            x_hi(2)
            x_hi(3)
            act.wait_ge(u_done, 1)
            do(tmp[:, 0, :], ps[:, 0, :], ACT.Identity).then_inc(u0_copied, 1)
            act.wait_ge(u_scale_made, 3)
            do(wide_hi[:, S_U:S_U + KT, 0:1], udc.rearrange("p (k o) -> p k o", o=1), ACT.Identity)
            for m in range(KT):
                hi_of(wide_hi[:, S_U + m, 1:T], u_tile(m)[:, 1:T], u_hi_made, scale=gain_mix[:, m:m + 1])
            def f_hi(m):
                act.wait_ge(f_made, 3 * (m + 1))
                hi_of(act_hi[:, m, :], tmp[:, 1 + 2 * (m % 2), :], f_hi_made)

            for m in range(KT):
                act.wait_ge(f_done, m + 1)
                if m >= 2:
                    act.wait_ge(f_made, 3 * (m - 1))
                do(tmp[:, 2 * (m % 2), 0:T // 2], ps[:, 2 + 2 * (m % 3), 0:T // 2], ACT.Identity).then_inc(f_q_copied, 1)
                if m:
                    f_hi(m - 1)
            f_hi(KT - 1)
            act.wait_ge(dec_loaded, 16)
            do(lgt[:, 0, :], dec, ACT.Abs).then_inc(act_chain, 1)
            act.wait_ge(act_chain, 1)
            do(lgt[:, 1, :], lgt[:, 0, :], ACT.Exp, scale=-1.0).then_inc(lg_exp, 1)

            def squares(n, free, two=False):
                do(small[:, 6, 0:1], eps[:, :], ACT.Sqrt)
                for m in range(KT):
                    act.wait_ge(free, m + 1)
                    if m >= 2:
                        act.wait_ge(squares_added, n * (KT - 2) + m - 1)
                    if two:
                        do(tmp[:, 1 if m == 0 else 3, :], res[:, m, :], ACT.Square, scale=col("g_final", m))
                    do(tmp[:, 0 if m == 0 else 2 if two else 1, :], res[:, m, :], ACT.Square).then_inc(res_squared, 1)

            def norm_hi(n, shift=False):
                act.wait_ge(norm_summed, n + 1)
                if n == 1:
                    do(tmp[:, 2, :], ps[:, 1, :], ACT.Sqrt, scale=1.0 / D, bias=eps_squared[:, :]).then_inc(norm_std, 1)
                    do(tmp[:, 3, :], ps[:, 0, :], ACT.Sqrt, scale=1.0 / D, bias=eps[:, :]).then_inc(norm_std, 1)
                else:
                    do(tmp[:, 2, :], ps[:, (4, None, 2, 0)[n], :], ACT.Sqrt, scale=1.0 / D, bias=eps[:, :]).then_inc(norm_std, 1)
                if n < 3:
                    for k in range(KT):
                        act.wait_ge(normed, n * KT + k + 1)
                        hi_of(act_hi[:, k, :], tmp[:, 5 + k % 2, :], norm_hi_made,
                              **({"bias": mod[:, 3 * KT + k:3 * KT + k + 1]} if shift else {}))

            def ffn_gate(f):
                def pair(j, u):
                    if f == 0:
                        act.wait_ge(conv_step[f], j * 3 + 3)
                        do(tmp[:, 1, :], tmp[:, 0, :], ACT.Silu).then_inc(silu_made[f], 1)
                    else:
                        act.wait_ge(up_done[f], j * 2 + 1)
                        do(tmp[:, 1, :], ps[:, 2 * u, :], ACT.Silu).then_inc(silu_made[f], 1)
                    act.wait_ge(prod_made[f], j + 1)
                    do(wide_hi[:, j, :], tmp[:, 2, :], ACT.Identity
                       ).then_inc(prod_hi_made[f], 1)

                with act.Fori(0, FT // 2) as i:
                    for u in range(2):
                        pair(i * 2 + u, u)

            squares(0, fnet_free)
            norm_hi(0, shift=True)
            ffn_gate(0)
            squares(1, dn_free[0], two=True)
            norm_hi(1)

            with act.Fori(0, KT // 2) as i:
                for u in range(2):
                    j = i * 2 + u
                    act.wait_ge(mix_done, j * 3 + 1)
                    do(tmp[:, 0, :], ps[:, 3 + 3 * u, :], ACT.Identity).then_inc(xc_copied, 1)
                    act.wait_ge(mix_free, j + 1)
                    do(wide_hi[:, j + S_CONV, :], tmp[:, 3, :], ACT.Identity
                       ).then_inc(mix_hi_made, 1)
            with act.Fori(0, 2 * KT // 4) as i:
                for u in range(4):
                    act.wait_ge(gate_done, i * 4 + u + 1)
                    do(gates[:, i * 4 + u, :], ps[:, 1 + u, :], ACT.Sigmoid
                       ).then_inc(gate_free, 1)

            def head(h):
                act.wait_ge(decay_args, h + 1)
                do(decay[:, :], decay[:, :], ACT.Exp).then_inc(decay_made, 1)
                for u in range(2 * QT):
                    act.wait_ge(rot_made, h * 2 * QT + u + 1)
                    hi_of(wide_hi[:, S_Q + u, :], tmp[:, 2 + u % 2, :], rot_hi_made)
                for a in range(TT):
                    act.wait_ge(v_done, h * TT + a + 1)
                    do(ps[:, 4 + a, :], ps[:, 4 + a, :], ACT.Identity, accum_out=small[:, 6, a:a + 1]).then_inc(v_summed, 1)
                act.wait_ge(v_summed, h * TT + TT)
                do(small[:, 7, :], small[:, 6, :], ACT.Identity, scale=-1.0 / V).then_inc(v_mean, 1)
                act.wait_ge(v_mean, h + 1)
                for a in range(TT):
                    hi_of(wide_hi[:, S_V + a, :], ps[:, 4 + a, :], v_hi_made, bias=small[:, 7, a:a + 1])
                for a in range(TT):
                    act.wait_ge(s_decayed, h * TT + a + 1)
                    hi_of(wide_hi[:, S_S + a, :], tmp[:, a % 2, :], s_hi_made)
                for e in range(VT):
                    act.wait_ge(o_done, h * VT + e + 1)
                    if e >= 2:
                        act.wait_ge(o_added, h * (VT - 1) + e - 1)
                    do(tmp[:, 5 if e == 0 else 6, :], ps[:, 4 + e, :], ACT.Square).then_inc(o_squared, 1)
                def gate(e):
                    act.wait_ge(gsw_done, h * VT + e + 1)
                    do(tmp[:, e, :], ps[:, e % 2, :], ACT.Silu).then_inc(gsw_silu, 1)

                def ret_hi(e):
                    act.wait_ge(ret_made, h * VT + e + 1)
                    hi_of(wide_hi[:, S_RET + e, :], tmp[:, e, :], ret_hi_made)

                gate(0)
                act.wait_ge(o_summed, h + 1)
                do(tmp[:, 6, :], ps[:, 2, :], ACT.Sqrt, scale=1.0 / V, bias=eps[:, :]).then_inc(o_std, 1)
                gate(1)
                gate(2)
                ret_hi(0)
                ret_hi(1)
                gate(3)
                ret_hi(2)
                ret_hi(3)

            head(0)
            with act.Fori(1, HEADS) as h:
                head(h)
            for m in range(KT):
                act.wait_ge(mid_added, (HEADS - 1) * KT + m + 1)
                hi_of(wide_hi[:, S_MERGE + m, :], gates[:, m, :], merge_hi_made)
            squares(2, wo_free)
            norm_hi(2)
            ffn_gate(1)
            squares(3, dn_free[1])
            norm_hi(3)

        @block.vector
        def _(dve):
            tt, ts, stt = nc.vector.tensor_tensor, nc.vector.tensor_scalar, nc.vector.scalar_tensor_tensor
            links = [0]

            def link(ins):
                links[0] += 1
                ins.then_inc(chain, 1)
                dve.wait_ge(chain, links[0])

            def lo_of(dst, src, hi, made, ready, n):
                dve.wait_ge(made, n)
                tt(dst, src, f32(hi), SUB).then_inc(ready, 1)

            def x_rstds(a):
                dve.wait_ge(x_std, a + 1)
                nc.vector.reciprocal(small[:, 2, a:a + 1], small[:, 1, a:a + 1]).then_inc(x_rstd, 1)

            def x_lo(a):
                dve.wait_ge(x_rstd, a + 1)
                dve.wait_ge(xr_hi_made, a + 1)
                stt(out=xr_lo[:, a, :], in0=x_tok[:, a, :], scalar=small[:, 2, a:a + 1], in1=f32(xr_hi[:, a, :]),
                    op0=MUL, op1=SUB).then_inc(xr_made, 1)

            x_rstds(0)
            x_lo(0)
            x_rstds(1)
            x_rstds(2)
            x_lo(1)
            x_rstds(3)
            x_lo(2)
            x_lo(3)

            def mod_chunk(c):
                if c == 2:
                    dve.wait_ge(mod_summed, 1)
                acc = mod_acc(c)
                for k in range(KT):
                    w = mod_weights(c, k)[:, 0, 0:D]
                    if k % MOD_STEPS == 0:
                        dve.wait_ge(*mod_loaded(c, k))
                    if k == 0:
                        ts(acc, w, silu_c[:, 0:1], None, MUL).then_inc(mod_step, 1)
                    else:
                        dve.wait_ge(mod_step, KT * c + k)
                        stt(out=acc, in0=w, scalar=silu_c[:, k:k + 1], in1=acc, op0=MUL, op1=ADD).then_inc(mod_step, 1)

            def mod_columns(c0, c1):
                s = slice(c0 * KT, c1 * KT)
                b = early_cols("b_mod", c0 * KT, (c1 - c0) * KT)
                dve.wait_ge(mod_summed, c1)
                tt(mod[:, s], ps[:, 7, s], b, ADD).then_inc(mod_read, 1)
                dve.wait_ge(mod_read, {2: 1, 3: 2, 5: 3, 6: 4}[c1])

            dve.wait_ge(silu_c_made, 1)
            mod_chunk(0)
            mod_chunk(1)
            mod_columns(0, 2)
            stt(out=gain_mix, in0=mod[:, KT:2 * KT], scalar=1.0, in1=early_cols("g_norm_mix", 0, KT),
                op0=ADD, op1=MUL).then_inc(u_scale_made, 1)
            ts(shift_dc, mod[:, 0:KT], float(T), None, MUL).then_inc(u_scale_made, 1)
            dve.wait_ge(u_scale_made, 2)
            dve.wait_ge(u_done, KT)
            dve.wait_ge(u0_copied, 1)
            nc.vector.tensor_copy(udc[:, 0:1], tmp[:, 0, 0:1])
            nc.vector.tensor_copy(udc[:, 1:7].rearrange("p (k o) -> p k o", o=1), ps[:, 1:7, 0:1])
            link(nc.vector.tensor_copy(udc[:, 7:8], ps[:, 0, 0:1]))
            link(tt(udc, udc, gain_mix, MUL))
            tt(udc, udc, shift_dc, ADD).then_inc(u_scale_made, 1)
            for m in range(KT):
                dve.wait_ge(u_hi_made, m + 1)
                if m == 0:
                    dve.wait_ge(u_scale_made, 3)
                    tt(wide_lo[:, S_U:S_U + KT, 0:1], udc.rearrange("p (k o) -> p k o", o=1), f32(wide_hi[:, S_U:S_U + KT, 0:1]), SUB)
                stt(out=wide_lo[:, S_U + m, 1:T], in0=u_tile(m)[:, 1:T], scalar=gain_mix[:, m:m + 1],
                    in1=f32(wide_hi[:, S_U + m, 1:T]), op0=MUL, op1=SUB).then_inc(u_made, 1)
            half = T // 2
            for m in range(KT):
                even, odd, f = ps[:, 1 + 2 * (m % 3), :], tmp[:, 2 * (m % 2), :], tmp[:, 1 + 2 * (m % 2), :]
                if m >= 2:
                    dve.wait_ge(f_ready, m - 1)
                dve.wait_ge(f_q_copied, m + 1)
                tt(f[:, 1:half], even[:, 1:half], odd[:, 1:half], SUB).then_inc(f_made, 1)
                tt(f[:, T - 1:half:-1], even[:, 1:half], odd[:, 1:half], ADD).then_inc(f_made, 1)
                nc.vector.tensor_copy(f[:, 0:half + 1:half], even[:, 0:half + 1:half]).then_inc(f_made, 1)
            mod_chunk(2)
            dve.wait_ge(f_ready, KT)
            mod_chunk(3)
            mod_columns(2, 3)

            dve.wait_ge(cols_loaded, 16)
            link(tt(gain_12[:, :], late_cols("g_final", KT), late_cols("g_mix_2", KT), MUL))

            def add_squares(n, m, two=False):
                if m:
                    dve.wait_ge(res_squared, n * KT + m + 1)
                    if two:
                        tt(tmp[:, 1, :], tmp[:, 1, :], tmp[:, 3, :], ADD)
                    tt(tmp[:, 0, :], tmp[:, 0, :], tmp[:, 2 if two else 1, :], ADD).then_inc(squares_added, 1)
                    dve.wait_ge(squares_added, n * (KT - 2) + m)

            dve.wait_ge(xt_loaded, 16)
            for m in range(KT):
                dve.wait_ge(fnet_done, m + 1)
                stt(out=res[:, m, :], in0=ps[:, m % 7, :], scalar=mod[:, 2 * KT + m:2 * KT + m + 1], in1=res[:, m, :],
                    op0=MUL, op1=ADD).then_inc(fnet_free, 1)
                if m:
                    add_squares(0, m - 1)
                if m == 2:
                    mod_chunk(4)
            mod_columns(3, 5)
            link(stt(out=gain_ffn[:, :], in0=mod[:, 4 * KT:5 * KT], scalar=1.0,
                     in1=late_cols("g_norm_ffn", KT), op0=ADD, op1=MUL))

            def norm(n, gain, shift=False):
                dve.wait_ge(norm_std, n + 1 + (n > 1))
                rstd = tmp[:, 2, :]
                nc.vector.reciprocal(rstd, rstd).then_inc(norm_rstd, 1)
                dve.wait_ge(norm_rstd, n + 1)
                for k in range(KT + 1):
                    if k < KT:
                        dst = tmp[:, 5 + k % 2, :] if n < 3 else gates[:, k, :]
                        if n < 3 and k >= 2:
                            dve.wait_ge(act_ready, n * KT + k - 1)
                        stt(out=dst, in0=res[:, k, :], scalar=gain(k), in1=rstd, op0=MUL, op1=MUL
                            ).then_inc(normed if n < 3 else out_made, 1)
                    if k == 0 or n == 3:
                        continue
                    k -= 1
                    dve.wait_ge(norm_hi_made, n * KT + k + 1)
                    hi = f32(act_hi[:, k, :])
                    if shift:
                        stt(out=act_lo[:, k, :], in0=tmp[:, 5 + k % 2, :], scalar=mod[:, 3 * KT + k:3 * KT + k + 1], in1=hi,
                            op0=ADD, op1=SUB).then_inc(act_ready, 1)
                    else:
                        tt(act_lo[:, k, :], tmp[:, 5 + k % 2, :], hi, SUB).then_inc(act_ready, 1)

            def ffn_product(f):
                def pair(j, u):
                    dve.wait_ge(up_done[f], j * 2 + 2 - (f == 0))
                    if f == 0:
                        g = ps[:, 2 * u, :]
                        w = [col("w_ffn_conv", j + FT * i) for i in range(3)]
                        c = tmp[:, 0, :]
                        ts(c, g, w[1], col("b_ffn_conv", j), MUL, ADD).then_inc(conv_step[f], 1)
                        dve.wait_ge(conv_step[f], j * 3 + 1)
                        stt(out=c[:, 1:T], in0=g[:, 0:T - 1], scalar=w[0], in1=c[:, 1:T], op0=MUL, op1=ADD).then_inc(conv_step[f], 1)
                        dve.wait_ge(conv_step[f], j * 3 + 2)
                        stt(out=c[:, 0:T - 1], in0=g[:, 1:T], scalar=w[2], in1=c[:, 0:T - 1], op0=MUL, op1=ADD).then_inc(conv_step[f], 1)
                        dve.wait_ge(up_done[f], j * 2 + 2)
                    dve.wait_ge(silu_made[f], j + 1)
                    tt(tmp[:, 2, :], ps[:, 2 * u + 1, :], tmp[:, 1, :], MUL).then_inc(prod_made[f], 1)
                    hi, lo = (w[:, j, :] for w in (wide_hi, wide_lo))
                    lo_of(lo, tmp[:, 2, :], hi, prod_hi_made[f], wide_ready[f], j + 1)
                    dve.wait_ge(wide_ready[f], j + 1)

                with dve.Fori(0, FT // 2) as i:
                    for u in range(2):
                        pair(i * 2 + u, u)

            norm(0, lambda k: gain_ffn[:, k:k + 1], shift=True)
            ffn_product(0)
            mod_chunk(5)
            mod_columns(5, 6)

            dve.wait_ge(lg_exp, 1)
            u, s, s2, p = (lgt[:, i, :] for i in (1, 2, 3, 4))
            link(ts(s, u, 2.0, None, ADD))
            link(nc.vector.reciprocal(s2, s))
            link(tt(s, u, s2, MUL))
            link(tt(s2, s, s, MUL))
            link(ts(p, s2, 1.0 / 17, None, MUL))
            for n in (15, 13, 11, 9, 7, 5, 3):
                link(stt(out=p, in0=p, scalar=1.0 / n, in1=s2, op0=ADD, op1=MUL))
            link(stt(out=p, in0=p, scalar=1.0, in1=s, op0=ADD, op1=MUL))
            link(ts(s, dec, 0.0, None, ALU.min))
            link(stt(out=lg[:, :], in0=p, scalar=-2.0, in1=s, op0=MUL, op1=ADD))
            link(ts(lg[:, HEADS:], lg[:, HEADS:], -1.0, None, MUL))
            for m in range(KT):
                dve.wait_ge(dn_done[0], m + 1)
                stt(out=res[:, m, :], in0=ps[:, m, :], scalar=mod[:, 5 * KT + m:5 * KT + m + 1], in1=res[:, m, :],
                    op0=MUL, op1=ADD).then_inc(dn_free[0], 1)
                if m:
                    add_squares(1, m - 1, two=True)
            norm(1, lambda k: gain_12[:, k:k + 1])
            dve.wait_ge(norm_std, 3)
            link(nc.vector.reciprocal(tmp[:, 3, :], tmp[:, 3, :]))
            for k in range(KT):
                stt(out=res[:, k, :], in0=res[:, k, :], scalar=col("g_final", k), in1=tmp[:, 3, :], op0=MUL, op1=MUL
                    ).then_inc(res_scaled, 1)

            with dve.Fori(0, KT // 2) as i:
                for u in range(2):
                    j = i * 2 + u
                    gb, gc = ps[:, (4 + 3 * u) % 8, :], ps[:, (5 + 3 * u) % 8, :]
                    w = [col("w_conv_2", j + KT * n) for n in range(3)]
                    dve.wait_ge(mix_done, j * 3 + 3)
                    dve.wait_ge(xc_copied, j + 1)
                    g, c = tmp[:, 1, :], tmp[:, 2, :]
                    tt(g, gc, tmp[:, 0, :], MUL).then_inc(mix_step, 1)
                    dve.wait_ge(mix_step, j * 4 + 1)
                    ts(c, g, w[1], None, MUL).then_inc(mix_step, 1)
                    dve.wait_ge(mix_step, j * 4 + 2)
                    stt(out=c[:, 1:T], in0=g[:, 0:T - 1], scalar=w[0], in1=c[:, 1:T], op0=MUL, op1=ADD).then_inc(mix_step, 1)
                    dve.wait_ge(mix_step, j * 4 + 3)
                    stt(out=c[:, 0:T - 1], in0=g[:, 1:T], scalar=w[2], in1=c[:, 0:T - 1], op0=MUL, op1=ADD).then_inc(mix_step, 1)
                    dve.wait_ge(mix_step, j * 4 + 4)
                    tt(tmp[:, 3, :], gb, c, MUL).then_inc(mix_free, 1)
                    hi, lo = (x[:, j + S_CONV, :] for x in (wide_hi, wide_lo))
                    lo_of(lo, tmp[:, 3, :], hi, mix_hi_made, mix_ready, j + 1)
                    dve.wait_ge(mix_ready, j + 1)

            def head(h):
                if not isinstance(h, int):
                    dve.wait_ge(ret_ready, h * VT)
                dve.wait_ge(rel_loaded, h * 16 + 16)
                ts(tmp_wide, decay[:, :], 0.0, lg[:, ds(h, 1)], ALU.max, MUL).then_inc(rot_step, 1)
                dve.wait_ge(rot_step, h * 10 + 1)
                ts(decay[:, :], decay[:, :], 0.0, lg[:, ds(h + HEADS, 1)], ALU.min, MUL).then_inc(rot_step, 1)
                dve.wait_ge(rot_step, h * 10 + 2)
                tt(decay[:, :], decay[:, :], tmp_wide, ADD).then_inc(decay_args, 1)
                for r in range(2):
                    a, b = ps[:, QT * r, :], ps[:, QT * r + 1, :]
                    n = h * 10 + 2 + 4 * r
                    dve.wait_ge(qk_done, h * 2 * QT + QT * (r + 1))
                    if r or not isinstance(h, int):
                        dve.wait_ge(rot_ready, h * 2 * QT + QT * r)
                    for i, (x0, x1, op) in enumerate(((0, 1, SUB), (1, 0, ADD))):
                        if i:
                            dve.wait_ge(rot_made, h * 2 * QT + QT * r + i)
                        tt(tmp[:, 0, :], a, rope[:, x0, :], MUL).then_inc(rot_step, 1)
                        tt(tmp[:, 1, :], b, rope[:, x1, :], MUL).then_inc(rot_step, 1)
                        dve.wait_ge(rot_step, n + 2 * i + 2)
                        tt(tmp[:, 2 + i, :], tmp[:, 0, :], tmp[:, 1, :], op).then_inc(rot_made, 1)
                    for i in range(QT):
                        lo_of(wide_lo[:, S_Q + QT * r + i, :], tmp[:, 2 + i, :], wide_hi[:, S_Q + QT * r + i, :],
                              rot_hi_made, rot_ready, h * 2 * QT + QT * r + i + 1)
                for a in range(TT):
                    dve.wait_ge(v_hi_made, h * TT + a + 1)
                    stt(out=wide_lo[:, S_V + a, :], in0=ps[:, 4 + a, :], scalar=small[:, 7, a:a + 1],
                        in1=f32(wide_hi[:, S_V + a, :]), op0=ADD, op1=SUB).then_inc(v_ready, 1)
                dve.wait_ge(decay_made, h + 1)
                for a in range(TT + 1):
                    if a < TT:
                        dve.wait_ge(s_done, h * TT + a + 1)
                        if a >= 2:
                            dve.wait_ge(s_ready, h * TT + a - 1)
                        c0 = (TT - 1 - a) * P
                        stt(out=tmp[:, a % 2, :], in0=ps[:, a, :], scalar=QK ** -0.5, in1=decay[:, c0:c0 + T],
                            op0=MUL, op1=MUL).then_inc(s_decayed, 1)
                    if a:
                        lo_of(wide_lo[:, S_S + a - 1, :], tmp[:, (a - 1) % 2, :], wide_hi[:, S_S + a - 1, :],
                              s_hi_made, s_ready, h * TT + a)
                if isinstance(h, int):
                    for m in range(KT):
                        dve.wait_ge(mid_done, m + 1)
                        tt(gates[:, m, :], ps[:, m % 4, :], gates[:, m, :], MUL).then_inc(mid_free, 1)
                else:
                    merge(h - 1)
                for e in range(1, VT):
                    dve.wait_ge(o_squared, h * VT + e + 1)
                    tt(tmp[:, 5, :], tmp[:, 5, :], tmp[:, 6, :], ADD).then_inc(o_added, 1)
                    dve.wait_ge(o_added, h * (VT - 1) + e)
                dve.wait_ge(o_std, h + 1)
                nc.vector.reciprocal(tmp[:, 6, :], tmp[:, 6, :]).then_inc(o_rstd, 1)

                def gated(e):
                    dve.wait_ge(gsw_silu, h * VT + e + 1)
                    stt(out=tmp[:, e, :], in0=ps[:, 4 + e, :], scalar=col("g_ret_2", h * VT + e), in1=tmp[:, e, :],
                        op0=MUL, op1=MUL).then_inc(o_gated, 1)

                def scaled(e):
                    dve.wait_ge(o_rstd, h + 1)
                    dve.wait_ge(o_gated, h * VT + e + 1)
                    tt(tmp[:, e, :], tmp[:, e, :], tmp[:, 6, :], MUL).then_inc(ret_made, 1)

                def ret_lo(e):
                    lo_of(wide_lo[:, S_RET + e, :], tmp[:, e, :], wide_hi[:, S_RET + e, :], ret_hi_made, ret_ready, h * VT + e + 1)

                gated(0)
                gated(1)
                scaled(0)
                scaled(1)
                gated(2)
                scaled(2)
                ret_lo(0)
                ret_lo(1)
                gated(3)
                scaled(3)
                ret_lo(2)
                ret_lo(3)

            def merge(h, last=False):
                dve.wait_ge(ret_ready, h * VT + VT)
                dve.wait_ge(s_ready, h * TT + (TT if last else 2 * TT))
                for m in range(KT):
                    if m >= 2:
                        dve.wait_ge(mid_added, h * KT + m - 1)
                    dve.wait_ge(mid_done, (h + 1) * KT + m + 1)
                    tt(tmp[:, m % 2, :], ps[:, m % 4, :], gates[:, KT + m, :], MUL).then_inc(mid_free, 1)
                    dve.wait_ge(mid_free, (h + 1) * KT + m + 1)
                    tt(gates[:, m, :], gates[:, m, :], tmp[:, m % 2, :], ADD).then_inc(mid_added, 1)
                    if last:
                        lo_of(wide_lo[:, S_MERGE + m, :], gates[:, m, :], wide_hi[:, S_MERGE + m, :], merge_hi_made, merge_ready, m + 1)

            dve.wait_ge(rope_loaded, 16)
            dve.wait_ge(mix_ready, KT)
            dve.wait_ge(gate_free, 2 * KT)
            head(0)
            with dve.Fori(1, HEADS) as h:
                head(h)
            merge(HEADS - 1, last=True)

            dve.wait_ge(res_scaled, KT)
            for m in range(KT):
                dve.wait_ge(wo_done, m + 1)
                tt(res[:, m, :], ps[:, 4 + m % 4, :], res[:, m, :], ADD).then_inc(wo_free, 1)
                if m:
                    add_squares(2, m - 1)
            norm(2, lambda k: col("g_ffn_2", k))
            ffn_product(1)
            for m in range(KT):
                dve.wait_ge(dn_done[1], m + 1)
                tt(res[:, m, :], ps[:, m, :], res[:, m, :], ADD).then_inc(dn_free[1], 1)
                if m:
                    add_squares(3, m - 1)
            norm(3, lambda k: col("g_final_2", k))


def kernel(**inputs):
    from concourse import bacc
    from concourse.bass_utils import run_bass_kernel_spmd

    F32 = mybir.dt.float32
    nc = bacc.Bacc("TRN2", target_bir_lowering=False, num_devices=1, dynamic_dma_scratch_size=64)
    a = {n: np.asarray(v) for n, v in inputs.items()}
    arrays = {n: np.ascontiguousarray(a[n][0]) for n in (
        "w_mod", "w_ffn_up", "w_ffn_down", "w_fnet_out", "w_in_2", "w_a_out_2", "w_r_out_2", "w_o_2",
        "w_ff_gate_2", "w_ff_up_2", "w_ff_down_2")}
    arrays["x"] = np.ascontiguousarray(a["x"][0])
    arrays["x_t"] = np.ascontiguousarray(a["x"][0].T)
    arrays["columns"] = np.ascontiguousarray(np.concatenate([a[n].reshape(-1) for n, _ in VECTORS]).reshape(COLS, P).T)
    arrays["decays"] = np.ascontiguousarray(np.broadcast_to(
        np.concatenate([a["dec_f_2"].reshape(-1), a["dec_b_2"].reshape(-1)]), (P, 2 * HEADS)))
    arrays.update(tables())
    t = {n: nc.dram_tensor(f"in_{n}", v.shape, F32, kind="ExternalInput").ap() for n, v in arrays.items()}
    out = nc.dram_tensor("out", (D, T), F32, kind="ExternalOutput").ap()
    build(nc, t, out)
    r = run_bass_kernel_spmd(nc, [{f"in_{n}": v for n, v in arrays.items()}], core_ids=[0])
    return np.ascontiguousarray(r.results[0]["out"].T)[None]
```

```python
from contextlib import ExitStack

import numpy as np
import concourse.bass as bass
from concourse import mybir

P = 128
D = 1024
T = 512
KT = D // P
TT = T // P
FF = 2816
FT = FF // P
GROUP = 256
HEADS, QK, V = 4, 256, 512
QT, VT = QK // P, V // P
EPS = 1e-6
PANEL = 8 * P
RAW, SPLIT = 4, 2
MOD_STEPS = 2
MOD_LOADS = KT // MOD_STEPS
MOD_AFTER = {2: 2, 4: 3, 6: 4}
PAIR = 2
OUT_POOL = 5
OUT_STORES = ((0, 2), (5, 6), (2, 5), (6, 8))
QUAD = 4
DOWN = FT // 2
REL = T + (TT - 1) * P

FNET = 0
UP = [FNET + KT, 0]
DN = [UP[0] + PAIR * FT, 0]
MIX = DN[0] + 2 * DOWN
GATE = MIX + 3 * KT
HEAD0 = GATE + 2 * KT
HEAD1 = HEAD0 + 2 * QT + VT + KT + VT
HEADP = 2 * QT + VT + VT + VT
ROUT = HEAD1 + (HEADS - 1) * HEADP
WO = ROUT + VT
UP[1] = WO + KT
DN[1] = UP[1] + PAIR * FT
PANELS = DN[1] + 2 * DOWN

NORMED = (3, 5, 6)
HALF = T // 2

XC, GB, GC, WQ, WK, WV, GSW, GA, GR = np.cumsum([0, D, D, D, D, D, 2 * D, 2 * D, D]).tolist()

VECTORS = [("c", KT), ("b_mod", 6 * KT), ("g_norm_mix", KT),
           ("g_norm_ffn", KT), ("g_final", KT),
           ("w_ffn_conv", 3 * FT), ("b_ffn_conv", FT), ("g_mix_2", KT), ("w_conv_2", 3 * KT),
           ("g_ret_2", HEADS * VT), ("g_ffn_2", KT), ("g_final_2", KT)]
AT, _n = {}, 0
for _name, _count in VECTORS:
    AT[_name] = _n
    _n += _count
COLS = _n
EARLY = AT["g_norm_ffn"]

S_XR, S_DFT, S_DFTD, S_U = 0, 8, 12, 14
S_CONV, S_RET, S_MERGE, S_Q, S_K, S_V, S_S = 0, 0, 4, 8, 10, 12, 16


def tables():
    l, k = np.arange(T)[:, None], np.arange(T // 2 + 1)[None]
    ang = 2 * np.pi * ((l * k) % T) / T
    dft_tokens = np.concatenate([np.cos(ang), np.sin(ang[:, 1:T // 2])], axis=1)
    d = np.arange(GROUP)
    ang = 2 * np.pi * ((d[:, None] * d[None]) % GROUP) / GROUP
    dft_features = np.concatenate([np.cos(ang), np.sin(ang)], axis=1) / np.sqrt(T * GROUP)
    freqs = np.float32(10000.0) ** (-np.arange(0, QK, 2, dtype=np.float32) / np.float32(QK))
    ang = (freqs[:, None] * np.arange(T, dtype=np.float32)[None]).astype(np.float32).astype(np.float64)
    rope = np.stack([np.cos(ang), np.sin(ang)])
    relative = np.arange(REL)[None] - (TT - 1) * P - np.arange(P)[:, None]
    made = {"dft_tokens": dft_tokens, "dft_features": dft_features, "rope": rope, "relative": relative}
    return {n: np.ascontiguousarray(v.astype(np.float32)) for n, v in made.items()}


def build(nc, t, out):
    F32, F32R = mybir.dt.float32, mybir.dt.float32r
    ALU, ACT = mybir.AluOpType, mybir.ActivationFunctionType
    MUL, ADD, SUB = ALU.mult, ALU.add, ALU.subtract
    ds = bass.ds
    ctx = ExitStack()
    with ctx:
        def sb(name, shape, dt=F32):
            return ctx.enter_context(nc.sbuf_tensor(name, shape, dt))

        def sem(name):
            return ctx.enter_context(nc.semaphore(name))

        res = sb("res", [P, KT, T])
        act_hi, act_lo = sb("act_hi", [P, KT, T], F32R), sb("act_lo", [P, KT, T], F32R)
        wide_hi, wide_lo = sb("wide_hi", [P, FT, T], F32R), sb("wide_lo", [P, FT, T], F32R)
        gates = sb("gates", [P, 2 * KT, T])
        raw = sb("raw", [P, RAW, PANEL])
        w_hi, w_lo = sb("w_hi", [P, SPLIT, PANEL], F32R), sb("w_lo", [P, SPLIT, PANEL], F32R)
        tmp = sb("tmp", [P, 7, T])
        rope = sb("rope", [P, 2, T])
        decay = sb("decay", [P, REL])
        cols = sb("cols", [P, COLS - EARLY])
        lg = sb("lg", [P, 2 * HEADS])
        mod = sb("mod", [P, 6 * KT])
        gain_ffn, gain_12 = sb("gain_ffn", [P, KT]), sb("gain_12", [P, KT])
        small = sb("small", [P, 8, TT])
        eps, eps_squared, zero = sb("eps", [P, 1]), sb("eps_squared", [P, 1]), sb("zero", [P, 1])
        ones = sb("ones", [P, P])
        eps_ones = sb("eps_ones", [P, P])
        ps = ctx.enter_context(nc.psum_tensor("ps", [P, 8, T], F32))

        early = tmp[:, 4, :]
        dec, silu_c, gain_mix, shift_dc, udc = (early[:, EARLY + 8 * i:EARLY + 8 * (i + 1)] for i in range(5))
        lgt = early[:, EARLY + 40:EARLY + 80].rearrange("p (i n) -> p i n", i=5)

        x_tok = res[:, :, :].rearrange("p k t -> p (k t)").rearrange("p (a d) -> p a d", a=TT)
        xr_hi, xr_lo = (w[:, S_XR:S_XR + 2 * TT, :].rearrange("p s t -> p (s t)").rearrange("p (a d) -> p a d", a=TT)
                        for w in (wide_hi, wide_lo))
        modw = gates[:, :, :].rearrange("p s t -> p (s t)").rearrange("p (k n) -> p k n", k=KT)
        modw_res = res[:, :, :].rearrange("p s t -> p (s t)").rearrange("p (k n) -> p k n", k=KT // 2)
        tmp_flat = tmp[:, :, :].rearrange("p s t -> p (s t)")
        tmp_wide = tmp[:, 5:7, :].rearrange("p s t -> p (s t)")[:, 0:REL]

        def col(name, i=0):
            return cols[:, ds(i + AT[name] - EARLY, 1)]

        def early_cols(name, i, n):
            return early[:, AT[name] + i:AT[name] + i + n]

        def late_cols(name, n):
            return cols[:, AT[name] - EARLY:AT[name] - EARLY + n]

        def u_tile(m):
            return tmp[:, 0, :] if m == 0 else ps[:, m % 7, :]

        def f32(ap):
            return ap.bitcast(F32)

        def mod_place(c, k):
            if c == 1:
                return k - KT // 2 if k >= KT // 2 else None
            return k if c == 0 else (k + KT // 2) % KT

        def mod_weights(c, k, n=1):
            at = mod_place(c, k)
            return modw_res[:, k:k + n, :] if at is None else modw[:, at:at + n, :]

        def mod_loaded(c, k):
            at = mod_place(c, k)
            if at is None:
                return modw_res_loaded[k // MOD_STEPS], 16
            before = [b for b in range(c) if any(mod_place(b, j) == at for j in range(KT))]
            return modw_loaded[at // MOD_STEPS], 16 * (len(before) + 1)

        def mod_acc(c):
            first = 2 if c in (1, 3) else 5
            return tmp_flat[:, first * T:first * T + D]

        x_loaded = [sem(f"x_loaded{i}") for i in range(TT)]
        early_loaded, dft_loaded, dftd_loaded, cols_loaded, dec_loaded = (
            sem(n) for n in ("early_loaded", "dft_loaded", "dftd_loaded", "cols_loaded", "dec_loaded"))
        rope_loaded, xt_loaded, rel_loaded = sem("rope_loaded"), sem("xt_loaded"), sem("rel_loaded")
        modw_loaded = [sem(f"modw_loaded{i}") for i in range(MOD_LOADS)]
        modw_res_loaded = [sem(f"modw_res_loaded{i}") for i in range(MOD_LOADS // 2)]
        raw_loaded = [sem(f"raw_loaded{i}") for i in range(RAW)]
        dft_hi_made, dft_split = sem("dft_hi_made"), sem("dft_split")
        hi_made, split_done, panel_used = sem("hi_made"), sem("split_done"), sem("panel_used")
        consts_set = sem("consts_set")
        chain, act_chain = sem("chain"), sem("act_chain")
        silu_c_made, x_squared, x_std, x_rstd = sem("silu_c_made"), sem("x_squared"), sem("x_std"), sem("x_rstd")
        xr_hi_made, xr_made = sem("xr_hi_made"), sem("xr_made")
        lg_exp, lg_made = sem("lg_exp"), sem("lg_made")
        mod_step, mod_summed, mod_read, u_scale_made = (
            sem(n) for n in ("mod_step", "mod_summed", "mod_read", "u_scale_made"))
        res_scaled, keys_done, key_scale_made = sem("res_scaled"), sem("keys_done"), sem("key_scale_made")
        u_done, u0_copied, udc_hi_made, udc_made, u_hi_made, u_made = (
            sem(n) for n in ("u_done", "u0_copied", "udc_hi_made", "udc_made", "u_hi_made", "u_made"))
        f_done, f_q_copied, f_made, f_hi_made, f_ready = (
            sem(n) for n in ("f_done", "f_q_copied", "f_made", "f_hi_made", "f_ready"))
        fnet_done, fnet_free = sem("fnet_done"), sem("fnet_free")
        res_squared, squares_added, norm_summed, norm_std, norm_rstd = (
            [sem(f"{n}{i}") for i in range(4)]
            for n in ("res_squared", "squares_added", "norm_summed", "norm_std", "norm_rstd"))
        normed, norm_hi_made, act_ready = sem("normed"), *(
            [sem(f"{n}{i}") for i in range(3)] for n in ("norm_hi_made", "act_ready"))
        up_done, conv_step, silu_made, prod_made, prod_hi_made, wide_ready = (
            [sem(f"{n}{f}") for f in range(2)]
            for n in ("up_done", "conv_step", "silu_made", "prod_made", "prod_hi_made", "wide_ready"))
        dn_done, dn_free = [sem("dn_done0"), sem("dn_done1")], [sem("dn_free0"), sem("dn_free1")]
        mix_done, mix_step, mix_free, mix_hi_made, mix_ready = (
            sem(n) for n in ("mix_done", "mix_step", "mix_free", "mix_hi_made", "mix_ready"))
        gate_done, gate_scaled, gate_free = sem("gate_done"), sem("gate_scaled"), sem("gate_free")
        decay_args, decay_made = sem("decay_args"), sem("decay_made")
        qk_done, rot_step, rot_made, rot_hi_made, rot_ready = (
            sem(n) for n in ("qk_done", "rot_step", "rot_made", "rot_hi_made", "rot_ready"))
        v_done, v_summed, v_mean, v_hi_made, v_ready = (sem(n) for n in ("v_done", "v_summed", "v_mean", "v_hi_made", "v_ready"))
        s_done, s_decayed, s_hi_made, s_ready = (sem(n) for n in ("s_done", "s_decayed", "s_hi_made", "s_ready"))
        mid_done, mid_free, mid_added = sem("mid_done"), sem("mid_free"), sem("mid_added")
        o_done, o_squared, o_added, o_summed, o_std, o_rstd = (
            sem(n) for n in ("o_done", "o_squared", "o_added", "o_summed", "o_std", "o_rstd"))
        gsw_done, gsw_scaled, gsw_silu, o_gated, ret_made, ret_hi_made, ret_ready = (
            sem(n) for n in ("gsw_done", "gsw_scaled", "gsw_silu", "o_gated", "ret_made", "ret_hi_made", "ret_ready"))
        merge_hi_made, merge_ready = sem("merge_hi_made"), sem("merge_ready")
        wo_done, wo_free = sem("wo_done"), sem("wo_free")
        out_gained, out_made, out_made_pool = (
            [sem(f"{n}{i}") for i in range(2)] for n in ("out_gained", "out_made", "out_made_pool"))
        out_stored = sem("out_stored")

        block = ctx.enter_context(nc.Block())

        @block.sync
        def _(sp):
            def view(w, k):
                return w.rearrange("(k p) n -> p k n", k=k)

            w_up = view(t["w_ffn_up"], KT)
            w_in = view(t["w_in_2"], KT)
            w_out_r = t["w_r_out_2"].rearrange("(h k p) n -> p h k n", h=HEADS, k=VT)

            def panel(p, slot, src, blocks, first=False):
                if not first:
                    sp.wait_ge(split_done, p - RAW + 1)
                dst = raw[:, slot, :].rearrange("p (k n) -> p k n", k=blocks)
                sp.dma_start(dst, src).then_inc(raw_loaded[slot], 16)

            def mod_chunk(c, tiles=range(0, KT, MOD_STEPS)):
                for k in tiles:
                    at = mod_place(c, k)
                    if at is None:
                        sp.wait_ge(xr_made, TT)
                        sp.wait_ge(xr_hi_made, TT)
                    before = [(b, j) for b in range(c) for j in range(KT) if at is not None and mod_place(b, j) == at]
                    if before:
                        b, j = before[-1]
                        sp.wait_ge(mod_step, b * KT + j + MOD_STEPS)
                    sp.dma_start(mod_weights(c, k, MOD_STEPS), view(t["w_mod"], KT)[:, k:k + MOD_STEPS, c * D:(c + 1) * D]
                                 ).then_inc(mod_loaded(c, k)[0], 16)

            w_fnet = view(t["w_fnet_out"], KT)

            def fnet_panel(m):
                panel(FNET + m, m % RAW, w_fnet[:, :, m * P:(m + 1) * P], KT, first=m < RAW)

            sp.dma_start(early[:, 0:EARLY], t["columns"][:, 0:EARLY]).then_inc(early_loaded, 16)
            sp.dma_start(raw[:, 0:2, :].rearrange("p s n -> p (s n)").rearrange("p (k n) -> p k n", k=TT),
                         view(t["dft_tokens"], TT)).then_inc(dft_loaded, 16)
            for a in range(TT):
                sp.dma_start(x_tok[:, a, :], t["x"][a * P:(a + 1) * P, :]).then_inc(x_loaded[a], 16)
            mod_chunk(0)
            mod_chunk(1)
            sp.dma_start(raw[:, 2, :].rearrange("p (k n) -> p k n", k=2), view(t["dft_features"], 2)).then_inc(dftd_loaded, 16)
            sp.wait_ge(dft_split, 2)
            fnet_panel(0)
            fnet_panel(1)
            mod_chunk(2)
            sp.dma_start(cols[:, :], t["columns"][:, EARLY:]).then_inc(cols_loaded, 16)
            sp.dma_start(dec, t["decays"]).then_inc(dec_loaded, 16)
            sp.wait_ge(mod_step, KT + KT // 2)
            sp.dma_start(res[:, :, :], view(t["x_t"], KT)).then_inc(xt_loaded, 16)
            sp.wait_ge(dft_split, 3)
            fnet_panel(2)
            fnet_panel(3)
            mod_chunk(3, range(0, KT // 2, MOD_STEPS))
            fnet_panel(4)
            mod_chunk(3, range(KT // 2, KT, MOD_STEPS))
            fnet_panel(5)
            fnet_panel(6)
            mod_chunk(4)
            fnet_panel(7)
            sp.dma_start(rope[:, :, :], t["rope"].rearrange("s p n -> p s n")).then_inc(rope_loaded, 16)

            def up_panels(f, j, u):
                base = UP[f] + PAIR * j
                slot = (UP[f] + PAIR * u) % RAW
                if f == 0:
                    g, v = w_up[:, :, ds(j * P, P)], w_up[:, :, ds(j * P + FF, P)]
                else:
                    g, v = (view(t[n], KT)[:, :, ds(j * P, P)] for n in ("w_ff_gate_2", "w_ff_up_2"))
                panel(base, slot, g, KT)
                panel(base + 1, (slot + 1) % RAW, v, KT)

            def ffn_panels(f, w_down, peel=0):
                for j in range(peel):
                    up_panels(f, j, j % 2)
                if peel:
                    mod_chunk(5)
                with sp.Fori(peel // 2, FT // 2) as i:
                    for u in range(2):
                        up_panels(f, i * 2 + u, u)
                w_dn = view(w_down, FT)
                for q in range(2):
                    for k in range(DOWN):
                        p = DN[f] + q * DOWN + k
                        panel(p, p % RAW, w_dn[:, 2 * k:2 * k + 2, q * QUAD * P:(q + 1) * QUAD * P], 2)

            ffn_panels(0, t["w_ffn_down"], peel=2)

            with sp.Fori(0, KT // 4) as i:
                for u in range(12):
                    j = i * 4 + u // 3
                    panel(i * 12 + MIX + u, (MIX + u) % RAW, w_in[:, :, ds(j * P + (XC, GB, GC)[u % 3], P)], KT)
            with sp.Fori(0, 2 * KT // 4) as i:
                for u in range(4):
                    panel(i * 4 + GATE + u, (GATE + u) % RAW, w_in[:, :, ds(i * 4 * P + GA + u * P, P)], KT)

            def rel_table(h):
                if isinstance(h, int):
                    assert h == 0
                else:
                    sp.wait_ge(s_decayed, h * TT)
                sp.dma_start(decay[:, :], t["relative"]).then_inc(rel_loaded, 16)

            def head_projections(h, base, b0):
                for u in range(2 * QT):
                    src = w_in[:, :, ds(h * QK + (WQ, WK)[u // QT] + (u % QT) * P, P)]
                    panel(base + u, (b0 + u) % RAW, src, KT)
                for u in range(VT):
                    src = w_in[:, 2 * u:2 * u + 2, ds(h * V + WV, V)]
                    panel(base + 2 * QT + u, (b0 + u) % RAW, src, 2)

            def head_gate(h, base, b0):
                for u in range(VT):
                    panel(base + u, (b0 + u) % RAW, w_in[:, :, ds(h * V + GSW + u * P, P)], KT)

            def ret_out(h, base, b0):
                for u in range(VT):
                    if isinstance(h, int):
                        src = w_out_r[:, h, :, 2 * u * P:2 * (u + 1) * P]
                    else:
                        src = w_out_r[:, ds(h, 1), :, 2 * u * P:2 * (u + 1) * P].rearrange("p h k n -> p (h k) n")
                    panel(base + u, (b0 + u) % RAW, src, VT)

            rel_table(0)
            head_projections(0, HEAD0, HEAD0)
            w_a = view(t["w_a_out_2"], KT)
            for m in range(KT):
                p = HEAD0 + 2 * QT + VT + m
                panel(p, p % RAW, w_a[:, :, m * P:(m + 1) * P], KT)
            head_gate(0, HEAD1 - VT, HEAD1)
            with sp.Fori(1, HEADS) as h:
                base = h * HEADP + (HEAD1 - HEADP)
                rel_table(h)
                head_projections(h, base, HEAD1)
                ret_out(h - 1, base + 2 * QT + VT, HEAD1)
                head_gate(h, base + 2 * QT + 2 * VT, HEAD1)
            ret_out(HEADS - 1, ROUT, ROUT)
            w_o = view(t["w_o_2"], KT)
            for m in range(KT):
                panel(WO + m, (WO + m) % RAW, w_o[:, :, m * P:(m + 1) * P], KT)
            ffn_panels(1, t["w_ff_down_2"])
            for i in range(2):
                t_ = slice(i * HALF, (i + 1) * HALF)
                for m0, m1 in OUT_STORES:
                    if m0 < OUT_POOL:
                        sp.wait_ge(out_made[i], m1)
                    else:
                        sp.wait_ge(out_made_pool[i], m1 - OUT_POOL)
                    sp.dma_start(out[m0 * P:m1 * P, t_].rearrange("(k p) n -> p k n", p=P), gates[:, m0:m1, t_]).then_inc(out_stored, 16)
            sp.wait_ge(out_stored, 16 * 2 * len(OUT_STORES))

        @block.gpsimd
        def _(pool):
            nc.gpsimd.memset(ones[:, :], 1.0).then_inc(consts_set, 1)
            nc.gpsimd.memset(zero[:, :], 0.0).then_inc(consts_set, 1)
            nc.gpsimd.memset(eps[:, :], EPS).then_inc(consts_set, 1)
            nc.gpsimd.memset(eps_squared[:, :], EPS * EPS).then_inc(consts_set, 1)
            nc.gpsimd.memset(eps_ones[:, :], EPS).then_inc(consts_set, 1)
            pool.wait_ge(consts_set, 5)
            for n, (slots, s0) in enumerate((((0, 1), S_DFT), ((1, 2), S_DFT + 2), ((2, 3), S_DFTD))):
                src = raw[:, slots[0], :]
                dst_hi, dst_lo = (w[:, s0:s0 + 2, :].rearrange("p s t -> p (s t)") for w in (wide_hi, wide_lo))
                if n != 1:
                    pool.wait_ge(dft_loaded if n == 0 else dftd_loaded, 16)
                nc.gpsimd.tensor_scalar(dst_hi, src, 1.0, 0.0, MUL, ADD).then_inc(dft_hi_made, 1)
                pool.wait_ge(dft_hi_made, n + 1)
                nc.gpsimd.tensor_tensor(dst_lo, src, f32(dst_hi), SUB).then_inc(dft_split, 1)

            def split(p, slot, two, loads, first=False):
                pool.wait_ge(raw_loaded[slot], loads)
                if not first:
                    pool.wait_ge(panel_used, p - SPLIT + 1)
                nc.gpsimd.tensor_tensor(w_hi[:, two, 0:1], raw[:, slot, 0:1], zero[:, :], ADD)
                nc.gpsimd.tensor_scalar(w_hi[:, two, 1:], raw[:, slot, 1:], 1.0, 0.0, MUL, ADD).then_inc(hi_made, 1)
                pool.wait_ge(hi_made, p + 1)
                nc.gpsimd.tensor_tensor(w_lo[:, two, :], raw[:, slot, :], f32(w_hi[:, two, :]), SUB).then_inc(split_done, 1)

            for p in range(RAW):
                split(p, p, p % SPLIT, 16, first=p < SPLIT)
                if p == SPLIT - 1:
                    for m in range(KT):
                        pool.wait_ge(f_hi_made, m + 1)
                        nc.gpsimd.tensor_tensor(act_lo[:, m, :], tmp[:, 1 + 2 * (m % 2), :], f32(act_hi[:, m, :]), SUB
                                                ).then_inc(f_ready, 1)
            with pool.Fori(1, PANELS // RAW) as i:
                for u in range(RAW):
                    split(i * RAW + u, u, u % SPLIT, i * 16 + 16)
            for i in range(2):
                t_ = slice(i * HALF, (i + 1) * HALF)
                for m in range(OUT_POOL, KT):
                    pool.wait_ge(out_gained[i], m + 1)
                    pool.wait_ge(norm_rstd[3], i + 1)
                    nc.gpsimd.tensor_tensor(gates[:, m, t_], gates[:, m, t_], tmp[:, 2, t_], MUL).then_inc(out_made_pool[i], 1)

        @block.tensor
        def _(pe):
            mm = nc.tensor.matmul

            def product(o, w, wl, a, al, start, stop, opens=False):
                ins = mm(o, w, a, start=start, stop=False)
                if opens:
                    ins.then_inc(panel_used, 1)
                mm(o, wl, a, start=False, stop=False)
                return mm(o, w, al, start=False, stop=stop)

            def w_block(two, b, n=P):
                return w_hi[:, two, b * n:(b + 1) * n], w_lo[:, two, b * n:(b + 1) * n]

            def tile(o, p, two, a_hi, a_lo, ready=None, k=KT, part=0, parts=1, again=False, between=None):
                if part == 0:
                    pe.wait_ge(split_done, p + 1)
                for b in range(k):
                    if ready:
                        pe.wait_ge(ready[0], ready[1] + b + 1)
                    ins = product(o, *w_block(two, parts * b + part), a_hi[:, b, :], a_lo[:, b, :], b == 0, b == k - 1,
                                  opens=not (isinstance(p, int) and p == 0) and part == 0 and b == 0 and not again)
                    if between and b == k - 3:
                        between()
                return ins

            def dft_tokens(tiles):
                for k in range(TT):
                    if tiles[0] == 0:
                        pe.wait_ge(xr_made, k + 1)
                    for m in tiles:
                        ins = product(ps[:, m % 7, :], xr_hi[:, k, m * P:(m + 1) * P], xr_lo[:, k, m * P:(m + 1) * P],
                                      wide_hi[:, S_DFT + k, :], wide_lo[:, S_DFT + k, :], k == 0, k == TT - 1)
                        if k == TT - 1:
                            ins.then_inc(u_done, 1)

            def mod_sums(c, bank=7):
                pe.wait_ge(mod_step, KT * (c + 1))
                if c in (2, 3):
                    pe.wait_ge(mod_read, c - 1)
                for u in range(KT):
                    ins = mm(ps[:, bank, c * KT + u:c * KT + u + 1], mod_acc(c)[:, u * P:(u + 1) * P], ones[:, 0:1],
                             start=True, stop=True)
                ins.then_inc(mod_summed, 1)

            pe.wait_ge(dft_split, 2)
            pe.wait_ge(consts_set, 5)
            dft_tokens(range(4))
            dft_tokens([4])
            dft_tokens([5])
            dft_tokens([6])
            mod_sums(0)
            pe.wait_ge(u0_copied, 1)
            dft_tokens([7])
            mod_sums(1)

            pe.wait_ge(udc_made, 1)
            pe.wait_ge(dft_split, 3)
            half = T // 2
            for m in range(KT):
                if m < 3:
                    pe.wait_ge(u_made, 2 * m + 3)
                else:
                    pe.wait_ge(f_made, 3 * (m - 2))
                pe.wait_ge(u_made, m // 2 * 2 + 2)
                g, e = m // 2, m % 2
                for part, (c0, n) in enumerate(((0, half + 2), (half, half))):
                    for k in range(2):
                        sl = slice(part * GROUP + e * P, part * GROUP + (e + 1) * P)
                        ins = product(ps[:, 1 + 2 * (m % 3) + part, 0:n], wide_hi[:, S_DFTD + k, sl], wide_lo[:, S_DFTD + k, sl],
                                      wide_hi[:, S_U + 2 * g + k, c0:c0 + n], wide_lo[:, S_U + 2 * g + k, c0:c0 + n],
                                      k == 0, k == 1)
                ins.then_inc(f_done, 1)

            for m in range(KT - 1):
                if m == 1:
                    pe.wait_ge(f_made, 3 * KT)
                tile(ps[:, m, :], FNET + m, m % 2, act_hi, act_lo, (f_ready, 0) if m == 0 else None).then_inc(fnet_done, 1)
                if m in MOD_AFTER:
                    mod_sums(MOD_AFTER[m])
            pe.wait_ge(fnet_free, 2)
            halves = [slice(i * HALF, (i + 1) * HALF) for i in range(2)]
            m = KT - 1

            def last_squares(i):
                pe.wait_ge(res_squared[0], KT + i)
                mm(ps[:, 4 + i, halves[i]], ones[:, :], tmp[:, 1, halves[i]], start=False, stop=True).then_inc(norm_summed[0], 1)

            tile(ps[:, 0, halves[0]], FNET + m, m % 2, act_hi[:, :, halves[0]], act_lo[:, :, halves[0]]).then_inc(fnet_done, 1)
            pe.wait_ge(squares_added[0], KT - 2)
            for i, t_ in enumerate(halves):
                mm(ps[:, 4 + i, t_], ones[:, :], tmp[:, 0, t_], start=True, stop=False)
            tile(ps[:, 1, halves[1]], FNET + m, m % 2, act_hi[:, :, halves[1]], act_lo[:, :, halves[1]], again=True,
                 between=lambda: last_squares(0)).then_inc(fnet_done, 1)
            last_squares(1)

            def norm(n, banks, tokens=slice(0, T)):
                pe.wait_ge(squares_added[n], KT - 1)
                if len(banks) == 2:
                    mm(ps[:, banks[1], tokens], ones[:, :], tmp[:, 1, tokens], start=True, stop=False)
                    mm(ps[:, banks[1], tokens], eps_ones[:, :], tmp[:, 0, tokens], start=False, stop=True)
                mm(ps[:, banks[0], tokens], ones[:, :], tmp[:, 0, tokens], start=True, stop=True).then_inc(norm_summed[n], 1)

            def ffn_up(f):
                def pair(j, u):
                    if not isinstance(j, int):
                        pe.wait_ge(prod_made[f], j - 1)
                    for s in range(PAIR):
                        tile(ps[:, 2 * u + s, :], j * PAIR + UP[f] + s, s, act_hi, act_lo,
                             (act_ready[2], 0) if f == 1 and isinstance(j, int) and j + s == 0 else None).then_inc(up_done[f], 1)
                        if f == 1 and isinstance(j, int) and j + s == 0:
                            norm(2, [4])

                if f == 0:
                    for i, t_ in enumerate(halves):
                        for s in range(PAIR):
                            ins = tile(ps[:, s, t_], UP[0] + s, s, act_hi[:, :, t_], act_lo[:, :, t_],
                                       (act_ready[0], i * KT) if s == 0 else None, again=s != i)
                            if i:
                                ins.then_inc(up_done[0], 1)
                else:
                    pair(0, 0)
                pair(1, 1)
                with pe.Fori(1, FT // 2) as i:
                    for u in range(2):
                        pair(i * 2 + u, u)

            def down_panel(f, q, k, two, p, order, start=False, stop=False, a0=None):
                pe.wait_ge(split_done, p + 1)
                if q == 0:
                    pe.wait_ge(wide_ready[f], k * 2 + 2)
                for n, (o, c) in enumerate(order):
                    a_hi, a_lo = (w[:, k * 2 + c, :] for w in (wide_hi, wide_lo))
                    ins = product(ps[:, QUAD * (1 - q) + o, :], *w_block(two, c * QUAD + o), a_hi, a_lo, start and c == 0, stop and c == 1,
                                  opens=n == 0)
                    if stop and c == 1:
                        ins.then_inc(dn_done[f], 1)

            def down_end(p0):
                pe.wait_ge(dn_free[1], QUAD)
                pe.wait_ge(split_done, p0 + 1)
                tiles = range(QUAD)
                order = ([(0, 0, o) for o in tiles] + [(1, 0, o) for o in tiles[:2]] + [(0, 1, o) for o in tiles] +
                         [(1, 0, o) for o in tiles[2:]] + [(1, 1, o) for o in tiles])
                for i, last, o in order:
                    t_ = halves[i]
                    if (i, last, o) == (0, 1, 0):
                        pe.wait_ge(split_done, p0 + 2)
                    for c in range(2):
                        k = 2 * (DOWN - 2 + last) + c
                        ins = product(ps[:, QUAD * i + o, t_], *w_block((p0 + last) % 2, c * QUAD + o),
                                      wide_hi[:, k, t_], wide_lo[:, k, t_], i == 1 and last == 0 and c == 0, last == 1 and c == 1,
                                      opens=i == 0 and o == 0 and c == 0)
                    if last:
                        ins.then_inc(dn_done[1], 1)
                    if (i, last, o) == (1, 1, 1):
                        pe.wait_ge(dn_free[1], KT)
                        norm(3, [0], halves[0])
                pe.wait_ge(squares_added[3], KT - 1 + 2)
                mm(ps[:, 1, halves[1]], ones[:, :], tmp[:, 0, halves[1]], start=True, stop=False)
                pe.wait_ge(res_squared[3], KT + 3)
                mm(ps[:, 1, halves[1]], ones[:, :], tmp[:, 3, halves[1]], start=False, stop=False)
                pe.wait_ge(res_squared[3], KT + 4)
                mm(ps[:, 1, halves[1]], ones[:, :], tmp[:, 1, halves[1]], start=False, stop=True).then_inc(norm_summed[3], 1)

            def ffn_down(f):
                by_c = [(o, c) for c in range(2) for o in range(QUAD)]
                by_o = [(o, c) for o in range(QUAD) for c in range(2)]
                for q in range(2):
                    p = DN[f] + q * DOWN
                    if q == 1:
                        pe.wait_ge(prod_made[f], FT)
                        if f == 0:
                            pe.wait_ge(mod_read, 4)
                    down_panel(f, q, 0, p % 2, p, by_c, start=True)
                    with pe.Fori(0, (DOWN - 3) // 2) as i:
                        for u in range(2):
                            down_panel(f, q, i * 2 + u + 1, (p + 1 + u) % 2, i * 2 + p + 1 + u, by_c)
                    if f == 1 and q == 1:
                        down_end(p + DOWN - 2)
                        continue
                    if f == 0 and q == 0:
                        pe.wait_ge(prod_made[0], FT)
                        mod_sums(5, 0)
                    down_panel(f, q, DOWN - 2, (p + DOWN - 2) % 2, p + DOWN - 2, by_c)
                    down_panel(f, q, DOWN - 1, (p + DOWN - 1) % 2, p + DOWN - 1, by_o, stop=True)

            ffn_up(0)
            ffn_down(0)

            def conv_tiles(j, u, first=False):
                if not first:
                    pe.wait_ge(mix_free, j - 1)
                for s in range(3):
                    tile(ps[:, (4 + 3 * u + s) % 8, :], j * 3 + MIX + s, (u + s) % 2, act_hi, act_lo,
                         (act_ready[1], 0) if first and u + s == 0 else None).then_inc(mix_done, 1)
                    if first and u == 0 and s == 1:
                        norm(1, [2, 3])

            pe.wait_ge(dn_free[0], QUAD)
            for j in range(2):
                conv_tiles(j, j, first=True)
            with pe.Fori(1, KT // 2) as i:
                for u in range(2):
                    conv_tiles(i * 2 + u, u)

            pe.wait_ge(mix_free, KT - 1)
            for g in range(4):
                tile(ps[:, 2 + g, :], GATE + g, g % 2, act_hi, act_lo).then_inc(gate_done, 1)
            with pe.Fori(1, 2 * KT // 4) as i:
                for u in range(4):
                    pe.wait_ge(gate_scaled, i * 4 + u - 3)
                    tile(ps[:, 2 + u, :], i * 4 + GATE + u, u % 2, act_hi, act_lo).then_inc(gate_done, 1)
            pe.wait_ge(mix_free, KT)

            for a in range(TT):
                ins = mm(ps[:, 7, a:a + 1], tmp[:, 4, a * P:(a + 1) * P], ones[:, 0:1], start=True, stop=True)
            ins.then_inc(keys_done, 1)

            def head_projections(h, base):
                for u in range(2 * QT):
                    if isinstance(h, int):
                        if u == 2:
                            pe.wait_ge(gate_scaled, 2 * KT)
                    elif u == 0:
                        pe.wait_ge(gsw_scaled, h * VT - 1)
                        pe.wait_ge(o_std, h)
                    elif u == 1:
                        pe.wait_ge(gsw_scaled, h * VT)
                    elif u == 2 * QT - 1:
                        pe.wait_ge(ret_made, h * VT)
                    tile(ps[:, u, :], base + u, u % 2, act_hi, act_lo).then_inc(qk_done, 1)
                if isinstance(h, int):
                    pe.wait_ge(key_scale_made, 1)
                for u in range(VT):
                    p = base + 2 * QT + u
                    pe.wait_ge(split_done, p + 1)
                    order = [(a, c) for c in range(2) for a in range(TT)] if u < VT - 1 else [(a, c) for a in range(TT) for c in range(2)]
                    for n, (a, c) in enumerate(order):
                        k = 2 * u + c
                        wh, wl = w_block(u % 2, c, V)
                        sl = slice(a * P, (a + 1) * P)
                        ins = product(ps[:, 4 + a, :], act_hi[:, k, sl], act_lo[:, k, sl], wh, wl, k == 0, k == KT - 1, opens=n == 0)
                        if u == VT - 1 and c == 1:
                            ins.then_inc(v_done, 1)

            def scores(h):
                pe.wait_ge(rot_ready, h * 2 * QT + 2 * QT)
                for a in range(TT):
                    sl = slice(a * P, (a + 1) * P)
                    for k in range(QT):
                        ins = product(ps[:, a, :], wide_hi[:, S_K + k, sl], wide_lo[:, S_K + k, sl],
                                      wide_hi[:, S_Q + k, :], wide_lo[:, S_Q + k, :], k == 0, k == QT - 1)
                    ins.then_inc(s_done, 1)

            def attend(h):
                pe.wait_ge(v_ready, h * TT + TT)
                for e in range(VT):
                    sl = slice(e * P, (e + 1) * P)
                    for k in range(TT):
                        if e == 0:
                            pe.wait_ge(s_ready, h * TT + k + 1)
                        ins = product(ps[:, 4 + e, :], wide_hi[:, S_V + k, sl], wide_lo[:, S_V + k, sl],
                                      wide_hi[:, S_S + k, :], wide_lo[:, S_S + k, :], k == 0, k == TT - 1)
                    ins.then_inc(o_done, 1)

            def head_gate(h, base):
                pe.wait_ge(mid_free, h * KT + KT)
                for e in range(VT):
                    if e >= 2:
                        pe.wait_ge(gsw_scaled, h * VT + e - 1)
                    tile(ps[:, e % 2, :], base + e, e % 2, act_hi, act_lo).then_inc(gsw_done, 1)
                    if e == 0:
                        pe.wait_ge(o_added, h * (VT - 1) + VT - 1)
                        mm(ps[:, 2, :], ones[:, :], tmp[:, 5, :], start=True, stop=True).then_inc(o_summed, 1)

            def ret_out(h, base, last=False):
                ret_hi, ret_lo = (w[:, S_RET:S_RET + VT, :] for w in (wide_hi, wide_lo))
                if last:
                    pe.wait_ge(gsw_scaled, HEADS * VT)
                    pe.wait_ge(o_std, HEADS)
                    pe.wait_ge(split_done, base + 1)
                    for m, k in [(m, k) for ks in (range(VT - 1), [VT - 1]) for m in range(2) for k in ks]:
                        pe.wait_ge(ret_ready, h * VT + k + 1)
                        ins = product(ps[:, m, :], *w_block(base % 2, 2 * k + m), ret_hi[:, k, :], ret_lo[:, k, :],
                                      k == 0, k == VT - 1, opens=m == 0 and k == 0)
                        if k == VT - 1:
                            ins.then_inc(mid_done, 1)
                for m in range(2 if last else 0, KT):
                    if m >= 4:
                        pe.wait_ge(mid_free, (h + 1) * KT + m - 3)
                    elif not last:
                        pe.wait_ge(s_decayed, h * TT + TT + m + 1)
                    tile(ps[:, m % 4, :], base + m // 2, (m // 2) % 2, ret_hi, ret_lo, (ret_ready, h * VT) if m == 0 else None,
                         k=VT, part=m % 2, parts=2).then_inc(mid_done, 1)

            head_projections(0, HEAD0)
            scores(0)
            for m in range(KT):
                if m < 4:
                    pe.wait_ge(s_decayed, m + 1)
                else:
                    pe.wait_ge(mid_free, m - 3)
                tile(ps[:, m % 4, :], HEAD0 + 2 * QT + VT + m, m % 2, wide_hi[:, S_CONV:S_CONV + KT, :],
                     wide_lo[:, S_CONV:S_CONV + KT, :], (mix_ready, 0) if m == 0 else None).then_inc(mid_done, 1)
            attend(0)
            head_gate(0, HEAD1 - VT)
            with pe.Fori(1, HEADS) as h:
                base = h * HEADP + (HEAD1 - HEADP)
                head_projections(h, base)
                scores(h)
                ret_out(h - 1, base + 2 * QT + VT)
                attend(h)
                head_gate(h, base + 2 * QT + 2 * VT)
            ret_out(HEADS - 1, ROUT, last=True)

            for m in range(KT):
                if m >= 4:
                    pe.wait_ge(wo_free, m - 3)
                tile(ps[:, 4 + m % 4, :], WO + m, m % 2, wide_hi[:, S_MERGE:S_MERGE + KT, :], wide_lo[:, S_MERGE:S_MERGE + KT, :],
                     (merge_ready, 0) if m == 0 else None).then_inc(wo_done, 1)
            ffn_up(1)
            ffn_down(1)

        @block.scalar
        def _(act):
            do = nc.scalar.activation

            def hi_of(dst, src, made, **how):
                do(dst, src, ACT.Identity, **how).then_inc(made, 1)

            act.wait_ge(early_loaded, 16)
            do(silu_c, early_cols("c", 0, KT), ACT.Silu).then_inc(silu_c_made, 1)
            act.wait_ge(consts_set, 5)
            do(small[:, 6, 0:1], eps[:, :], ACT.Sqrt)
            def x_squares(a):
                act.wait_ge(x_loaded[a], 16)
                if a:
                    act.wait_ge(x_squared, a)
                do(tmp[:, 0:2, :].rearrange("p s t -> p (s t)"), x_tok[:, a, :], ACT.Square,
                   accum_out=small[:, 0, a:a + 1]).then_inc(x_squared, 1)
                act.wait_ge(x_squared, a + 1)
                do(small[:, 1, a:a + 1], small[:, 0, a:a + 1], ACT.Sqrt, scale=1.0 / D, bias=eps[:, :]).then_inc(x_std, 1)

            def x_hi(a):
                act.wait_ge(x_rstd, a + 1)
                hi_of(xr_hi[:, a, :], x_tok[:, a, :], xr_hi_made, scale=small[:, 2, a:a + 1])

            x_squares(0)
            x_hi(0)
            x_squares(1)
            x_squares(2)
            x_hi(1)
            x_squares(3)
            x_hi(2)
            x_hi(3)
            act.wait_ge(u_done, 1)
            do(tmp[:, 0, :], ps[:, 0, :], ACT.Identity).then_inc(u0_copied, 1)
            act.wait_ge(u_scale_made, 1)
            for m in range(KT):
                if m == 2:
                    act.wait_ge(u_scale_made, 3)
                    do(wide_hi[:, S_U:S_U + KT, 0:1], udc.rearrange("p (k o) -> p k o", o=1), ACT.Identity).then_inc(udc_hi_made, 1)
                hi_of(wide_hi[:, S_U + m, 1:T], u_tile(m)[:, 1:T], u_hi_made, scale=gain_mix[:, m:m + 1])
            def f_hi(m):
                act.wait_ge(f_made, 3 * (m + 1))
                hi_of(act_hi[:, m, :], tmp[:, 1 + 2 * (m % 2), :], f_hi_made)

            for m in range(KT):
                act.wait_ge(f_done, m + 1)
                if m >= 2:
                    act.wait_ge(f_made, 3 * (m - 1))
                do(tmp[:, 2 * (m % 2), 0:T // 2], ps[:, 2 + 2 * (m % 3), 0:T // 2], ACT.Identity).then_inc(f_q_copied, 1)
                if m:
                    f_hi(m - 1)
            f_hi(KT - 1)
            act.wait_ge(dec_loaded, 16)
            do(lgt[:, 0, :], dec, ACT.Abs).then_inc(act_chain, 1)
            act.wait_ge(act_chain, 1)
            do(lgt[:, 1, :], lgt[:, 0, :], ACT.Exp, scale=-1.0).then_inc(lg_exp, 1)

            def load_sqrt():
                do(small[:, 6, 0:1], eps[:, :], ACT.Sqrt)

            halves = [slice(i * HALF, (i + 1) * HALF) for i in range(2)]

            def square(n, m, tokens=slice(0, T)):
                if m >= 2:
                    act.wait_ge(squares_added[n], m - 1)
                do(tmp[:, 0 if m == 0 else 1, tokens], res[:, m, tokens], ACT.Square).then_inc(res_squared[n], 1)

            def square_both(m):
                if m >= 3:
                    act.wait_ge(squares_added[1], m - 2)
                s = 0 if m == 0 else 2 if m % 2 else 5
                do(tmp[:, s + 1, :], res[:, m, :], ACT.Square, scale=col("g_final", m))
                do(tmp[:, s, :], res[:, m, :], ACT.Square).then_inc(res_squared[1], 1)

            def gained_hi(n, m, gain):
                hi_of(act_hi[:, m, :], res[:, m, :], norm_hi_made[n], scale=gain)

            def std(n, dst, bank, tokens=slice(0, T), count=1):
                act.wait_ge(norm_summed[n], count)
                do(dst[:, tokens], ps[:, bank, tokens], ACT.Sqrt, scale=1.0 / D, bias=eps[:, :]).then_inc(norm_std[n], 1)

            def ffn_gate(f):
                def pair(j):
                    act.wait_ge(conv_step[f], j * 3 + 3 if f == 0 else j * 2 + 1)
                    do(tmp[:, 1, :], tmp[:, 0, :], ACT.Silu).then_inc(silu_made[f], 1)
                    act.wait_ge(prod_made[f], j + 1)
                    hi_of(wide_hi[:, j, :], tmp[:, 2, :], prod_hi_made[f])

                with act.Fori(0, FT // 2) as i:
                    for u in range(2):
                        pair(i * 2 + u)

            load_sqrt()
            for m in range(KT - 1):
                act.wait_ge(fnet_free, m + 1)
                square(0, m)
            for i, t_ in enumerate(halves):
                act.wait_ge(fnet_free, KT + i)
                square(0, KT - 1, t_)
                if i == 0:
                    std(0, tmp[:, 2, :], 4, t_, 1)
            for i, t_ in enumerate(halves):
                if i:
                    std(0, tmp[:, 2, :], 5, t_, 2)
                for k in range(KT):
                    act.wait_ge(normed, i * KT + k + 1)
                    hi_of(act_hi[:, k, t_], tmp[:, NORMED[k % 3], t_], norm_hi_made[0], bias=mod[:, 3 * KT + k:3 * KT + k + 1])
            ffn_gate(0)

            load_sqrt()
            for m in range(KT):
                act.wait_ge(dn_free[0], m + 1)
                gained_hi(1, m, gain_12[:, m:m + 1])
                if m < QUAD:
                    square_both(m)
            for m in range(QUAD, KT):
                square_both(m)
            act.wait_ge(norm_summed[1], 1)
            do(tmp[:, 4, :], ps[:, 3, :], ACT.Sqrt, scale=1.0 / D, bias=eps_squared[:, :]).then_inc(norm_std[1], 1)
            std(1, tmp[:, 6, :], 2)

            with act.Fori(0, KT // 2) as i:
                for u in range(2):
                    j = i * 2 + u
                    act.wait_ge(mix_free, j + 1)
                    hi_of(wide_hi[:, j + S_CONV, :], tmp[:, 3, :], mix_hi_made)
            with act.Fori(0, 2 * KT // 4) as i:
                for u in range(4):
                    act.wait_ge(gate_scaled, i * 4 + u + 1)
                    do(gates[:, i * 4 + u, :], tmp[:, u, :], ACT.Sigmoid).then_inc(gate_free, 1)

            def head(h):
                act.wait_ge(decay_args, h + 1)
                do(decay[:, :], decay[:, :], ACT.Exp).then_inc(decay_made, 1)
                for u in range(2 * QT):
                    act.wait_ge(rot_made, h * 2 * QT + u + 1)
                    hi_of(wide_hi[:, S_Q + u, :], tmp[:, 2 + u % 2, :], rot_hi_made)
                for a in range(TT):
                    act.wait_ge(v_done, h * TT + a + 1)
                    do(ps[:, 4 + a, :], ps[:, 4 + a, :], ACT.Identity, accum_out=small[:, 6, a:a + 1]).then_inc(v_summed, 1)
                act.wait_ge(v_summed, h * TT + TT)
                do(small[:, 7, :], small[:, 6, :], ACT.Identity, scale=-1.0 / V).then_inc(v_mean, 1)
                act.wait_ge(v_mean, h + 1)
                for a in range(TT):
                    hi_of(wide_hi[:, S_V + a, :], ps[:, 4 + a, :], v_hi_made, bias=small[:, 7, a:a + 1])
                for a in range(TT):
                    act.wait_ge(s_decayed, h * TT + a + 1)
                    hi_of(wide_hi[:, S_S + a, :], tmp[:, a % 2, :], s_hi_made)
                for e in range(VT):
                    act.wait_ge(o_done, h * VT + e + 1)
                    if e >= 2:
                        act.wait_ge(o_added, h * (VT - 1) + e - 1)
                    do(tmp[:, 5 if e == 0 else 6, :], ps[:, 4 + e, :], ACT.Square).then_inc(o_squared, 1)

                def gate(e):
                    act.wait_ge(gsw_scaled, h * VT + e + 1)
                    do(tmp[:, e, :], tmp[:, e, :], ACT.Silu).then_inc(gsw_silu, 1)

                def ret_hi(e):
                    act.wait_ge(ret_made, h * VT + e + 1)
                    hi_of(wide_hi[:, S_RET + e, :], tmp[:, e, :], ret_hi_made)

                gate(0)
                act.wait_ge(o_summed, h + 1)
                do(tmp[:, 6, :], ps[:, 2, :], ACT.Sqrt, scale=1.0 / V, bias=eps[:, :]).then_inc(o_std, 1)
                gate(1)
                gate(2)
                ret_hi(0)
                ret_hi(1)
                ret_hi(2)
                gate(3)
                ret_hi(3)

            head(0)
            with act.Fori(1, HEADS) as h:
                head(h)
            for m in range(KT):
                act.wait_ge(mid_added, (HEADS - 1) * KT + m + 1)
                hi_of(wide_hi[:, S_MERGE + m, :], gates[:, m, :], merge_hi_made)
            load_sqrt()
            for m in range(KT):
                act.wait_ge(wo_free, m + 1)
                gained_hi(2, m, col("g_ffn_2", m))
                square(2, m)
            std(2, tmp[:, 4, :], 4)
            ffn_gate(1)

            load_sqrt()

            def out_gain(m, i):
                do(gates[:, m, halves[i]], res[:, m, halves[i]], ACT.Identity, scale=col("g_final_2", m)).then_inc(out_gained[i], 1)

            def last_square(n, m, tokens):
                if n >= 3:
                    act.wait_ge(squares_added[3], n - 2)
                do(tmp[:, 0 if n == 0 else 1 if n % 2 else 3, tokens], res[:, m, tokens], ACT.Square).then_inc(res_squared[3], 1)

            for m in range(KT):
                act.wait_ge(dn_free[1], m + 1)
                if m < QUAD:
                    last_square(m, m, slice(0, T))
                    out_gain(m, 0)
                    out_gain(m, 1)
                else:
                    last_square(m, m, halves[0])
            for m in range(QUAD, KT):
                act.wait_ge(dn_free[1], m + QUAD + 1)
                last_square(m + QUAD, m, halves[1])
                if m == QUAD + 1:
                    std(3, tmp[:, 2, :], 0, halves[0], 1)
                if m < KT - 1:
                    out_gain(m, 0)
            out_gain(KT - 1, 0)
            std(3, tmp[:, 2, :], 1, halves[1], 2)
            for m in range(QUAD, KT):
                out_gain(m, 1)

        @block.vector
        def _(dve):
            tt, ts, stt = nc.vector.tensor_tensor, nc.vector.tensor_scalar, nc.vector.scalar_tensor_tensor
            links = [0]

            def link(ins):
                links[0] += 1
                ins.then_inc(chain, 1)
                dve.wait_ge(chain, links[0])

            def lo_of(dst, src, hi, made, ready, n):
                dve.wait_ge(made, n)
                tt(dst, src, f32(hi), SUB).then_inc(ready, 1)

            def x_rstds(a):
                dve.wait_ge(x_std, a + 1)
                nc.vector.reciprocal(small[:, 2, a:a + 1], small[:, 1, a:a + 1]).then_inc(x_rstd, 1)

            def x_lo(a):
                dve.wait_ge(x_rstd, a + 1)
                dve.wait_ge(xr_hi_made, a + 1)
                stt(out=xr_lo[:, a, :], in0=x_tok[:, a, :], scalar=small[:, 2, a:a + 1], in1=f32(xr_hi[:, a, :]),
                    op0=MUL, op1=SUB).then_inc(xr_made, 1)

            x_rstds(0)
            x_lo(0)
            x_rstds(1)
            x_rstds(2)
            x_lo(1)
            x_rstds(3)
            x_lo(2)
            x_lo(3)

            def mod_chunk(c):
                if c == 2:
                    dve.wait_ge(mod_summed, 1)
                acc = mod_acc(c)
                for k in range(KT):
                    w = mod_weights(c, k)[:, 0, 0:D]
                    if k % MOD_STEPS == 0:
                        dve.wait_ge(*mod_loaded(c, k))
                    if k == 0:
                        ts(acc, w, silu_c[:, 0:1], None, MUL).then_inc(mod_step, 1)
                    else:
                        dve.wait_ge(mod_step, KT * c + k)
                        stt(out=acc, in0=w, scalar=silu_c[:, k:k + 1], in1=acc, op0=MUL, op1=ADD).then_inc(mod_step, 1)

            def mod_columns(c0, c1, bank=7):
                s = slice(c0 * KT, c1 * KT)
                b = early_cols("b_mod", c0 * KT, (c1 - c0) * KT)
                dve.wait_ge(mod_summed, c1)
                tt(mod[:, s], ps[:, bank, s], b, ADD).then_inc(mod_read, 1)
                dve.wait_ge(mod_read, {2: 1, 3: 2, 5: 3, 6: 4}[c1])

            dve.wait_ge(silu_c_made, 1)
            mod_chunk(0)
            mod_chunk(1)
            dve.wait_ge(u_done, KT)
            dve.wait_ge(u0_copied, 1)
            nc.vector.tensor_copy(udc[:, 0:1], tmp[:, 0, 0:1])
            nc.vector.tensor_copy(udc[:, 1:7].rearrange("p (k o) -> p k o", o=1), ps[:, 1:7, 0:1])
            link(nc.vector.tensor_copy(udc[:, 7:8], ps[:, 0, 0:1]))
            mod_columns(0, 2)
            stt(out=gain_mix, in0=mod[:, KT:2 * KT], scalar=1.0, in1=early_cols("g_norm_mix", 0, KT),
                op0=ADD, op1=MUL).then_inc(u_scale_made, 1)
            ts(shift_dc, mod[:, 0:KT], float(T), None, MUL).then_inc(u_scale_made, 1)
            dve.wait_ge(u_scale_made, 2)
            link(tt(udc, udc, gain_mix, MUL))
            tt(udc, udc, shift_dc, ADD).then_inc(u_scale_made, 1)
            for m in range(KT):
                dve.wait_ge(u_hi_made, m + 1)
                if m == 2:
                    dve.wait_ge(udc_hi_made, 1)
                    tt(wide_lo[:, S_U:S_U + KT, 0:1], udc.rearrange("p (k o) -> p k o", o=1), f32(wide_hi[:, S_U:S_U + KT, 0:1]), SUB).then_inc(udc_made, 1)
                stt(out=wide_lo[:, S_U + m, 1:T], in0=u_tile(m)[:, 1:T], scalar=gain_mix[:, m:m + 1],
                    in1=f32(wide_hi[:, S_U + m, 1:T]), op0=MUL, op1=SUB).then_inc(u_made, 1)
            half = T // 2
            for m in range(KT):
                even, odd, f = ps[:, 1 + 2 * (m % 3), :], tmp[:, 2 * (m % 2), :], tmp[:, 1 + 2 * (m % 2), :]
                if m >= 2:
                    dve.wait_ge(f_ready, m - 1)
                dve.wait_ge(f_q_copied, m + 1)
                tt(f[:, 1:half], even[:, 1:half], odd[:, 1:half], SUB).then_inc(f_made, 1)
                tt(f[:, T - 1:half:-1], even[:, 1:half], odd[:, 1:half], ADD).then_inc(f_made, 1)
                nc.vector.tensor_copy(f[:, 0:half + 1:half], even[:, 0:half + 1:half]).then_inc(f_made, 1)
            mod_chunk(2)
            dve.wait_ge(f_ready, KT)
            mod_chunk(3)
            mod_columns(2, 3)

            dve.wait_ge(cols_loaded, 16)
            link(tt(gain_12[:, :], late_cols("g_final", KT), late_cols("g_mix_2", KT), MUL))

            halves = [slice(i * HALF, (i + 1) * HALF) for i in range(2)]

            def add_squares(n, m, both=False):
                if m:
                    s = 1 if not both else 2 if m % 2 else 5
                    dve.wait_ge(res_squared[n], m + 1)
                    if both:
                        tt(tmp[:, 1, :], tmp[:, 1, :], tmp[:, s + 1, :], ADD)
                    tt(tmp[:, 0, :], tmp[:, 0, :], tmp[:, s, :], ADD).then_inc(squares_added[n], 1)
                    dve.wait_ge(squares_added[n], m)

            def gained_lo(n, m, gain):
                dve.wait_ge(norm_hi_made[n], m + 1)
                stt(out=act_lo[:, m, :], in0=res[:, m, :], scalar=gain, in1=f32(act_hi[:, m, :]), op0=MUL, op1=SUB
                    ).then_inc(act_ready[n], 1)

            def rstd(n, std, count=1, tokens=slice(0, T)):
                dve.wait_ge(norm_std[n], count)
                nc.vector.reciprocal(std[:, tokens], std[:, tokens]).then_inc(norm_rstd[n], 1)
                dve.wait_ge(norm_rstd[n], count)

            dve.wait_ge(xt_loaded, 16)
            def fnet_residual(m, bank, tokens, n):
                dve.wait_ge(fnet_done, n)
                stt(out=res[:, m, tokens], in0=ps[:, bank, tokens], scalar=mod[:, 2 * KT + m:2 * KT + m + 1],
                    in1=res[:, m, tokens], op0=MUL, op1=ADD).then_inc(fnet_free, 1)

            for m in range(KT - 1):
                fnet_residual(m, m, slice(0, T), m + 1)
                if m:
                    add_squares(0, m - 1)
                if m == 2:
                    mod_chunk(4)
            add_squares(0, KT - 2)
            mod_columns(3, 5)
            link(stt(out=gain_ffn[:, :], in0=mod[:, 4 * KT:5 * KT], scalar=1.0,
                     in1=late_cols("g_norm_ffn", KT), op0=ADD, op1=MUL))
            fnet_residual(KT - 1, 0, halves[0], KT)
            rstd(0, tmp[:, 2, :], 1, halves[0])
            fnet_residual(KT - 1, 1, halves[1], KT + 1)

            def ffn_product(f):
                def pair(j, u):
                    dve.wait_ge(up_done[f], j * 2 + 1)
                    g, value = ps[:, 2 * u, :], ps[:, 2 * u + 1, :]
                    if f == 0:
                        w = [col("w_ffn_conv", j + FT * i) for i in range(3)]
                        c = tmp[:, 0, :]
                        ts(c, g, w[1], col("b_ffn_conv", j), MUL, ADD).then_inc(conv_step[f], 1)
                        dve.wait_ge(conv_step[f], j * 3 + 1)
                        stt(out=c[:, 1:T], in0=g[:, 0:T - 1], scalar=w[0], in1=c[:, 1:T], op0=MUL, op1=ADD).then_inc(conv_step[f], 1)
                        dve.wait_ge(conv_step[f], j * 3 + 2)
                        stt(out=c[:, 0:T - 1], in0=g[:, 1:T], scalar=w[2], in1=c[:, 0:T - 1], op0=MUL, op1=ADD).then_inc(conv_step[f], 1)
                        dve.wait_ge(up_done[f], j * 2 + 2)
                    else:
                        tt(tmp[:, 0, :], g, tmp[:, 4, :], MUL).then_inc(conv_step[f], 1)
                        dve.wait_ge(up_done[f], j * 2 + 2)
                        tt(tmp[:, 3, :], value, tmp[:, 4, :], MUL).then_inc(conv_step[f], 1)
                        dve.wait_ge(conv_step[f], j * 2 + 2)
                        value = tmp[:, 3, :]
                    dve.wait_ge(silu_made[f], j + 1)
                    tt(tmp[:, 2, :], value, tmp[:, 1, :], MUL).then_inc(prod_made[f], 1)
                    hi, lo = (w[:, j, :] for w in (wide_hi, wide_lo))
                    lo_of(lo, tmp[:, 2, :], hi, prod_hi_made[f], wide_ready[f], j + 1)
                    dve.wait_ge(wide_ready[f], j + 1)

                with dve.Fori(0, FT // 2) as i:
                    for u in range(2):
                        pair(i * 2 + u, u)

            for i, t_ in enumerate(halves):
                if i:
                    rstd(0, tmp[:, 2, :], 2, t_)
                for k in range(KT + 1):
                    n = i * KT + k
                    if k < KT:
                        if n >= 3:
                            dve.wait_ge(act_ready[0], n - 2)
                        stt(out=tmp[:, NORMED[k % 3], t_], in0=res[:, k, t_], scalar=gain_ffn[:, k:k + 1], in1=tmp[:, 2, t_],
                            op0=MUL, op1=MUL).then_inc(normed, 1)
                    if k:
                        dve.wait_ge(norm_hi_made[0], n)
                        stt(out=act_lo[:, k - 1, t_], in0=tmp[:, NORMED[(k - 1) % 3], t_], scalar=mod[:, 3 * KT + k - 1:3 * KT + k],
                            in1=f32(act_hi[:, k - 1, t_]), op0=ADD, op1=SUB).then_inc(act_ready[0], 1)
            ffn_product(0)
            mod_chunk(5)
            mod_columns(5, 6, 0)

            dve.wait_ge(lg_exp, 1)
            u, s, s2, p = (lgt[:, i, :] for i in (1, 2, 3, 4))
            link(ts(s, u, 2.0, None, ADD))
            link(nc.vector.reciprocal(s2, s))
            link(tt(s, u, s2, MUL))
            link(tt(s2, s, s, MUL))
            link(ts(p, s2, 1.0 / 17, None, MUL))
            for n in (15, 13, 11, 9, 7, 5, 3):
                link(stt(out=p, in0=p, scalar=1.0 / n, in1=s2, op0=ADD, op1=MUL))
            link(stt(out=p, in0=p, scalar=1.0, in1=s, op0=ADD, op1=MUL))
            link(ts(s, dec, 0.0, None, ALU.min))
            link(stt(out=lg[:, :], in0=p, scalar=-2.0, in1=s, op0=MUL, op1=ADD))
            link(ts(lg[:, HEADS:], lg[:, HEADS:], -1.0, None, MUL))
            for m in range(KT):
                dve.wait_ge(dn_done[0], m + 1)
                stt(out=res[:, m, :], in0=ps[:, (m + QUAD) % KT, :], scalar=mod[:, 5 * KT + m:5 * KT + m + 1], in1=res[:, m, :],
                    op0=MUL, op1=ADD).then_inc(dn_free[0], 1)
                if m < QUAD:
                    gained_lo(1, m, gain_12[:, m:m + 1])
                    add_squares(1, m, both=True)
                elif m > QUAD:
                    gained_lo(1, m - 1, gain_12[:, m - 1:m])
            gained_lo(1, KT - 1, gain_12[:, KT - 1:KT])
            for m in range(QUAD, KT):
                add_squares(1, m, both=True)
            scale, scale_squared = tmp[:, 4, :], tmp[:, 5, :]
            rstd(1, scale)
            link(tt(scale_squared, scale, scale, MUL))

            with dve.Fori(0, KT // 2) as i:
                for u in range(2):
                    j = i * 2 + u
                    xc, gb, gc = (ps[:, (s + 3 * u) % 8, :] for s in (4, 5, 6))
                    w = [col("w_conv_2", j + KT * n) for n in range(3)]
                    x, g, c = tmp[:, 0, :], tmp[:, 1, :], tmp[:, 2, :]
                    dve.wait_ge(mix_done, j * 3 + 1)
                    tt(x, xc, scale_squared, MUL).then_inc(mix_step, 1)
                    dve.wait_ge(mix_step, j * 6 + 1)
                    dve.wait_ge(mix_done, j * 3 + 3)
                    tt(g, gc, x, MUL).then_inc(mix_step, 1)
                    dve.wait_ge(mix_step, j * 6 + 2)
                    ts(c, g, w[1], None, MUL).then_inc(mix_step, 1)
                    dve.wait_ge(mix_step, j * 6 + 3)
                    stt(out=c[:, 1:T], in0=g[:, 0:T - 1], scalar=w[0], in1=c[:, 1:T], op0=MUL, op1=ADD).then_inc(mix_step, 1)
                    dve.wait_ge(mix_step, j * 6 + 4)
                    stt(out=c[:, 0:T - 1], in0=g[:, 1:T], scalar=w[2], in1=c[:, 0:T - 1], op0=MUL, op1=ADD).then_inc(mix_step, 1)
                    dve.wait_ge(mix_step, j * 6 + 5)
                    tt(x, gb, c, MUL).then_inc(mix_step, 1)
                    dve.wait_ge(mix_step, j * 6 + 6)
                    tt(tmp[:, 3, :], x, scale, MUL).then_inc(mix_free, 1)
                    hi, lo = (x[:, j + S_CONV, :] for x in (wide_hi, wide_lo))
                    lo_of(lo, tmp[:, 3, :], hi, mix_hi_made, mix_ready, j + 1)
                    dve.wait_ge(mix_ready, j + 1)

            dve.wait_ge(norm_std[1], 2)
            link(nc.vector.reciprocal(tmp[:, 6, :], tmp[:, 6, :]))
            for k in range(KT):
                stt(out=res[:, k, :], in0=res[:, k, :], scalar=col("g_final", k), in1=tmp[:, 6, :], op0=MUL, op1=MUL
                    ).then_inc(res_scaled, 1)

            def gate_scale(g, u):
                dve.wait_ge(gate_done, g + 1)
                if not isinstance(g, int):
                    dve.wait_ge(gate_free, g - 3)
                tt(tmp[:, u, :], ps[:, 2 + u, :], scale, MUL).then_inc(gate_scaled, 1)

            for g in range(4):
                gate_scale(g, g)
            with dve.Fori(1, 2 * KT // 4) as i:
                for u in range(4):
                    gate_scale(i * 4 + u, u)

            def head(h):
                if not isinstance(h, int):
                    dve.wait_ge(ret_ready, h * VT)
                dve.wait_ge(rel_loaded, h * 16 + 16)
                ts(tmp_wide, decay[:, :], 0.0, lg[:, ds(h, 1)], ALU.max, MUL).then_inc(rot_step, 1)
                dve.wait_ge(rot_step, h * 10 + 1)
                ts(decay[:, :], decay[:, :], 0.0, lg[:, ds(h + HEADS, 1)], ALU.min, MUL).then_inc(rot_step, 1)
                dve.wait_ge(rot_step, h * 10 + 2)
                tt(decay[:, :], decay[:, :], tmp_wide, ADD).then_inc(decay_args, 1)
                for r in range(2):
                    a, b = ps[:, QT * r, :], ps[:, QT * r + 1, :]
                    n = h * 10 + 2 + 4 * r
                    dve.wait_ge(qk_done, h * 2 * QT + QT * (r + 1))
                    if r or not isinstance(h, int):
                        dve.wait_ge(rot_ready, h * 2 * QT + QT * r)
                    for i, (x0, x1, op) in enumerate(((0, 1, SUB), (1, 0, ADD))):
                        if i:
                            dve.wait_ge(rot_made, h * 2 * QT + QT * r + i)
                        tt(tmp[:, 0, :], a, rope[:, x0, :], MUL).then_inc(rot_step, 1)
                        tt(tmp[:, 1, :], b, rope[:, x1, :], MUL).then_inc(rot_step, 1)
                        dve.wait_ge(rot_step, n + 2 * i + 2)
                        tt(tmp[:, 2 + i, :], tmp[:, 0, :], tmp[:, 1, :], op).then_inc(rot_made, 1)
                    for i in range(QT):
                        lo_of(wide_lo[:, S_Q + QT * r + i, :], tmp[:, 2 + i, :], wide_hi[:, S_Q + QT * r + i, :],
                              rot_hi_made, rot_ready, h * 2 * QT + QT * r + i + 1)
                for a in range(TT):
                    dve.wait_ge(v_hi_made, h * TT + a + 1)
                    stt(out=wide_lo[:, S_V + a, :], in0=ps[:, 4 + a, :], scalar=small[:, 7, a:a + 1],
                        in1=f32(wide_hi[:, S_V + a, :]), op0=ADD, op1=SUB).then_inc(v_ready, 1)
                dve.wait_ge(decay_made, h + 1)
                for a in range(TT + 1):
                    if a < TT:
                        dve.wait_ge(s_done, h * TT + a + 1)
                        if a >= 2:
                            dve.wait_ge(s_ready, h * TT + a - 1)
                        c0 = (TT - 1 - a) * P
                        stt(out=tmp[:, a % 2, :], in0=ps[:, a, :], scalar=key_scale[:, a:a + 1], in1=decay[:, c0:c0 + T],
                            op0=MUL, op1=MUL).then_inc(s_decayed, 1)
                    if a:
                        lo_of(wide_lo[:, S_S + a - 1, :], tmp[:, (a - 1) % 2, :], wide_hi[:, S_S + a - 1, :],
                              s_hi_made, s_ready, h * TT + a)
                if isinstance(h, int):
                    for m in range(KT):
                        dve.wait_ge(mid_done, m + 1)
                        tt(gates[:, m, :], ps[:, m % 4, :], gates[:, m, :], MUL).then_inc(mid_free, 1)
                else:
                    merge(h - 1)
                for e in range(1, VT):
                    dve.wait_ge(o_squared, h * VT + e + 1)
                    tt(tmp[:, 5, :], tmp[:, 5, :], tmp[:, 6, :], ADD).then_inc(o_added, 1)
                    dve.wait_ge(o_added, h * (VT - 1) + e)

                def gsw(e):
                    dve.wait_ge(gsw_done, h * VT + e + 1)
                    tt(tmp[:, e, :], ps[:, e % 2, :], scale, MUL).then_inc(gsw_scaled, 1)

                def gated(e):
                    dve.wait_ge(gsw_silu, h * VT + e + 1)
                    stt(out=tmp[:, e, :], in0=ps[:, 4 + e, :], scalar=col("g_ret_2", h * VT + e), in1=tmp[:, e, :],
                        op0=MUL, op1=MUL).then_inc(o_gated, 1)

                def scaled(e):
                    dve.wait_ge(o_rstd, h + 1)
                    dve.wait_ge(o_gated, h * VT + e + 1)
                    tt(tmp[:, e, :], tmp[:, e, :], tmp[:, 6, :], MUL).then_inc(ret_made, 1)

                def ret_lo(e):
                    lo_of(wide_lo[:, S_RET + e, :], tmp[:, e, :], wide_hi[:, S_RET + e, :], ret_hi_made, ret_ready, h * VT + e + 1)

                gsw(0)
                dve.wait_ge(o_std, h + 1)
                nc.vector.reciprocal(tmp[:, 6, :], tmp[:, 6, :]).then_inc(o_rstd, 1)
                gated(0)
                gsw(1)
                gated(1)
                scaled(0)
                scaled(1)
                gsw(2)
                gated(2)
                scaled(2)
                ret_lo(0)
                ret_lo(1)
                ret_lo(2)
                gsw(3)
                gated(3)
                scaled(3)
                ret_lo(3)

            def merged_lo(m):
                lo_of(wide_lo[:, S_MERGE + m, :], gates[:, m, :], wide_hi[:, S_MERGE + m, :], merge_hi_made, merge_ready, m + 1)

            def merge(h, last=False):
                dve.wait_ge(ret_ready, h * VT + VT)
                dve.wait_ge(s_ready, h * TT + (TT if last else 2 * TT))
                for m in range(KT):
                    if m >= 2:
                        dve.wait_ge(mid_added, h * KT + m - 1)
                    dve.wait_ge(mid_done, (h + 1) * KT + m + 1)
                    tt(tmp[:, m % 2, :], ps[:, m % 4, :], gates[:, KT + m, :], MUL).then_inc(mid_free, 1)
                    dve.wait_ge(mid_free, (h + 1) * KT + m + 1)
                    tt(gates[:, m, :], gates[:, m, :], tmp[:, m % 2, :], ADD).then_inc(mid_added, 1)
                    if last and m:
                        merged_lo(m - 1)
                if last:
                    merged_lo(KT - 1)

            dve.wait_ge(rope_loaded, 16)
            dve.wait_ge(mix_ready, KT)
            dve.wait_ge(gate_free, 2 * KT)
            key_scale = small[:, 3, :]
            dve.wait_ge(keys_done, 1)
            ts(key_scale, ps[:, 7, 0:TT], QK ** -0.5 / P, None, MUL).then_inc(key_scale_made, 1)
            for s in range(2):
                ins = tt(rope[:, s, :], rope[:, s, :], scale, MUL)
            link(ins)
            head(0)
            with dve.Fori(1, HEADS) as h:
                head(h)
            merge(HEADS - 1, last=True)

            dve.wait_ge(res_scaled, KT)
            for m in range(KT):
                dve.wait_ge(wo_done, m + 1)
                tt(res[:, m, :], ps[:, 4 + m % 4, :], res[:, m, :], ADD).then_inc(wo_free, 1)
                gained_lo(2, m, col("g_ffn_2", m))
                add_squares(2, m)
            rstd(2, tmp[:, 4, :])
            ffn_product(1)

            def last_added(n, tokens):
                if n:
                    dve.wait_ge(res_squared[3], n + 1)
                    tt(tmp[:, 0, tokens], tmp[:, 0, tokens], tmp[:, 1 if n % 2 else 3, tokens], ADD).then_inc(squares_added[3], 1)
                    dve.wait_ge(squares_added[3], n)

            for m in range(KT):
                dve.wait_ge(dn_done[1], m + 1)
                tt(res[:, m, :], ps[:, (m + QUAD) % KT, :], res[:, m, :], ADD).then_inc(dn_free[1], 1)
                if m < QUAD:
                    last_added(m, slice(0, T))
                elif m > QUAD:
                    last_added(m - 1, halves[0])
            last_added(KT - 1, halves[0])

            def second_half(m):
                dve.wait_ge(dn_done[1], m + QUAD + 1)
                tt(res[:, m, halves[1]], ps[:, m, halves[1]], res[:, m, halves[1]], ADD).then_inc(dn_free[1], 1)

            def result(i):
                for m in range(OUT_POOL):
                    dve.wait_ge(out_gained[i], m + 1)
                    tt(gates[:, m, halves[i]], gates[:, m, halves[i]], tmp[:, 2, halves[i]], MUL).then_inc(out_made[i], 1)

            second_half(QUAD)
            second_half(QUAD + 1)
            last_added(KT, halves[1])
            last_added(KT + 1, halves[1])
            second_half(QUAD + 2)
            second_half(QUAD + 3)
            rstd(3, tmp[:, 2, :], 1, halves[0])
            result(0)
            rstd(3, tmp[:, 2, :], 2, halves[1])
            result(1)


def kernel(**inputs):
    from concourse import bacc
    from concourse.bass_utils import run_bass_kernel_spmd

    F32 = mybir.dt.float32
    nc = bacc.Bacc("TRN2", target_bir_lowering=False, num_devices=1, dynamic_dma_scratch_size=64)
    a = {n: np.asarray(v) for n, v in inputs.items()}
    arrays = {n: np.ascontiguousarray(a[n][0]) for n in (
        "w_mod", "w_ffn_up", "w_ffn_down", "w_fnet_out", "w_in_2", "w_a_out_2", "w_r_out_2", "w_o_2",
        "w_ff_gate_2", "w_ff_up_2", "w_ff_down_2")}
    arrays["x"] = np.ascontiguousarray(a["x"][0])
    arrays["x_t"] = np.ascontiguousarray(a["x"][0].T)
    arrays["columns"] = np.ascontiguousarray(np.concatenate([a[n].reshape(-1) for n, _ in VECTORS]).reshape(COLS, P).T)
    arrays["decays"] = np.ascontiguousarray(np.broadcast_to(
        np.concatenate([a["dec_f_2"].reshape(-1), a["dec_b_2"].reshape(-1)]), (P, 2 * HEADS)))
    arrays.update(tables())
    t = {n: nc.dram_tensor(f"in_{n}", v.shape, F32, kind="ExternalInput").ap() for n, v in arrays.items()}
    out = nc.dram_tensor("out", (D, T), F32, kind="ExternalOutput").ap()
    build(nc, t, out)
    r = run_bass_kernel_spmd(nc, [{f"in_{n}": v for n, v in arrays.items()}], core_ids=[0])
    return np.ascontiguousarray(r.results[0]["out"].T)[None]
```
